# Optimizing a Trainium2 kernel written in Bass

```python
import math
import jax, jax.numpy as jnp
from jax import lax
import numpy as np

D_MODEL = 1024
BATCH = 1
SEQ = 512
DEPTH = 1

HEAD_DIM = 64
Q_BLOCK = 128
NSA_Q_HEADS = 8
NSA_KV_GROUPS = 2
NSA_HPG = NSA_Q_HEADS // NSA_KV_GROUPS
CMP_BLOCK = 32
CMP_STRIDE = 16
CMP_HIDDEN = 4 * HEAD_DIM
SLC_BLOCK = 64
N_SELECT = 16
N_LOCAL_FORCED = 2
WIN = 512
DIL_PATTERNS = ((128, 1), (512, 4), (2048, 16))
DIL_HPG = 4
DIL_HEADS = DIL_HPG * len(DIL_PATTERNS)
REL_BUCKETS = 32
REL_MAX_DIST = 2048
N_HEADS_TOTAL = NSA_Q_HEADS + DIL_HEADS
D_FF = 2816
EPS = 1e-6
NEG = -1e30
BIG = 1e30
NSA_Q_W = NSA_Q_HEADS * HEAD_DIM
NSA_KV_W = NSA_KV_GROUPS * HEAD_DIM
DIL_W = DIL_HEADS * HEAD_DIM
PROJ_WIDTHS = (NSA_Q_W, NSA_KV_W, NSA_KV_W, NSA_KV_W, NSA_KV_W, NSA_KV_W, NSA_KV_W,
               3 * NSA_Q_HEADS, DIL_W, DIL_W, DIL_W, D_MODEL, D_MODEL)
PROJ_WIDTH = sum(PROJ_WIDTHS)
BRANCH_A_W = NSA_Q_W
BRANCH_B_W = DIL_HPG * HEAD_DIM

kernel_name = "hybrid_nsa_dilated_macaron_block"

def rms_norm(x, g):
    xf = x.astype(jnp.float32)
    y = xf * lax.rsqrt(jnp.mean(xf * xf, axis=-1, keepdims=True) + EPS)
    return (y * g.astype(jnp.float32)).astype(x.dtype)

def swiglu(x, w_gu, w_down):
    g, u = jnp.split(x @ w_gu, 2, axis=-1)
    return (jax.nn.silu(g) * u) @ w_down

def t5_bucket(dist):
    max_exact = REL_BUCKETS // 2
    d = jnp.maximum(dist, 0)
    df = jnp.maximum(d, max_exact).astype(jnp.float32)
    large = max_exact + (jnp.log(df / max_exact) / math.log(REL_MAX_DIST / max_exact)
                         * (REL_BUCKETS - max_exact)).astype(jnp.int32)
    large = jnp.minimum(large, REL_BUCKETS - 1)
    return jnp.where(d < max_exact, d, large)

def masked_softmax(s, mask):
    s = jnp.where(mask, s, NEG)
    m = jnp.max(s, axis=-1, keepdims=True)
    p = jnp.where(mask, jnp.exp(s - m), 0.0)
    den = jnp.sum(p, axis=-1, keepdims=True)
    probs = p / jnp.maximum(den, 1e-30)
    lse = m[..., 0] + jnp.log(jnp.maximum(den[..., 0], 1e-30))
    return probs, lse

def nsa_attention(q, k_cmp, v_cmp, k_slc, v_slc, k_win, v_win, gates,
                  pos_k, w1_k, w2_k, pos_v, w1_v, w2_v, rel_tab):
    B_, S_, H, dh = q.shape
    G, hpg = NSA_KV_GROUPS, NSA_HPG
    scale = dh ** -0.5
    dtype = q.dtype
    n_cmp = (S_ - CMP_BLOCK) // CMP_STRIDE + 1
    blk_idx = np.arange(n_cmp)[:, None] * CMP_STRIDE + np.arange(CMP_BLOCK)[None, :]
    cmp_end = jnp.asarray(blk_idx[:, -1], jnp.int32)

    def compress(a, pos, w1, w2):
        blocks = a[:, blk_idx] + pos[None, None, :, None, :]
        blocks = blocks.transpose(0, 1, 3, 2, 4).reshape(B_, n_cmp, G, CMP_BLOCK * dh)
        return (jax.nn.silu(blocks @ w1) @ w2).transpose(0, 2, 1, 3)

    kc = compress(k_cmp, pos_k, w1_k, w2_k)
    vc = compress(v_cmp, pos_v, w1_v, w2_v)
    n_slc = S_ // SLC_BLOCK
    n_sel = min(N_SELECT, n_slc)
    slc_start = np.arange(n_slc) * SLC_BLOCK
    overlap = (blk_idx[:, :1] < slc_start[None] + SLC_BLOCK) & (blk_idx[:, -1:] >= slc_start[None])
    cmp_to_slc = jnp.asarray(overlap, jnp.float32)
    slc_ids = jnp.arange(n_slc, dtype=jnp.int32)
    qg = q.reshape(B_, S_, G, hpg, dh).transpose(0, 2, 3, 1, 4)
    gg = gates.reshape(B_, S_, G, hpg, 3).transpose(0, 2, 3, 1, 4)
    ks = k_slc.transpose(0, 2, 1, 3)
    vs = v_slc.transpose(0, 2, 1, 3)
    kw = jnp.pad(k_win.transpose(0, 2, 1, 3), ((0, 0), (0, 0), (WIN, 0), (0, 0)))
    vw = jnp.pad(v_win.transpose(0, 2, 1, 3), ((0, 0), (0, 0), (WIN, 0), (0, 0)))
    tab = rel_tab.reshape(REL_BUCKETS, G, hpg)
    tab_g = tab.transpose(1, 0, 2)
    g_ids = jnp.arange(G)[None, :, None, None]
    gather_rows = jax.vmap(jax.vmap(lambda a, i: a[i]))
    n_wk = WIN + Q_BLOCK
    dist_w = np.arange(Q_BLOCK)[:, None] + WIN - np.arange(n_wk)[None, :]
    band_w = jnp.asarray((dist_w >= 0) & (dist_w < WIN))
    bias_w = tab[t5_bucket(jnp.asarray(dist_w, jnp.int32))].transpose(2, 3, 0, 1)

    def chunk(c):
        t0 = c * Q_BLOCK
        t = t0 + jnp.arange(Q_BLOCK, dtype=jnp.int32)
        qc = lax.dynamic_slice_in_dim(qg, t0, Q_BLOCK, axis=3)
        gc = lax.dynamic_slice_in_dim(gg, t0, Q_BLOCK, axis=3)
        dist_c = t[:, None] - cmp_end[None, :]
        s_c = jnp.einsum('bghqd,bgkd->bghqk', qc, kc, preferred_element_type=jnp.float32) * scale
        s_c = s_c + tab[t5_bucket(dist_c)].transpose(2, 3, 0, 1)
        p_c, _ = masked_softmax(s_c, dist_c >= 0)
        o_c = jnp.einsum('bghqk,bgkd->bghqd', p_c.astype(dtype), vc)
        imp = jnp.einsum('bghqk,ks->bgqs', p_c, cmp_to_slc)
        rel = (t // SLC_BLOCK)[:, None] - slc_ids[None, :]
        forced = (slc_ids[None, :] == 0) | ((rel >= 0) & (rel < N_LOCAL_FORCED))
        score = jnp.where(forced, BIG, jnp.where(rel < 0, NEG, imp))
        _, sel = lax.top_k(score, n_sel)
        pos = (sel[..., None] * SLC_BLOCK + jnp.arange(SLC_BLOCK, dtype=jnp.int32))
        pos = pos.reshape(B_, G, Q_BLOCK, n_sel * SLC_BLOCK)
        pos_flat = pos.reshape(B_, G, Q_BLOCK * n_sel * SLC_BLOCK)
        k_sel = gather_rows(ks, pos_flat).reshape(B_, G, Q_BLOCK, n_sel * SLC_BLOCK, dh)
        v_sel = gather_rows(vs, pos_flat).reshape(B_, G, Q_BLOCK, n_sel * SLC_BLOCK, dh)
        dist_s = t[:, None] - pos
        bias_s = jnp.moveaxis(tab_g[g_ids, t5_bucket(dist_s)], -1, 2)
        s_s = jnp.einsum('bghqd,bgqkd->bghqk', qc, k_sel, preferred_element_type=jnp.float32) * scale + bias_s
        p_s, _ = masked_softmax(s_s, (dist_s >= 0)[:, :, None])
        o_s = jnp.einsum('bghqk,bgqkd->bghqd', p_s.astype(dtype), v_sel)
        kwc = lax.dynamic_slice_in_dim(kw, t0, n_wk, axis=2)
        vwc = lax.dynamic_slice_in_dim(vw, t0, n_wk, axis=2)
        kpos = t0 - WIN + jnp.arange(n_wk, dtype=jnp.int32)
        s_w = jnp.einsum('bghqd,bgkd->bghqk', qc, kwc, preferred_element_type=jnp.float32) * scale + bias_w
        p_w, _ = masked_softmax(s_w, band_w & (kpos >= 0)[None, :])
        o_w = jnp.einsum('bghqk,bgkd->bghqd', p_w.astype(dtype), vwc)
        return gc[..., 0:1] * o_c + gc[..., 1:2] * o_s + gc[..., 2:3] * o_w

    out = lax.map(chunk, jnp.arange(S_ // Q_BLOCK, dtype=jnp.int32))
    return out.transpose(1, 0, 4, 2, 3, 5).reshape(B_, S_, H * dh)

def strided_band_attention(q, k, v, rel_tab, steps, dilation):
    B_, S_, h, dh = q.shape
    L = S_ // dilation
    n_blk = -(-L // Q_BLOCK)
    Lp = n_blk * Q_BLOCK
    N = B_ * dilation

    def blocks(a):
        a = a.reshape(B_, L, dilation, h, dh).transpose(0, 2, 1, 3, 4).reshape(N, L, h, dh)
        a = jnp.pad(a, ((0, 0), (0, Lp - L), (0, 0), (0, 0)))
        return a.reshape(N, n_blk, Q_BLOCK, h, dh)

    def with_prev(a):
        prev = jnp.pad(a[:, :-1], ((0, 0), (1, 0), (0, 0), (0, 0), (0, 0)))
        return jnp.concatenate([prev, a], axis=2)

    qb = blocks(q)
    kk = with_prev(blocks(k))
    vv = with_prev(blocks(v))
    qi = np.arange(Q_BLOCK)[:, None]
    kj = np.arange(2 * Q_BLOCK)[None, :]
    dist = qi + Q_BLOCK - kj
    mask = ((dist >= 0) & (dist <= steps))[None] & \
        ((np.arange(n_blk)[:, None, None] > 0) | (kj[None] >= Q_BLOCK))
    bias = rel_tab[t5_bucket(jnp.asarray(dist * dilation, jnp.int32))].transpose(2, 0, 1)
    s = jnp.einsum('nbqhd,nbkhd->nbhqk', qb, kk, preferred_element_type=jnp.float32) * dh ** -0.5 + bias
    p, lse = masked_softmax(s, jnp.asarray(mask)[None, :, None])
    o = jnp.einsum('nbhqk,nbkhd->nbqhd', p.astype(v.dtype), vv).reshape(N, Lp, h, dh)[:, :L]
    lse = lse.transpose(0, 1, 3, 2).reshape(N, Lp, h)[:, :L]

    def unstride(a):
        return a.reshape((B_, dilation, L) + a.shape[2:]).swapaxes(1, 2).reshape((B_, S_) + a.shape[2:])

    return unstride(o), unstride(lse)

def dilated_attention(q, k, v, rel_tab):
    B_, S_, _, dh = q.shape
    outs, lses = [], []
    for g, (window, dilation) in enumerate(DIL_PATTERNS):
        hs = slice(g * DIL_HPG, (g + 1) * DIL_HPG)
        o, lse = strided_band_attention(q[:, :, hs], k[:, :, hs], v[:, :, hs], rel_tab[:, hs],
                                        window // dilation, dilation)
        outs.append(o)
        lses.append(lse)
    w = jax.nn.softmax(jnp.stack(lses), axis=0)
    o = jnp.sum(w[..., None] * jnp.stack(outs).astype(jnp.float32), axis=0).astype(q.dtype)
    return o.reshape(B_, S_, DIL_HPG * dh)

def setup_inputs(seed: int = 0) -> dict:
    key = jax.random.key(seed)
    ks = jax.random.split(key, 24)

    def w(k, shape, fan_in):
        return jax.random.normal(k, shape, jnp.float32) * fan_in ** -0.5

    def gain(k):
        return 1.0 + 0.05 * jax.random.normal(k, (DEPTH, D_MODEL), jnp.float32)

    L = DEPTH
    return {
        "x": jax.random.normal(ks[0], (BATCH, SEQ, D_MODEL), jnp.float32),
        "ffn1_norm_pre": gain(ks[1]),
        "ffn1_w_gu": w(ks[2], (L, D_MODEL, 2 * D_FF), D_MODEL),
        "ffn1_w_down": w(ks[3], (L, D_FF, D_MODEL), D_FF),
        "ffn1_norm_post": gain(ks[4]),
        "mix_norm_pre": gain(ks[5]),
        "w_in": w(ks[6], (L, D_MODEL, PROJ_WIDTH), D_MODEL),
        "cmp_pos_k": 0.1 * jax.random.normal(ks[7], (L, CMP_BLOCK, HEAD_DIM), jnp.float32),
        "cmp_w1_k": w(ks[8], (L, CMP_BLOCK * HEAD_DIM, CMP_HIDDEN), CMP_BLOCK * HEAD_DIM),
        "cmp_w2_k": w(ks[9], (L, CMP_HIDDEN, HEAD_DIM), CMP_HIDDEN),
        "cmp_pos_v": 0.1 * jax.random.normal(ks[10], (L, CMP_BLOCK, HEAD_DIM), jnp.float32),
        "cmp_w1_v": w(ks[11], (L, CMP_BLOCK * HEAD_DIM, CMP_HIDDEN), CMP_BLOCK * HEAD_DIM),
        "cmp_w2_v": w(ks[12], (L, CMP_HIDDEN, HEAD_DIM), CMP_HIDDEN),
        "w_branch_nsa": w(ks[13], (L, BRANCH_A_W, D_MODEL), BRANCH_A_W),
        "w_branch_dil": w(ks[14], (L, BRANCH_B_W, D_MODEL), BRANCH_B_W),
        "w_out": w(ks[15], (L, D_MODEL, D_MODEL), D_MODEL),
        "mix_norm_post": gain(ks[16]),
        "ffn2_norm_pre": gain(ks[17]),
        "ffn2_w_gu": w(ks[18], (L, D_MODEL, 2 * D_FF), D_MODEL),
        "ffn2_w_down": w(ks[19], (L, D_FF, D_MODEL), D_FF),
        "ffn2_norm_post": gain(ks[20]),
        "rel_bias": 0.1 * jax.random.normal(ks[21], (REL_BUCKETS, N_HEADS_TOTAL), jnp.float32),
    }

def reference(x, ffn1_norm_pre, ffn1_w_gu, ffn1_w_down, ffn1_norm_post, mix_norm_pre, w_in,
              cmp_pos_k, cmp_w1_k, cmp_w2_k, cmp_pos_v, cmp_w1_v, cmp_w2_v,
              w_branch_nsa, w_branch_dil, w_out, mix_norm_post,
              ffn2_norm_pre, ffn2_w_gu, ffn2_w_down, ffn2_norm_post, rel_bias):
    B_, S_, _ = x.shape
    split_idx = [int(i) for i in np.cumsum(PROJ_WIDTHS)[:-1]]

    def heads(a, n):
        return a.reshape(B_, S_, n, HEAD_DIM)

    for l in range(DEPTH):
        x = x + 0.5 * rms_norm(swiglu(rms_norm(x, ffn1_norm_pre[l]), ffn1_w_gu[l], ffn1_w_down[l]),
                               ffn1_norm_post[l])
        h = rms_norm(x, mix_norm_pre[l])
        (q_n, kc, vc, ksl, vsl, kwn, vwn, g_n, q_d, k_d, v_d, g_a, g_b) = jnp.split(h @ w_in[l], split_idx, axis=-1)
        y_nsa = nsa_attention(heads(q_n, NSA_Q_HEADS), heads(kc, NSA_KV_GROUPS), heads(vc, NSA_KV_GROUPS),
                              heads(ksl, NSA_KV_GROUPS), heads(vsl, NSA_KV_GROUPS),
                              heads(kwn, NSA_KV_GROUPS), heads(vwn, NSA_KV_GROUPS),
                              jax.nn.sigmoid(g_n).reshape(B_, S_, NSA_Q_HEADS, 3),
                              cmp_pos_k[l], cmp_w1_k[l], cmp_w2_k[l], cmp_pos_v[l], cmp_w1_v[l], cmp_w2_v[l],
                              rel_bias[:, :NSA_Q_HEADS])
        y_dil = dilated_attention(heads(q_d, DIL_HEADS), heads(k_d, DIL_HEADS), heads(v_d, DIL_HEADS),
                                  rel_bias[:, NSA_Q_HEADS:])
        merged = jax.nn.sigmoid(g_a) * (y_nsa @ w_branch_nsa[l]) + jax.nn.sigmoid(g_b) * (y_dil @ w_branch_dil[l])
        x = x + rms_norm(merged @ w_out[l], mix_norm_post[l])
        x = x + 0.5 * rms_norm(swiglu(rms_norm(x, ffn2_norm_pre[l]), ffn2_w_gu[l], ffn2_w_down[l]),
                               ffn2_norm_post[l])
    return x


_drawn_inputs = setup_inputs


def setup_inputs(seed=0):
    import zlib

    import numpy as np

    out = dict(_drawn_inputs(seed))
    spreads = {}
    factors = {'cmp_pos_k': 5.941, 'ffn2_norm_post': 3.745}
    for name, (base, spread) in spreads.items():
        noise = np.random.default_rng([zlib.crc32(name.encode()), seed]).standard_normal(out[name].shape)
        drawn = base * np.exp(spread * noise) if base else spread * noise
        out[name] = __import__('jax').numpy.asarray(drawn.astype(out[name].dtype))
    for name, factor in factors.items():
        out[name] = (out[name] * factor).astype(out[name].dtype)
    return out
```

```python
import math

import concourse.bass as bass
import numpy as np
from concourse import mybir

F32 = mybir.dt.float32
F32R = mybir.dt.float32r
ALU = mybir.AluOpType
ACT = mybir.ActivationFunctionType
AX_X = mybir.AxisListType.X

P = 128
S, D, F = 512, 1024, 2816
NT = S // P
KD = D // P
KF = F // P
HD = 64
NSA_H, NSA_G, HPG = 8, 2, 4
DIL_H, SLOTS = 12, 4
CB, CS = 32, 16
NCMP = (S - CB) // CS + 1
CPAD = 32
BUCKETS, MAX_DIST = 32, 2048
EPS = 1e-6
SCALE = HD ** -0.5
MASKED = 1e30
BIGGEST = 3e38

QN = 0
KCMP, VCMP, KSLC, VSLC, KWIN, VWIN = (NSA_H * HD + i * NSA_G * HD for i in range(6))
GN = NSA_H * HD + 6 * NSA_G * HD
QD = GN + 3 * NSA_H
KDL = QD + DIL_H * HD
VDL = KDL + DIL_H * HD
GA = VDL + DIL_H * HD
GB = GA + D

DIL_KEYS = 2 * P
NSA_W = 640
CMP_W = 1024
D0_W = 384
D12_W = 256
NSA_AT, CMP_AT = 0, NSA_W
D0_AT = CMP_AT + CMP_W
D1_AT = D0_AT + D0_W
D2_AT = D1_AT + D12_W
TAB_W = D2_AT + D12_W
CMP_ZERO = CB - 1 + CS * (CPAD - 1)

W = 2048
UP, DOWN = KF, KF // 2
FFN1 = 0
PROJ = FFN1 + UP + DOWN
NPROJ, NV, NCOMP = 10, 4, 4
VST = PROJ + NPROJ
COMP = VST + NV
GATE = COMP + NCOMP
NGATE = 8
BDIL = GATE + NGATE
BNSA = BDIL + 1
OUT = BNSA + 2
FFN2 = OUT + 4
STEPS = FFN2 + UP + DOWN
PAIR_PROJ = UP
PAIR_GATE = PAIR_PROJ + NPROJ + NV
PAIR_FFN2 = PAIR_GATE + NGATE


def bucket(d):
    d = np.maximum(d, 0)
    exact = BUCKETS // 2
    large = exact + (np.log(np.maximum(d, exact).astype(np.float32) / np.float32(exact))
                     / np.float32(math.log(MAX_DIST / exact)) * (BUCKETS - exact)).astype(np.int32)
    return np.where(d < exact, d, np.minimum(large, BUCKETS - 1))


def bucket_table():
    i = np.arange(TAB_W)
    dist = np.zeros(TAB_W, np.int64)
    keep = np.ones(TAB_W, bool)
    a = i[NSA_AT:CMP_AT] - NSA_AT
    dist[NSA_AT:CMP_AT] = S - 1 - a
    dist[CMP_AT:D0_AT] = np.arange(CMP_W) - (CMP_ZERO)
    d0 = DIL_KEYS - 1 - np.arange(D0_W)
    dist[D0_AT:D1_AT] = d0
    keep[D0_AT:D1_AT] = d0 <= P
    d1 = P - 1 - np.arange(D12_W)
    dist[D1_AT:D2_AT] = 4 * d1
    dist[D2_AT:TAB_W] = 4 * d1
    keep[D2_AT:TAB_W] = d1 % 4 == 0
    keep &= dist >= 0
    out = np.zeros((BUCKETS + 1, TAB_W), np.float32)
    out[bucket(dist), i] = keep
    out[BUCKETS] = ~keep
    return out


def units():
    dil, nsa = [], []
    for j in range(DIL_H):
        if j < SLOTS:
            dil.append([("d0", j, t, [t - 1, t] if t else [0]) for t in (0, 1)])
            dil.append([("d0", j, t, [t - 1, t]) for t in (2, 3)])
        else:
            dil.append([("d12", j, r, [r]) for r in range(4)])
    for c in range(NSA_H):
        h = c // 2 + HPG * (c % 2)
        full = lambda b, t: (b, h, t, list(range(t + 1)))
        nsa += [[full("s", 1), full("w", 1)], [full("s", 3)], [full("w", 3)],
                [full("s", 0), full("s", 2)], [full("w", 2), full("w", 0)]]
    return dil, nsa


def place(row):
    kind, _, t, _ = row
    return (t // 2 * 2 if t % 2 else 4 + t // 2) + (kind == "w") * (1 if t % 2 else 2)


def layer_kernel(nc, x, g1_pre, w1_gu, w1_down, g1_post, gm_pre, w_in, pos_k, cw1_k, cw2_k,
                 pos_v, cw1_v, cw2_v, w_bn, w_bd, w_out, gm_post, g2_pre, w2_gu, w2_down, g2_post,
                 rel, onehot, out):
    DIL, NSA = units()
    NDU, NNU = len(DIL), len(NSA)

    K = 1024
    ARENA = 207 * K
    base = (nc.sbuf_base + 31) // 32 * 32
    nc.alloc_sbuf_tensor("arena", [P, ARENA], mybir.dt.uint8)

    def at(name, offset, shape, dt=F32):
        return nc.alloc_sbuf_tensor_at(name, [P] + shape, dt, offset=base + offset)

    xres = at("xres", 0, [KD, S])
    xn_hi = at("xn_hi", 16 * K, [KD, S], F32R)
    xn_lo = at("xn_lo", 32 * K, [KD, S], F32R)
    ring_raw = at("ring_raw", 48 * K, [2, W])
    ring_hi = at("ring_hi", 64 * K, [2, W], F32R)
    ring_lo = at("ring_lo", 80 * K, [2, W], F32R)
    R = 96 * K
    Y = R + 88 * K
    SM = Y + 16 * K
    hT_hi = at("hT_hi", R, [KF * S], F32R)
    hT_lo = at("hT_lo", R + 44 * K, [KF * S], F32R)
    ysb = at("ysb", Y, [KD, S])
    silu_g = at("silu_g", Y, [2, S])
    h_f32 = at("h_f32", Y + 4 * K, [2, S])
    x_tok = at("x_tok", R, [NT, D])
    gains_row = at("gains_row", R + 16 * K, [P])
    onehot_sb = at("onehot_sb", R + 56 * K, [TAB_W])
    bias_vec = at("bias_vec", R + 68 * K, [TAB_W])
    o_tok = at("o_tok", R, [NT, D])
    qn = at("qn", R, [4, S])
    kv4 = at("kv4", R + 8 * K, [4, S])
    qd = at("qd", R + 16 * K, [6, S])
    kd = at("kd", R + 28 * K, [6, S])
    v_all = at("v_all", R + 40 * K, [NT, D])
    bias_d0 = at("bias_d0", R + 56 * K, [SLOTS, DIL_KEYS])
    bias_d12 = at("bias_d12", R + 60 * K, [8, P])
    bias_cT = at("bias_cT", R + 64 * K, [NSA_G, S])
    o_dil = at("o_dil", R + 68 * K, [3, 4, SLOTS, HD])
    s_sb = at("s_sb", R + 80 * K, [2, S])
    p_sb = at("p_sb", R + 84 * K, [2, S])
    pT_sb = at("pT_sb", R + 88 * K, [2, S])
    y_nsa = at("y_nsa", R + 92 * K, [NT, NSA_H, HD])
    wg_raw = at("wg_raw", R + 68 * K, [KD, 24])
    wg_hi = at("wg_hi", R + 68 * K + 768, [KD, 24], F32R)
    wg_lo = at("wg_lo", R + 69 * K + 512, [KD, 24], F32R)
    w2k = at("w2k", R + 70 * K + 256, [2, 2, HD])
    w2v = at("w2v", R + 71 * K + 256, [2, HD])
    vb_hi = at("vb_hi", R + 72 * K, [16, 64], F32R)
    vb_lo = at("vb_lo", R + 76 * K, [16, 64], F32R)
    blk = at("blk", R + 80 * K, [16, 64])
    kb_hi = at("kb_hi", R + 84 * K, [16, 64], F32R)
    kb_lo = at("kb_lo", R + 88 * K, [16, 64], F32R)
    pair_k = at("pair_k", R + 92 * K, [NSA_G, S])
    pair_v = at("pair_v", R + 96 * K, [NSA_G, S])
    kcT = at("kcT", R + 100 * K, [CPAD])
    vc_diag = at("vc_diag", R + 100 * K + 128, [NSA_G, HPG * HD])
    gates = at("gates", R + 102 * K + 128, [NT, NSA_H, 3])
    f_nsa = at("f_nsa", R + 102 * K + 512, [2, 8])
    f_c = at("f_c", R + 102 * K + 640, [NT, 8])
    nm_c = at("nm_c", R + 102 * K + 768, [2, 8])
    den_c = at("den_c", R + 102 * K + 832, [8])
    st_p = at("st_p", R + 103 * K, [4, 4, SLOTS])
    st_0 = at("st_0", R + 103 * K + 256, [NT, 2, SLOTS])
    st_n = at("st_n", R + 103 * K + 384, [NT, 4, SLOTS])
    e_n = at("e_n", R + 103 * K + 640, [3, NT, SLOTS])
    w_n = at("w_n", R + 103 * K + 832, [NT, SLOTS])
    bias_n = at("bias_n", R + 16 * K, [NSA_H, S])
    o_tmp = at("o_tmp", R + 32 * K, [2, S])
    sig = at("sig", R + 16 * K, [2 * KD, S])
    yn_hi = at("yn_hi", R + 48 * K, [4, S], F32R)
    yn_lo = at("yn_lo", R + 56 * K, [4, S], F32R)
    yd_hi = at("yd_hi", R, [2, S], F32R)
    yd_lo = at("yd_lo", R + 4 * K, [2, S], F32R)
    yd = at("yd", R + 8 * K, [2, S])
    mrg = at("mrg", R + 80 * K, [2, 2, S])
    o = [SM]

    def small(name, shape, dt=F32):
        t = at(name, o[0], shape, dt)
        o[0] += (4 * int(np.prod(shape)) + 31) // 32 * 32
        assert o[0] <= ARENA
        return t

    sq = small("sq", [S])
    acc = small("acc", [S])
    hid_k = at("hid_k", SM, [2, 64])
    hid_v = at("hid_v", SM + 2 * K, [2, NSA_G, HPG, CPAD])
    ident = small("ident", [P])
    ones = small("ones", [1])
    eps = small("eps", [1])
    gains = small("gains", [6, KD])
    sd = small("sd", [NT])
    rstd = small("rstd", [NT])
    tab = small("tab", [20])
    posT = small("posT", [2, 16])
    stat_m = small("stat_m", [16])
    stat_d = small("stat_d", [16])
    c_p = small("c_p", [4, 2, SLOTS])
    c_n = small("c_n", [NT, 2, SLOTS])
    valid = small("valid", [1])
    ps = nc.alloc_psum_tensor("ps", [P, 8, S], F32)

    vec_dram = nc.dram_tensor("bias_by_distance", [20, TAB_W], F32, kind="Internal").ap()
    rep_n = nc.dram_tensor("bias_rows_sparse", [P, NSA_H, NSA_W], F32, kind="Internal").ap()
    rep_d0 = nc.dram_tensor("bias_rows_dense", [P, SLOTS, D0_W], F32, kind="Internal").ap()
    rep_d1 = nc.dram_tensor("bias_rows_strided4", [P, SLOTS, D12_W], F32, kind="Internal").ap()
    rep_d2 = nc.dram_tensor("bias_rows_strided16", [P, SLOTS, D12_W], F32, kind="Internal").ap()
    rep_c = nc.dram_tensor("bias_rows_compressed", [CPAD, NSA_H, CMP_W], F32, kind="Internal").ap()
    st_dram = nc.dram_tensor("dilated_stats", [S, 16], F32, kind="Internal").ap()
    c_dram = nc.dram_tensor("dilated_weights", [S, 8], F32, kind="Internal").ap()

    sem = lambda name: nc.alloc_semaphore(name)
    raw_loaded = [sem("raw_loaded0"), sem("raw_loaded1")]
    hi_ready, lo_ready, w_used = sem("hi_ready"), sem("lo_ready"), sem("w_used")
    x_loaded, small_loaded, gains_loaded = sem("x_loaded"), sem("small_loaded"), sem("gains_loaded")
    consts, vec_mm, vec_copied, vec_stored = sem("consts"), sem("vec_mm"), sem("vec_copied"), sem("vec_stored")
    tab_ready, rows_stored = sem("tab_ready"), sem("rows_stored")
    xT_done = sem("xT_done")
    act_read, dve_read = sem("act_read"), sem("dve_read")
    h_ready, hhi_ready, hlo_ready = sem("h_ready"), sem("hhi_ready"), sem("hlo_ready")
    y_done, y_squared, y_summed = sem("y_done"), sem("y_squared"), sem("y_summed")
    ss_done, sd_ready, rstd_ready, rb_ready = sem("ss_done"), sem("sd_ready"), sem("rstd_ready"), sem("rb_ready")
    x_scaled, x_new, x_squared = sem("x_scaled"), sem("x_new"), sem("x_squared")
    u_ready, xhi_ready, xlo_ready = sem("u_ready"), sem("xhi_ready"), sem("xlo_ready")
    oT_done, o_copied, out_stored = sem("oT_done"), sem("o_copied"), sem("out_stored")
    biases_loaded, bias_n_loaded, cmp_loaded = sem("biases_loaded"), sem("bias_n_loaded"), sem("cmp_loaded")
    wg_loaded, wg_hi_ready, wg_lo_ready = sem("wg_loaded"), sem("wg_hi_ready"), sem("wg_lo_ready")
    gn_done, gates_ready = sem("gn_done"), sem("gates_ready")
    pairs_loaded, blk_ready, bhi_ready, blo_ready = [sem("pair_k_loaded"), sem("pair_v_loaded")], sem("blk_ready"), sem("bhi_ready"), sem("blo_ready")
    hid_ready, c2_done, kc_ready = sem("hid_ready"), sem("c2_done"), sem("kc_ready")
    s_done, s_biased, p_ready, pT_done, pT_ready, o_read = (
        sem("s_done"), sem("s_biased"), sem("p_ready"), sem("pT_done"), sem("pT_ready"), sem("o_read"))
    sc_done, sc_min, sc_sub, pc_ready, pcT_done, pcT_ready, oc_done, yc_ready = (
        sem("sc_done"), sem("sc_min"), sem("sc_sub"), sem("pc_ready"), sem("pcT_done"), sem("pcT_ready"), sem("oc_done"), sem("yc_ready"))
    stats_stored, stats_loaded, e_in, e_ready, c_ready, c_stored, c_loaded = (
        sem("stats_stored"), sem("stats_loaded"), sem("e_in"), sem("e_ready"), sem("c_ready"), sem("c_stored"), sem("c_loaded"))
    w2_loaded = sem("w2_loaded")
    cT_gains = sem("gains_transposed")
    gains_ready = sem("gains_ready")
    o_nsa_read = sem("o_nsa_read")
    pv_done = sem("pv_done")
    odil_scaled, ydT_done, yd_summed, ydhi_ready, ydlo_ready = (
        sem("odil_scaled"), sem("ydT_done"), sem("yd_summed"), sem("ydhi_ready"), sem("ydlo_ready"))
    y_nsa_ready, ynT_done, ynhi_ready, ynlo_ready = sem("y_nsa_ready"), sem("ynT_done"), sem("ynhi_ready"), sem("ynlo_ready")
    b_done, b_gated, a_done, a_gated, merged, mhi_ready, mlo_ready = (
        sem("b_done"), sem("b_gated"), sem("a_done"), sem("a_gated"), sem("merged"), sem("mhi_ready"), sem("mlo_ready"))
    dve_chain = sem("dve_chain")

    f32 = lambda ap: ap.bitcast(F32)
    heads2 = lambda ap: ap.rearrange("p (a b) -> p a b", b=HD)
    by_k = lambda ap: ap.rearrange("(k p) c -> p k c", p=P)
    MODES = ((0, 0), (0, 1), (1, 0))
    ring = (ring_hi, ring_lo)
    xn = (xn_hi, xn_lo)
    hT = (hT_hi, hT_lo)

    def cmp_banks(t):
        return (0, 1) if t % 2 == 0 else (2, 3)

    def stat_dil(row):
        _, j, t, _ = row
        g, slot = j // SLOTS, j % SLOTS
        if g == 0:
            return st_0[:, t, 0, slot:slot + 1], st_0[:, t, 1, slot:slot + 1]
        return (st_p[:, t, 2 * (g - 1), slot:slot + 1], st_p[:, t, 2 * (g - 1) + 1, slot:slot + 1])

    def stat_nsa(turn):
        def of(row):
            i = 8 * (turn % 2) + place(row)
            return stat_m[:, i:i + 1], stat_d[:, i:i + 1]
        return of

    def stats_of(u):
        return stat_dil if u < NDU else stat_nsa((u - NDU) // 5)

    def paired_views(dst, c):
        out = []
        for h in range(2):
            to = dst[:, c % 2, :].rearrange("p (k h g d) -> p k h g d", h=2, g=2, d=HD)[:, :, h]
            of = ring_raw[:, c % 2, :].rearrange("p (k g h d) -> p k g h d", h=2, g=2, d=HD)[:, :, :, h]
            out.append((to, of))
        return out

    def y_event(p, m):
        if p == 1:
            return (w_used, OUT + m // 2 + 1) if m % 2 else (y_done, KD - 1 + m // 2 + 1)
        first, end = (0, PROJ) if p == 0 else (KD - 1 + 4, STEPS)
        return (y_done, first + m + 1) if m < KD - 1 else (w_used, end)

    def b_event(m):
        return (b_done, m + 1) if m < KD - 1 else (w_used, BDIL + 1)

    def a_event(m):
        return (a_done, m + 1 - m // 4) if m % 4 < 3 else (w_used, BNSA + m // 4 + 1)

    ALL = DIL + NSA
    NU = len(ALL)
    block = nc.Block()
    with block:

        @block.sync
        def _(sp):
            for t in range(NT):
                sp.dma_start(x_tok[:, t, :], x[t * P:t * P + P, :]).then_inc(x_loaded, 16)

            def load(i, c, first, second):
                if not (isinstance(i, int) and 2 * i + c < 2):
                    sp.wait_ge(lo_ready, 2 * i + (c - 1))
                for dst, src in (first, second):
                    sp.dma_start(dst, src).then_inc(raw_loaded[c % 2], 16)

            def view(c, inner):
                return ring_raw[:, c % 2, :].rearrange("p (k c) -> p k c", c=inner)

            def load_up(w_gu, base, i, u):
                v = view(base + u, 256)
                load(i, base + u,
                     (v[:, :, 0:P], by_k(w_gu[:, bass.ds(i * (2 * P) + u * P, P)])),
                     (v[:, :, P:256], by_k(w_gu[:, bass.ds(i * (2 * P) + (u * P + F), P)])))

            def load_down(w_down, base, i, u):
                v = view(base + u, D)
                load(i, base + u, (v[:, 0, :], w_down[bass.ds(i * (4 * P) + 2 * u * P, P), :]),
                     (v[:, 1, :], w_down[bass.ds(i * (4 * P) + (2 * u + 1) * P, P), :]))

            def load_cols(n, w, c0):
                v = view(n, 256)
                src = by_k(w[:, c0:c0 + 256])
                load(0, n, (v[:, 0:4, :], src[:, 0:4, :]), (v[:, 4:8, :], src[:, 4:8, :]))

            def load_two(n, w, c0, c1):
                v = view(n, 256)
                load(0, n, (v[:, :, 0:P], by_k(w[:, c0:c0 + P])), (v[:, :, P:256], by_k(w[:, c1:c1 + P])))

            def load_ffn(w_gu, w_down, base):
                for u in range(2):
                    load_up(w_gu, base, 0, u)
                with sp.Fori(1, UP // 2) as i:
                    for u in range(2):
                        load_up(w_gu, base, i, u)
                load_down(w_down, base + UP, 0, 0)
                with sp.Fori(0, (DOWN - 1) // 2) as i:
                    for u in range(1, 3):
                        load_down(w_down, base + UP, i, u)

            load_ffn(w1_gu, w1_down, FFN1)
            for i in range(2):
                load_two(PROJ + i, w_in, QN + P * i, QN + P * (i + 2))
            load_cols(PROJ + 2, w_in, KCMP)
            load_two(PROJ + 3, w_in, KSLC, KWIN)
            for i in range(3):
                load_cols(PROJ + 4 + i, w_in, QD + 256 * i)
            for i in range(3):
                load_cols(PROJ + 7 + i, w_in, KDL + 256 * i)
            load_two(VST, w_in, VSLC, VWIN)
            for i in range(3):
                load_cols(VST + 1 + i, w_in, VDL + 256 * i)
            for i, w in enumerate((cw1_k, cw1_k, cw1_v, cw1_v)):
                load_cols(COMP + i, w[(i % 2) * D:(i % 2) * D + D, :], 0)
            for i in range(NGATE):
                load_cols(GATE + i, w_in, GA + 256 * i)
            v = view(BDIL, D)
            load(0, BDIL, (v[:, 0, :], w_bd[0:P, :]), (v[:, 1, :], w_bd[P:2 * P, :]))
            for i in range(2):
                v, src = view(BNSA + i, S), by_k(w_bn[:, i * S:i * S + S])
                load(0, BNSA + i, (v[:, 0:2, :], src[:, 0:2, :]), (v[:, 2:4, :], src[:, 2:4, :]))
            for i in range(4):
                load_cols(OUT + i, w_out, 256 * i)
            load_ffn(w2_gu, w2_down, FFN2)
            for i in range(4):
                sp.wait_ge(o_copied, 2 * i + 2)
                sp.dma_start(out[:, 256 * i:256 * i + 256].rearrange("(t p) d -> p t d", p=P),
                             o_tok[:, :, 256 * i:256 * i + 256]).then_inc(out_stored, 16)
            sp.wait_ge(out_stored, 64)

        @block.gpsimd
        def _(pool):
            for i, g in enumerate((g1_pre, g1_post, gm_pre, gm_post, g2_pre, g2_post)):
                pool.dma_start(gains_row[i * KD:i * KD + KD, :], g.rearrange("(m p) -> m p", p=P)).then_inc(gains_loaded, 16)
            for i, pos in enumerate((pos_k, pos_v)):
                pool.dma_start(gains_row[6 * KD + 16 * i:6 * KD + 16 * i + 16, :],
                               pos.rearrange("(l e) d -> l (e d)", e=2)).then_inc(gains_loaded, 16)
            pool.memset(ident[:, :], 0.0).then_inc(consts, 1)
            pool.memset(ones[:, :], 1.0).then_inc(consts, 1)
            pool.memset(eps[:, :], EPS).then_inc(consts, 1)
            pool.memset(valid[:, :], 1.0).then_inc(consts, 1)
            pool.wait_ge(consts, 4)
            pool.affine_select(out=ident[:, :], in_=ident[:, :], compare_op=ALU.not_equal, fill=1.0,
                               base=0, pattern=[[-1, P]], channel_multiplier=1).then_inc(consts, 1)
            pool.affine_select(out=valid[:, :], in_=valid[:, :], compare_op=ALU.is_ge, fill=0.0,
                               base=-(CB - 1), pattern=[[0, 1]], channel_multiplier=1).then_inc(consts, 1)
            pool.dma_start(tab[0:BUCKETS, :], rel).then_inc(small_loaded, 16)
            pool.dma_start(onehot_sb[0:BUCKETS + 1, :], onehot).then_inc(small_loaded, 16)
            pool.wait_ge(vec_copied, 5)
            pool.dma_start(vec_dram, bias_vec[0:20, :]).then_inc(vec_stored, 16)
            pool.wait_ge(vec_stored, 16)

            for dst, head, at0 in ((rep_n, 0, NSA_AT), (rep_d0, NSA_H, D0_AT), (rep_d1, NSA_H + SLOTS, D1_AT),
                                   (rep_d2, NSA_H + 2 * SLOTS, D2_AT), (rep_c, 0, CMP_AT)):
                rows, heads, width = dst.shape
                src = bass.AP(tensor=vec_dram.tensor, offset=head * TAB_W + at0,
                              ap=[[0, rows], [TAB_W, heads], [1, width]])
                pool.dma_start(dst, src).then_inc(rows_stored, 16)
            pool.wait_ge(rows_stored, 80)

            def spread(rows, step, first, width):
                n, heads, w = rows.shape
                return bass.AP(tensor=rows.tensor, offset=first, ap=[[heads * w - step, n], [w, heads], [1, width]])

            pool.wait_ge(w_used, PROJ)
            pool.dma_start(wg_raw[:, :, :], by_k(w_in[:, GN:GN + 24])).then_inc(wg_loaded, 16)
            for dst, w2 in ((w2k[:, :, 0, :], cw2_k), (w2k[:, :, 1, :], cw2_k), (w2v[:, :, :], cw2_v)):
                pool.dma_start(dst, w2.rearrange("(c p) d -> p c d", p=P)).then_inc(w2_loaded, 16)
            pool.dma_start(bias_d0[:, :, :], spread(rep_d0, 1, P - 1, DIL_KEYS)).then_inc(biases_loaded, 16)
            pool.dma_start(bias_d12[:, 0:4, :], spread(rep_d1, 1, P - 1, P)).then_inc(biases_loaded, 16)
            pool.dma_start(bias_d12[:, 4:8, :], spread(rep_d2, 1, P - 1, P)).then_inc(biases_loaded, 16)
            for g in range(NSA_G):
                for h in range(HPG):
                    src = bass.AP(tensor=rep_c.tensor, offset=(g * HPG + h) * CMP_W + CMP_ZERO - (CB - 1),
                                  ap=[[NSA_H * CMP_W - CS, CPAD], [1, S]])
                    pool.dma_start(bias_cT[h * CPAD:(h + 1) * CPAD, g, :], src).then_inc(cmp_loaded, 16)
            for i, (pair, chunk_ready) in enumerate(((pair_k, act_read), (pair_v, dve_read))):
                pool.wait_ge(chunk_ready, PAIR_PROJ + 3 if i == 0 else 3)
                if i == 0:
                    pool.wait_ge(xhi_ready, 2 * KD)
                for g in range(NSA_G):
                    src = kv4[g * HD:g * HD + HD, i, :]
                    pool.dma_start(pair[0:HD, g, :], src).then_inc(pairs_loaded[i], 16)
                    pool.dma_start(pair[HD:P, g, 0:S - 1], src[:, 1:S]).then_inc(pairs_loaded[i], 16)
            pool.wait_ge(s_done, NDU)
            pool.dma_start(bias_n[:, :, :], spread(rep_n, 1, P - 1, S)).then_inc(bias_n_loaded, 16)
            pool.wait_ge(p_ready, NDU)
            pool.dma_start(st_dram.rearrange("(l r) c -> l (r c)", r=4),
                           st_p[:, :, :, :].rearrange("p a b c -> p (a b c)")).then_inc(stats_stored, 16)
            pool.wait_ge(stats_stored, 16)
            pool.dma_start(st_n[:, :, :, :].rearrange("p t a b -> p t (a b)"),
                           st_dram.rearrange("(t p) c -> p t c", p=P)).then_inc(stats_loaded, 16)
            pool.wait_ge(c_ready, 1)
            pool.dma_start(c_dram.rearrange("(t p) c -> p t c", p=P),
                           c_n[:, :, :, :].rearrange("p t a b -> p t (a b)")).then_inc(c_stored, 16)
            pool.wait_ge(c_stored, 16)
            pool.dma_start(c_p[:, :, :, :].rearrange("p a b c -> p (a b c)"),
                           c_dram.rearrange("(l r) c -> l (r c)", r=4)).then_inc(c_loaded, 16)
            pool.wait_ge(c_loaded, 16)
            pool.wait_ge(o_read, NDU)
            for g in range(3):
                for r in range(4):
                    c = e_n[:, 0, r, :] if g == 0 else c_p[:, r, g - 1, :]
                    pool.tensor_tensor(o_dil[:, g, r, :, :], o_dil[:, g, r, :, :],
                                       c.unsqueeze(2).broadcast_to([P, SLOTS, HD]), ALU.mult).then_inc(odil_scaled, 1)

        @block.scalar
        def _(act):
            def hi(i, c, paired=False):
                act.wait_ge(raw_loaded[c % 2], 32 * i + 32 * (c // 2 + 1))
                if not (isinstance(i, int) and 2 * i + c < 2):
                    act.wait_ge(w_used, 2 * i + (c - 1))
                for dst, src in paired_views(ring_hi, c) if paired else [(ring_hi[:, c % 2, :], ring_raw[:, c % 2, :])]:
                    e = act.activation(dst, src, ACT.Copy)
                e.then_inc(hi_ready, 1)

            def root(i):
                act.wait_ge(ss_done, i + 1)
                act.activation(sd[:, :], ps[:, 4 if i % 2 else 6, 0:NT], ACT.Sqrt, scale=1.0 / D,
                               bias=eps[:, :]).then_inc(sd_ready, 1)

            def split_norm(r):
                for m in range(KD):
                    act.wait_ge(x_new, KD * r + m + 1)
                    act.activation(ysb[:, m, :], xres[:, m, :], ACT.Square).then_inc(x_squared, 1)
                root(2 * r)
                for m in range(KD):
                    act.wait_ge(u_ready, KD * r + m + 1)
                    act.activation(xn_hi[:, m, :], ysb[:, m, :], ACT.Copy).then_inc(xhi_ready, 1)

            def take_y(p, m):
                act.wait_ge(*y_event(p, m))
                act.activation(ysb[:, m, :], ps[:, m, :], ACT.Copy)
                if m >= 2:
                    act.wait_ge(y_summed, 7 * p + m - 1)
                act.activation((sq if m else acc)[:, :], ps[:, m, :], ACT.Square).then_inc(y_squared, 1)

            def ffn(base, pair0, h0, p):
                def up(i, u):
                    slot = (base + u) % 2
                    act.wait_ge(w_used, 2 * i + (base + u + 1))
                    if not (isinstance(i, int) and 2 * i + u < 2):
                        act.wait_ge(h_ready, 2 * i + (h0 + u - 1))
                    act.activation(silu_g[:, u, :], ps[:, 2 * slot, :], ACT.Silu).then_inc(act_read, 1)
                    hi(i, base + u + 2)
                    act.wait_ge(h_ready, 2 * i + (h0 + u + 1))
                    act.activation(hT_hi[:, bass.ds(i * (2 * S) + u * S, S)], h_f32[:, u, :], ACT.Copy).then_inc(hhi_ready, 1)

                for u in range(2):
                    up(0, u)
                if p == 0:
                    for c in range(5):
                        act.wait_ge(vec_mm, c + 1)
                        w = min(S, TAB_W - c * S)
                        act.activation(bias_vec[0:20, c * S:c * S + w], ps[0:20, 4 + c % 2, 0:w], ACT.Copy,
                                       scale=-1.0).then_inc(vec_copied, 1)
                with act.Fori(1, UP // 2) as i:
                    for u in range(2):
                        up(i, u)
                n = base + UP + 2
                hi(0, n)
                with act.Fori(0, (DOWN - 3) // 2) as i:
                    for u in range(1, 3):
                        hi(i, n + u)
                if p == 0:
                    hi(0, PROJ, paired=True)
                for m in range(KD):
                    take_y(p, m)
                root(2 * p + 1)

            hi(0, 0)
            hi(0, 1)
            split_norm(0)
            ffn(FFN1, 0, 0, 0)
            split_norm(1)
            hi(0, PROJ + 1, paired=True)

            def take(dst, src, scale, strided):
                if strided:
                    dst = dst.rearrange("p (r l) -> p l r", r=4)
                    src = src.rearrange("p (l r) -> p l r", r=4)
                act.activation(dst, src, ACT.Copy, scale=scale).then_inc(act_read, 1)

            for i in range(NPROJ):
                n = PROJ + i
                act.wait_ge(w_used, n + 1)
                src = ps[:, 2 * (n % 2), :]
                if i < 2:
                    take(qn[:, 2 * i, :], src, -SCALE, False)
                elif i < 4:
                    take(kv4[:, 2 * (i - 2), :], src, 1.0, False)
                elif i < 7:
                    take(qd[:, 2 * (i - 4), :], src, -SCALE, i > 4)
                else:
                    take(kd[:, 2 * (i - 7), :], src, 1.0, i > 7)
                hi(0, n + 2)
                if i == 1:
                    act.wait_ge(wg_loaded, 16)
                    act.activation(wg_hi[:, :, :], wg_raw[:, :, :], ACT.Copy).then_inc(wg_hi_ready, 1)
                if i in (6, 8):
                    act.wait_ge(blk_ready, 2 if i == 6 else 4)
                    act.activation((kb_hi if i == 6 else vb_hi)[:, :, :], blk[:, :, :], ACT.Copy).then_inc(bhi_ready, 1)
            for i in range(NV):
                n = VST + i
                act.wait_ge(w_used, n + 1)
                act.activation(v_all[:, 0:2, 256 * i:256 * i + 256],
                               ps[:, 2 * (n % 2), :].rearrange("p (t c) -> p t c", c=256), ACT.Copy).then_inc(act_read, 1)
                hi(0, n + 2)
            for i in range(NCOMP):
                n = COMP + i
                act.wait_ge(w_used, n + 1)
                hi(0, n + 2)
                if i % 2:
                    for c in range(2):
                        src, dst = ps[:, 4 + 2 * (i // 2) + c, 0:64], hid_k[:, c, :]
                        if i == 3:
                            dst = hid_v[:, c, :, :, :]
                            src = src.rearrange("p (g n) -> p g n", g=NSA_G).unsqueeze(2).broadcast_to([P, NSA_G, HPG, CPAD])
                        act.activation(dst, src, ACT.Silu).then_inc(hid_ready, 1)
            act.wait_ge(gn_done, 1)
            act.activation(gates[:, :, :, :].rearrange("p t h b -> p t (h b)"),
                           ps[:, 3, 0:NT * 24].rearrange("p (t c) -> p t c", c=24), ACT.Sigmoid).then_inc(gates_ready, 1)

            def exps(u):
                act.wait_ge(s_biased, u + 1)
                if u >= 2:
                    act.wait_ge(pT_done, u - 1)
                c0 = 0
                for row in ALL[u]:
                    c1 = c0 + P * len(row[3])
                    least, den = stats_of(u)(row)
                    e = act.activation(p_sb[:, u % 2, c0:c1], s_sb[:, u % 2, c0:c1], ACT.Exp, bias=least,
                                       scale=-1.0, accum_out=den)
                    c0 = c1
                e.then_inc(p_ready, 1)

            def take_o(u):
                act.wait_ge(pv_done, u + 1)
                _, j, r0, _ = ALL[u][0]
                rows = len(ALL[u])
                act.activation(o_dil[:, j // SLOTS, r0:r0 + rows, j % SLOTS, :],
                               heads2(ps[:, 5 + u % 2, 0:HD * rows]), ACT.Copy).then_inc(o_read, 1)

            for u in range(NDU + 3):
                if u < NDU:
                    exps(u)
                if u >= 3:
                    take_o(u - 3)
            act.wait_ge(pT_done, NDU)
            for t in range(NT):
                act.wait_ge(sc_sub, t + 1)
                if t >= 2:
                    act.wait_ge(pcT_done, t - 1)
                act.activation(p_sb[:, t % 2, 0:256], s_sb[:, t % 2, 0:256], ACT.Exp, scale=-1.0).then_inc(pc_ready, 1)
            act.wait_ge(pcT_done, NT)
            for u in range(NDU, NU):
                exps(u)
                if u == NDU + 8:
                    act.wait_ge(e_in, 1)
                    act.activation(e_n[:, :, :, :], e_n[:, :, :, :], ACT.Exp, scale=-1.0).then_inc(e_ready, 1)

            act.wait_ge(y_nsa_ready, 1)
            for i in range(NGATE):
                n = GATE + i
                act.wait_ge(w_used, n + 1)
                for c in range(2):
                    e = act.activation(sig[:, 2 * i + c, :], ps[:, 2 * (n % 2) + c, :], ACT.Sigmoid)
                e.then_inc(act_read, 1)
                hi(0, n + 2)
                if i == 4:
                    for c in range(2):
                        act.wait_ge(yd_summed, 3 * (c + 1))
                        act.activation(yd_hi[:, c, :], yd[:, c, :], ACT.Copy).then_inc(ydhi_ready, 1)
                if i == 6:
                    for c in range(4):
                        act.wait_ge(ynT_done, c + 1)
                        act.activation(yn_hi[:, c, :], ps[:, 4 + c, :], ACT.Copy).then_inc(ynhi_ready, 1)
            hi(0, BDIL + 2)
            for i in range(2):
                for m in range(4 * i, 4 * i + 4):
                    act.wait_ge(merged, m + 1)
                    act.activation(xn_hi[:, m, :], mrg[:, m % 2, 1, :], ACT.Copy).then_inc(mhi_ready, 1)
                hi(0, BNSA + i + 2)
            for i in range(4):
                take_y(1, 2 * i)
                take_y(1, 2 * i + 1)
                if i < 3:
                    hi(0, OUT + i + 2)
            root(3)
            split_norm(2)
            hi(0, FFN2 + 1)
            ffn(FFN2, PAIR_FFN2, UP, 2)
            for m in range(KD):
                act.wait_ge(oT_done, m + 1)
                act.activation(o_tok[:, :, m * P:m * P + P], ps[:, m % 4, :].rearrange("p (t c) -> p t c", c=P),
                               ACT.Copy).then_inc(o_copied, 1)

        @block.vector
        def _(dve):
            chained = [0]

            def chain(instruction):
                chained[0] += 1
                instruction.then_inc(dve_chain, 1)
                dve.wait_ge(dve_chain, chained[0])

            def lo(i, c, paired=False):
                dve.wait_ge(hi_ready, 2 * i + (c + 1))
                whole = [(ring_lo[:, c % 2, :], ring_raw[:, c % 2, :])]
                rounded = [ring_hi[:, c % 2, :]]
                if paired:
                    whole, rounded = paired_views(ring_lo, c), [dst for dst, _ in paired_views(ring_hi, c)]
                for (dst, src), r in zip(whole, rounded):
                    e = dve.tensor_tensor(dst, src, f32(r), ALU.subtract)
                e.then_inc(lo_ready, 1)

            def invert(i):
                dve.wait_ge(sd_ready, i + 1)
                dve.reciprocal(rstd[:, :], sd[:, :]).then_inc(rstd_ready, 1)
                dve.wait_ge(rb_ready, i + 1)

            def split_norm(r, g):
                invert(2 * r)
                for m in range(KD + 1):
                    if m < KD:
                        dve.scalar_tensor_tensor(out=ysb[:, m, :], in0=xres[:, m, :], scalar=gains[:, g, m:m + 1],
                                                 in1=ps[:, 7, :], op0=ALU.mult, op1=ALU.mult).then_inc(u_ready, 1)
                    if m:
                        dve.wait_ge(xhi_ready, KD * r + m)
                        dve.tensor_tensor(xn_lo[:, m - 1, :], ysb[:, m - 1, :], f32(xn_hi[:, m - 1, :]),
                                          ALU.subtract).then_inc(xlo_ready, 1)

            def sum_y(p, m):
                dve.wait_ge(y_squared, KD * p + m + 1)
                if m >= 2:
                    dve.wait_ge(y_summed, 7 * p + m - 1)
                dve.tensor_tensor(acc[:, :], acc[:, :], sq[:, :], ALU.add).then_inc(y_summed, 1)

            def add_y(p, g):
                invert(2 * p + 1)
                for m in range(KD + 1):
                    if m < KD:
                        dve.scalar_tensor_tensor(out=ysb[:, m, :], in0=ysb[:, m, :], scalar=gains[:, g, m:m + 1],
                                                 in1=ps[:, 5, :], op0=ALU.mult, op1=ALU.mult).then_inc(x_scaled, 1)
                    if m:
                        dve.wait_ge(x_scaled, KD * p + m)
                        dve.tensor_tensor(xres[:, m - 1, :], xres[:, m - 1, :], ysb[:, m - 1, :],
                                          ALU.add).then_inc(x_new, 1)

            def ffn(base, pair0, h0, p, g):
                def up(i, u):
                    slot = (base + u) % 2
                    dve.wait_ge(act_read, 2 * i + (pair0 + u + 1))
                    if not (isinstance(i, int) and 2 * i + u < 2):
                        dve.wait_ge(hhi_ready, 2 * i + (h0 + u - 1))
                    dve.tensor_tensor(h_f32[:, u, :], silu_g[:, u, :], ps[:, 2 * slot + 1, :],
                                      ALU.mult).then_inc(h_ready, 1)
                    lo(i, base + u + 2)
                    dve.wait_ge(hhi_ready, 2 * i + (h0 + u + 1))
                    at_j = bass.ds(i * (2 * S) + u * S, S)
                    dve.tensor_tensor(hT_lo[:, at_j], h_f32[:, u, :], f32(hT_hi[:, at_j]),
                                      ALU.subtract).then_inc(hlo_ready, 1)

                for u in range(2):
                    up(0, u)
                if p == 0:
                    dve.wait_ge(vec_stored, 16)
                with dve.Fori(1, UP // 2) as i:
                    for u in range(2):
                        up(i, u)
                n = base + UP + 2
                lo(0, n)
                with dve.Fori(0, (DOWN - 3) // 2) as i:
                    for u in range(1, 3):
                        lo(i, n + u)
                if p == 0:
                    lo(0, PROJ, paired=True)
                for m in range(1, KD):
                    sum_y(p, m)
                add_y(p, g)

            dve.memset(tab[BUCKETS:BUCKETS + 1, :], -MASKED).then_inc(tab_ready, 1)
            dve.wait_ge(cT_gains, 1)
            chain(dve.tensor_copy(gains[:, :, :].rearrange("p a b -> p (a b)"), ps[:, 5, 0:6 * KD]))
            dve.tensor_copy(posT[:, :, :].rearrange("p a b -> p (a b)"), ps[:, 5, 6 * KD:80])
            for g in (1, 5):
                e = dve.tensor_scalar(gains[:, g, :], gains[:, g, :], 0.5, None, ALU.mult)
            chain(e)
            for m in range(KD):
                dve.wait_ge(xT_done, m + 1)
                dve.tensor_copy(xres[:, m, :], ps[:, m % 4, :]).then_inc(x_new, 1)
            lo(0, 0)
            lo(0, 1)
            split_norm(0, 0)
            ffn(FFN1, 0, 0, 0, 1)
            split_norm(1, 2)
            lo(0, PROJ + 1, paired=True)

            dve.wait_ge(xlo_ready, 2 * KD)
            chain(dve.memset(vc_diag[:, :, :], 0.0))

            def take(dst, src, scale, strided):
                if strided:
                    dst = dst.rearrange("p (r l) -> p l r", r=4)
                    src = src.rearrange("p (l r) -> p l r", r=4)
                dve.tensor_scalar(dst, src, scale, None, ALU.mult).then_inc(dve_read, 1)

            def blocks(i, pair):
                dve.wait_ge(pairs_loaded[i], 64)
                if i == 0:
                    chain(dve.memset(blk[:, :, :], 0.0))
                else:
                    dve.wait_ge(blo_ready, i)
                    dve.wait_ge(bhi_ready, i)
                for g in range(NSA_G):
                    src = pair[:, g, :].rearrange("p (n l) -> p l n", l=CS)
                    for half in range(2):
                        dst = blk[:, 8 * half:8 * half + 8, g * CPAD:g * CPAD + NCMP]
                        e = dve.tensor_tensor(dst, src[:, 0:CS:2, half:half + NCMP],
                                              posT[:, i, 8 * half:8 * half + 8].unsqueeze(2).broadcast_to([P, 8, NCMP]),
                                              ALU.add)
                    e.then_inc(blk_ready, 1)

            for i in range(NPROJ):
                n = PROJ + i
                dve.wait_ge(w_used, n + 1)
                src = ps[:, 2 * (n % 2) + 1, :]
                if i < 2:
                    take(qn[:, 2 * i + 1, :], src, -SCALE, False)
                elif i < 4:
                    take(kv4[:, 2 * (i - 2) + 1, :], src, 1.0, False)
                elif i < 7:
                    take(qd[:, 2 * (i - 4) + 1, :], src, -SCALE, i > 4)
                else:
                    take(kd[:, 2 * (i - 7) + 1, :], src, 1.0, i > 7)
                lo(0, n + 2)
                if i == 1:
                    dve.wait_ge(wg_hi_ready, 1)
                    dve.tensor_tensor(wg_lo[:, :, :], wg_raw[:, :, :], f32(wg_hi[:, :, :]), ALU.subtract).then_inc(wg_lo_ready, 1)
                if i in (5, 7):
                    blocks((i - 5) // 2, pair_k if i == 5 else pair_v)
                if i in (6, 8):
                    b_hi, b_lo = (kb_hi, kb_lo) if i == 6 else (vb_hi, vb_lo)
                    dve.wait_ge(bhi_ready, (i - 4) // 2)
                    dve.tensor_tensor(b_lo[:, :, :], blk[:, :, :], f32(b_hi[:, :, :]), ALU.subtract).then_inc(blo_ready, 1)
            for i in range(NV):
                n = VST + i
                dve.wait_ge(w_used, n + 1)
                dve.tensor_copy(v_all[:, 2:4, 256 * i:256 * i + 256],
                                ps[:, 2 * (n % 2) + 1, :].rearrange("p (t c) -> p t c", c=256)).then_inc(dve_read, 1)
                lo(0, n + 2)
            for i in range(NCOMP):
                lo(0, COMP + i + 2)
            dve.wait_ge(c2_done, 2)
            dve.tensor_copy(kcT[0:HD, :], ps[0:HD, 4, 0:CPAD])
            dve.tensor_copy(kcT[HD:P, :], ps[HD:P, 4, CPAD:2 * CPAD])
            for h in range(HPG):
                rows = slice(h * CPAD, (h + 1) * CPAD)
                e = dve.tensor_copy(vc_diag[rows, :, h * HD:h * HD + HD], heads2(ps[rows, 5, 0:NSA_G * HD]))
            e.then_inc(kc_ready, 1)

            def bias_of(row):
                kind, h, t, keys = row
                if kind == "d0":
                    return bias_d0[:, h, DIL_KEYS - P * len(keys):DIL_KEYS]
                if kind == "d12":
                    return bias_d12[:, h - SLOTS, :]
                return bias_n[:, h, S - P * len(keys):S]

            def add_bias(u):
                dve.wait_ge(s_done, u + 1)
                if u >= 2:
                    dve.wait_ge(p_ready, u - 1)
                c0 = 0
                for row in ALL[u]:
                    c1 = c0 + P * len(row[3])
                    least, _ = stats_of(u)(row)
                    e = dve.tensor_tensor_reduce(out=s_sb[:, u % 2, c0:c1], in0=ps[:, u % 3, c0:c1], in1=bias_of(row),
                                                 scale=1.0, scalar=BIGGEST, op0=ALU.add, op1=ALU.min, accum_out=least)
                    c0 = c1
                e.then_inc(s_biased, 1)

            def take_pT(u):
                dve.wait_ge(pT_done, u + 1)
                if u >= 2:
                    dve.wait_ge(pv_done, u - 1)
                w = P * sum(len(row[3]) for row in ALL[u])
                dve.tensor_copy(pT_sb[:, u % 2, 0:w], ps[:, 3 + u % 2, 0:w]).then_inc(pT_ready, 1)

            dve.wait_ge(biases_loaded, 48)
            for u in range(NDU + 2):
                if u < NDU:
                    add_bias(u)
                if u >= 2:
                    take_pT(u - 2)

            dve.wait_ge(p_ready, NDU)
            dve.wait_ge(pv_done, NDU)
            dve.wait_ge(gates_ready, 1)
            by_head = lambda ap: ap.rearrange("p (h n) -> p h n", n=CPAD)
            spread_head = lambda ap, n: ap.unsqueeze(2).broadcast_to([P, NSA_H, n])

            def cmp_scores(t):
                dve.wait_ge(sc_done, t + 1)
                b0, b1 = cmp_banks(t)
                both = ps[:, b0:b1 + 1, 0:P].rearrange("p g (h n) -> p g h n", n=CPAD)
                least = nm_c[:, t % 2, :].rearrange("p (g h) -> p g h", g=NSA_G)
                chain(dve.tensor_reduce(least, both, AX_X, ALU.min))
                if t >= 2:
                    dve.wait_ge(pc_ready, t - 1)
                dve.tensor_tensor(s_sb[:, t % 2, 0:256].rearrange("p (g h n) -> p g h n", g=NSA_G, n=CPAD), both,
                                  least.unsqueeze(3).broadcast_to([P, NSA_G, HPG, CPAD]), ALU.subtract).then_inc(sc_sub, 1)

            def cmp_out(t):
                dve.wait_ge(pc_ready, t + 1)
                chain(dve.tensor_reduce(den_c[:, :], by_head(p_sb[:, t % 2, 0:256]), AX_X, ALU.add))
                chain(dve.reciprocal(den_c[:, :], den_c[:, :]))
                chain(dve.tensor_tensor(f_c[:, t, :], den_c[:, :], gates[:, t, :, 0], ALU.mult))
                if t == 0:
                    chain(dve.tensor_scalar(f_c[:, t, :], f_c[:, t, :], valid[:, :], None, ALU.mult))
                dve.wait_ge(pcT_done, t + 1)
                if t >= 2:
                    dve.wait_ge(oc_done, t - 1)
                dve.tensor_copy(pT_sb[:, t % 2, 0:256], ps[:, 4 + 3 * (t % 2), 0:256]).then_inc(pcT_ready, 1)
                dve.wait_ge(oc_done, t + 1)
                dve.tensor_tensor(y_nsa[:, t, :, :], heads2(ps[:, 5 + t % 2, :]), spread_head(f_c[:, t, :], HD),
                                  ALU.mult).then_inc(yc_ready, 1)

            for t in range(NT + 1):
                if t < NT:
                    cmp_scores(t)
                if t:
                    cmp_out(t - 1)

            def take_head(turn):
                h = turn // 2 + HPG * (turn % 2)
                o8 = 8 * (turn % 2)
                u1 = NDU + 5 * (turn + 1)
                dve.wait_ge(p_ready, u1)
                den = stat_d[:, o8:o8 + 8]
                f = f_nsa[:, turn % 2, :]
                chain(dve.reciprocal(f, den))
                odd, even = f[:, 0:4].rearrange("p (t b) -> p t b", b=2), f[:, 4:8].rearrange("p (b t) -> p t b", b=2)
                dve.tensor_tensor(odd, odd, gates[:, 1:NT:2, h, 1:3], ALU.mult)
                chain(dve.tensor_tensor(even, even, gates[:, 0:NT:2, h, 1:3], ALU.mult))
                dve.wait_ge(pv_done, u1)
                o = o_tmp[:, turn % 2, :].rearrange("p (b t d) -> p t b d", b=2, d=HD)
                o_ps = ps[:, 5 + turn % 2, :]
                spread4 = lambda ap: ap.unsqueeze(3).broadcast_to([P, 2, 2, HD])
                dve.tensor_tensor(o[:, 1:NT:2], o_ps[:, 0:256].rearrange("p (t b d) -> p t b d", b=2, d=HD), spread4(odd), ALU.mult)
                dve.tensor_tensor(o[:, 0:NT:2], o_ps[:, 256:512].rearrange("p (b t d) -> p t b d", b=2, d=HD), spread4(even),
                                  ALU.mult).then_inc(o_nsa_read, 1)
                dve.wait_ge(o_nsa_read, turn + 1)
                for b in range(2):
                    chain(dve.tensor_tensor(y_nsa[:, :, h, :], y_nsa[:, :, h, :],
                                            heads2(o_tmp[:, turn % 2, b * 256:b * 256 + 256]), ALU.add))

            def dil_weights():
                dve.wait_ge(stats_loaded, 16)
                st = lambda g, k: st_0[:, :, k, :] if g == 0 else st_n[:, :, 2 * (g - 1) + k, :]
                chain(dve.tensor_tensor(w_n[:, :, :], st(0, 0), st(1, 0), ALU.min))
                chain(dve.tensor_tensor(w_n[:, :, :], w_n[:, :, :], st(2, 0), ALU.min))
                for g in range(3):
                    e = dve.tensor_tensor(e_n[:, g, :, :], st(g, 0), w_n[:, :, :], ALU.subtract)
                e.then_inc(e_in, 1)

            def dil_norm():
                st = lambda g, k: st_0[:, :, k, :] if g == 0 else st_n[:, :, 2 * (g - 1) + k, :]
                dve.wait_ge(e_ready, 1)
                chain(dve.tensor_tensor(w_n[:, :, :], e_n[:, 0, :, :], st(0, 1), ALU.mult))
                for g in (1, 2):
                    chain(dve.tensor_tensor(st(g, 1), e_n[:, g, :, :], st(g, 1), ALU.mult))
                    chain(dve.tensor_tensor(w_n[:, :, :], w_n[:, :, :], st(g, 1), ALU.add))
                chain(dve.reciprocal(w_n[:, :, :], w_n[:, :, :]))
                for g in (1, 2):
                    dve.tensor_tensor(c_n[:, :, g - 1, :], e_n[:, g, :, :], w_n[:, :, :], ALU.mult)
                dve.tensor_tensor(e_n[:, 0, :, :], e_n[:, 0, :, :], w_n[:, :, :], ALU.mult).then_inc(c_ready, 1)

            dve.wait_ge(bias_n_loaded, 16)
            dve.wait_ge(pc_ready, NT)
            dve.wait_ge(oc_done, NT)
            for i in range(NNU + 5):
                u = NDU + i
                if i < NNU:
                    add_bias(u)
                if 2 <= i < NNU + 2:
                    take_pT(u - 2)
                if i == 6:
                    dil_weights()
                if i == 11:
                    dil_norm()
                if i >= 9 and (i - 9) % 5 == 0:
                    take_head((i - 9) // 5)
            e = dve.memset(w_n[:, :, :], 0.0)
            e.then_inc(y_nsa_ready, 1)

            for i in range(NGATE):
                lo(0, GATE + i + 2)
                if i == 3:
                    for c in range(2):
                        for g in range(3):
                            dve.wait_ge(ydT_done, 3 * c + g + 1)
                            src = ps[:, 4 + (3 * c + g) % 4, :]
                            if g == 0:
                                dve.tensor_copy(yd[:, c, :], src).then_inc(yd_summed, 1)
                            else:
                                dve.wait_ge(yd_summed, 3 * c + g)
                                dst = yd[:, c, :].rearrange("p (l r) -> p r l", r=4)
                                dve.tensor_tensor(dst, src.rearrange("p (r l) -> p r l", r=4), dst,
                                                  ALU.add).then_inc(yd_summed, 1)
                if i == 4:
                    for c in range(2):
                        dve.wait_ge(ydhi_ready, c + 1)
                        dve.tensor_tensor(yd_lo[:, c, :], yd[:, c, :], f32(yd_hi[:, c, :]), ALU.subtract).then_inc(ydlo_ready, 1)
                if i == 6:
                    for c in range(4):
                        dve.wait_ge(ynhi_ready, c + 1)
                        dve.tensor_tensor(yn_lo[:, c, :], ps[:, 4 + c, :], f32(yn_hi[:, c, :]), ALU.subtract).then_inc(ynlo_ready, 1)
            dve.wait_ge(act_read, PAIR_FFN2)
            for m in range(KD):
                dve.wait_ge(*b_event(m))
                dve.tensor_tensor(sig[:, KD + m, :], sig[:, KD + m, :], ps[:, 4 + m % 4, :], ALU.mult).then_inc(b_gated, 1)
            lo(0, BDIL + 2)
            for m in range(KD):
                dve.wait_ge(*a_event(m))
                if m == 0:
                    dve.wait_ge(b_gated, KD)
                if m >= 2:
                    dve.wait_ge(mhi_ready, m - 1)
                dve.tensor_tensor(mrg[:, m % 2, 0, :], sig[:, m, :], ps[:, m % 4, :], ALU.mult).then_inc(a_gated, 1)
                dve.wait_ge(a_gated, m + 1)
                dve.tensor_tensor(mrg[:, m % 2, 1, :], mrg[:, m % 2, 0, :], sig[:, KD + m, :], ALU.add).then_inc(merged, 1)
                dve.wait_ge(mhi_ready, m + 1)
                dve.tensor_tensor(xn_lo[:, m, :], mrg[:, m % 2, 1, :], f32(xn_hi[:, m, :]), ALU.subtract).then_inc(mlo_ready, 1)
                if m % 4 == 3:
                    lo(0, BNSA + m // 4 + 2)
            for i in range(4):
                for m in (2 * i, 2 * i + 1):
                    if m:
                        sum_y(1, m)
                if i < 3:
                    lo(0, OUT + i + 2)
            add_y(1, 3)
            split_norm(2, 4)
            lo(0, FFN2 + 1)
            ffn(FFN2, PAIR_FFN2, UP, 2, 5)

        @block.tensor
        def _(pe):
            def part(kind, slot, k0, width):
                return ring[kind][:, slot, k0:k0 + width]

            def cols_step(slot, norm=None):
                for k in range(KD):
                    if norm is not None:
                        pe.wait_ge(xlo_ready, KD * norm + k + 1)
                    for c in range(2):
                        for i, (a, b) in enumerate(MODES):
                            e = pe.matmul(ps[:, 2 * slot + c, :], part(a, slot, k * 256 + c * P, P), xn[b][:, k, :],
                                          start=(k == 0 and i == 0), stop=(k == KD - 1 and i == 2))
                e.then_inc(w_used, 1)

            def column_sums(bank, src, first, last):
                for t in range(NT):
                    e = pe.matmul(ps[:, bank, t:t + 1], src[:, t * P:t * P + P], ones[:, :],
                                  start=(first and t == 0), stop=last, skip_group_check=True)
                return e

            def spread_rstd(i, bank):
                pe.wait_ge(rstd_ready, i + 1)
                for t in range(NT):
                    e = pe.matmul(ps[:, bank, t * P:t * P + P], rstd[:, t:t + 1].broadcast_to([P, P]), ident[:, :],
                                  start=True, stop=True)
                e.then_inc(rb_ready, 1)

            def split_norm(r):
                for m in range(KD):
                    pe.wait_ge(x_squared, KD * r + m + 1)
                    e = column_sums(6, ysb[:, m, :], m == 0, m == KD - 1)
                e.then_inc(ss_done, 1)
                spread_rstd(2 * r, 7)

            def norm_y(p):
                pe.wait_ge(y_summed, 7 * p + 7)
                column_sums(4, acc[:, :], True, True).then_inc(ss_done, 1)
                spread_rstd(2 * p + 1, 5)

            def ffn(base, pair0, h0, p, norm):
                def up(i, u):
                    pe.wait_ge(lo_ready, 2 * i + (base + u + 1))
                    if not (isinstance(i, int) and 2 * i + u < 2):
                        pe.wait_ge(h_ready, 2 * i + (h0 + u - 1))
                    cols_step((base + u) % 2, norm if isinstance(i, int) and 2 * i + u == 0 else None)

                def down(i, u, order=range(KD), start=False, stop=False):
                    n0 = base + UP + u
                    pe.wait_ge(lo_ready, 2 * i + (n0 + 1))
                    for m in order:
                        if start and m == 0:
                            pe.wait_ge(h_ready, h0 + UP)
                        for kk in range(2):
                            at_k = bass.ds(i * (4 * S) + (2 * u + kk) * S, S)
                            for q, (a, b) in enumerate(MODES):
                                e = pe.matmul(ps[:, m, :], part(a, n0 % 2, kk * D + m * P, P), hT[b][:, at_k],
                                              start=(start and kk == 0 and q == 0), stop=(stop and kk == 1 and q == 2),
                                              skip_group_check=True)
                        if stop and m < KD - 1:
                            e.then_inc(y_done, 1)
                    e.then_inc(w_used, 1)

                for u in range(2):
                    up(0, u)
                if p == 0:
                    pe.wait_ge(small_loaded, 32)
                    pe.wait_ge(tab_ready, 1)
                    for c in range(5):
                        if c >= 2:
                            pe.wait_ge(vec_copied, c - 1)
                        w = min(S, TAB_W - c * S)
                        pe.matmul(ps[0:20, 4 + c % 2, 0:w], tab[0:BUCKETS + 1, :], onehot_sb[0:BUCKETS + 1, c * S:c * S + w],
                                  start=True, stop=True).then_inc(vec_mm, 1)
                with pe.Fori(1, UP // 2) as i:
                    for u in range(2):
                        up(i, u)
                pe.wait_ge(hlo_ready, h0 + UP - 2)
                if p == 0:
                    pe.wait_ge(vec_copied, 5)
                down(0, 0, order=(4, 5, 6, 7, 0, 1, 2, 3), start=True)
                with pe.Fori(0, (DOWN - 3) // 2) as i:
                    for u in range(1, 3):
                        down(i, u)
                down(0, DOWN - 2)
                pe.wait_ge(hlo_ready, h0 + UP)
                down(0, DOWN - 1, stop=True)
                norm_y(p)

            pe.wait_ge(consts, 6)
            pe.wait_ge(gains_loaded, 128)
            pe.transpose(ps[:, 5, 0:80], gains_row[0:80, :], ident[0:80, 0:80]).then_inc(cT_gains, 1)
            pe.wait_ge(x_loaded, 64)
            for m in range(KD):
                if m >= 4:
                    pe.wait_ge(x_new, m - 3)
                for t in range(NT):
                    e = pe.transpose(ps[:, m % 4, t * P:t * P + P], x_tok[:, t, m * P:m * P + P], ident[:, :])
                e.then_inc(xT_done, 1)
            split_norm(0)
            ffn(FFN1, 0, 0, 0, 0)
            split_norm(1)

            def proj(i, u):
                pe.wait_ge(lo_ready, 2 * i + (PROJ + u + 1))
                if not (isinstance(i, int) and i == 0):
                    pe.wait_ge(act_read, 2 * i + (PAIR_PROJ + u - 1))
                    pe.wait_ge(dve_read, 2 * i + (u - 1))
                cols_step((PROJ + u) % 2, 1 if isinstance(i, int) and i == 0 and u == 0 else None)

            for u in range(2):
                proj(0, u)
            with pe.Fori(1, NPROJ // 2) as i:
                for u in range(2):
                    proj(i, u)
            for i in range(NV):
                n = VST + i
                slot = n % 2
                pe.wait_ge(lo_ready, n + 1)
                pe.wait_ge(act_read, PAIR_PROJ + NPROJ + i - 1)
                pe.wait_ge(dve_read, NPROJ + i - 1)
                for t in range(NT):
                    tokens = slice(t * P, t * P + P) if i < 2 else slice(t, S, 4)
                    for k in range(KD):
                        for q, (a, b) in enumerate(MODES):
                            e = pe.matmul(ps[:, 2 * slot + t // 2, (t % 2) * 256:(t % 2) * 256 + 256],
                                          xn[b][:, k, tokens], part(a, slot, k * 256, 256),
                                          start=(k == 0 and q == 0), stop=(k == KD - 1 and q == 2))
                e.then_inc(w_used, 1)
            for i in range(NCOMP):
                n = COMP + i
                pe.wait_ge(lo_ready, n + 1)
                kv = i // 2
                if i % 2 == 0:
                    pe.wait_ge(blo_ready, kv + 1)
                blocks = ((kb_hi, kb_lo), (vb_hi, vb_lo))[kv]
                for c in range(2):
                    for l in range(8):
                        for q, (a, b) in enumerate(MODES):
                            e = pe.matmul(ps[:, 4 + 2 * kv + c, 0:64], part(a, n % 2, l * 256 + c * P, P),
                                          blocks[b][:, 8 * (i % 2) + l, :],
                                          start=(i % 2 == 0 and l == 0 and q == 0), stop=(i % 2 == 1 and l == 7 and q == 2),
                                          skip_group_check=True)
                e.then_inc(w_used, 1)
            pe.wait_ge(wg_lo_ready, 1)
            pe.wait_ge(dve_read, NPROJ + NV)
            pe.wait_ge(act_read, PAIR_GATE)
            wg = (wg_hi, wg_lo)
            for t in range(NT):
                for k in range(KD):
                    for q, (a, b) in enumerate(MODES):
                        e = pe.matmul(ps[:, 3, t * 24:t * 24 + 24], xn[b][:, k, t * P:t * P + P], wg[a][:, k, :],
                                      start=(k == 0 and q == 0), stop=(k == KD - 1 and q == 2))
            e.then_inc(gn_done, 1)
            pe.wait_ge(w2_loaded, 48)
            pe.wait_ge(hid_ready, 4)
            for c in range(2):
                e = pe.matmul(ps[:, 4, 0:64], w2k[:, c, :, :].rearrange("p a b -> p (a b)"), hid_k[:, c, :],
                              start=(c == 0), stop=(c == 1))
            e.then_inc(c2_done, 1)
            for g in range(NSA_G):
                for c in range(2):
                    e = pe.matmul(ps[:, 5, g * HD:g * HD + HD],
                                  hid_v[:, c, g, :, :].rearrange("p a b -> p (a b)"), w2v[:, c, :], start=(c == 0), stop=(c == 1))
            e.then_inc(c2_done, 1)

            def widen(row):
                kind, h, t, _ = row
                if (kind, t) == ("w", 0) or h == DIL_H - 1:
                    return 0, 0
                return (HD, 0) if (kind, t) == ("w", 2) else (0, HD)

            def operands(row):
                before, after = widen(row)
                kind, h, t, keys = row
                if kind[0] == "d":
                    rows = slice((h % 2) * HD, (h % 2) * HD + HD)
                    q = qd[rows, h // 2, t * P:t * P + P]
                    k = kd[rows, h // 2, keys[0] * P:(keys[-1] + 1) * P]
                    v = [v_all[:, x, 256 + h * HD:256 + h * HD + HD + after] for x in keys]
                else:
                    g = h // HPG
                    rows = slice(g * HD, g * HD + HD)
                    q = qn[rows, h % HPG, t * P:t * P + P]
                    k = kv4[rows, 2 + (kind == "w"), keys[0] * P:(keys[-1] + 1) * P]
                    c0 = (kind == "w") * P + g * HD
                    v = [v_all[:, x, c0 - before:c0 + HD + after] for x in keys]
                return q, k, v

            def scores(u):
                if u >= 3:
                    pe.wait_ge(s_biased, u - 2)
                c0 = 0
                for row in ALL[u]:
                    q, k, _ = operands(row)
                    c1 = c0 + P * len(row[3])
                    e = pe.matmul(ps[:, u % 3, c0:c1], q, k, start=True, stop=True)
                    c0 = c1
                e.then_inc(s_done, 1)

            def transposes(u):
                pe.wait_ge(p_ready, u + 1)
                if u >= 2:
                    pe.wait_ge(pT_ready, u - 1)
                n = sum(len(row[3]) for row in ALL[u])
                for x in range(n):
                    e = pe.transpose(ps[:, 3 + u % 2, x * P:x * P + P], p_sb[:, u % 2, x * P:x * P + P], ident[:, :])
                e.then_inc(pT_done, 1)

            def values(u):
                pe.wait_ge(pT_ready, u + 1)
                x = 0
                for i, row in enumerate(ALL[u]):
                    _, _, v = operands(row)
                    if u < NDU:
                        bank, o0 = 5 + u % 2, i * HD
                    else:
                        bank, o0 = 5 + (u - NDU) // 5 % 2, place(row) * HD
                    before, after = widen(row)
                    for j, vj in enumerate(v):
                        e = pe.matmul(ps[:, bank, o0 - before:o0 + HD + after], pT_sb[:, u % 2, x * P:x * P + P], vj,
                                      start=(j == 0), stop=(j == len(v) - 1))
                        x += 1
                e.then_inc(pv_done, 1)

            pe.wait_ge(kc_ready, 1)
            pe.wait_ge(gates_ready, 1)
            for i in range(NDU + 3):
                if i < NDU:
                    scores(i)
                if 2 <= i < NDU + 2:
                    transposes(i - 2)
                if i >= 3:
                    if i >= 5:
                        pe.wait_ge(o_read, i - 4)
                    values(i - 3)
            pe.wait_ge(cmp_loaded, 16 * NSA_H)
            pe.wait_ge(s_biased, NDU)
            pe.wait_ge(pT_ready, NDU)
            pe.wait_ge(o_read, NDU)

            def cmp_scores(t):
                banks = cmp_banks(t)
                if t >= 2:
                    pe.wait_ge(sc_sub, t - 1)
                for g in range(NSA_G):
                    pe.matmul(ps[:, banks[g], 0:P], bias_cT[:, g, t * P:t * P + P], ident[:, :],
                              start=True, stop=False, skip_group_check=True)
                for h in range(NSA_H):
                    rows = slice((h // HPG) * HD, (h // HPG) * HD + HD)
                    c0 = h % HPG * CPAD
                    e = pe.matmul(ps[:, banks[h // HPG], c0:c0 + CPAD], qn[rows, h % HPG, t * P:t * P + P],
                                  kcT[rows, :], start=False, stop=True, skip_group_check=True)
                e.then_inc(sc_done, 1)

            for t in range(NT + 1):
                if t < NT:
                    cmp_scores(t)
                if t:
                    s = t - 1
                    pe.wait_ge(pc_ready, s + 1)
                    if s >= 2:
                        pe.wait_ge(pcT_ready, s - 1)
                    for g in range(NSA_G):
                        e = pe.transpose(ps[:, 4 + 3 * (s % 2), g * P:g * P + P], p_sb[:, s % 2, g * P:g * P + P], ident[:, :])
                    e.then_inc(pcT_done, 1)
                    pe.wait_ge(pcT_ready, s + 1)
                    if s >= 2:
                        pe.wait_ge(yc_ready, s - 1)
                    for g in range(NSA_G):
                        e = pe.matmul(ps[:, 5 + s % 2, g * 256:g * 256 + 256], pT_sb[:, s % 2, g * P:g * P + P],
                                      vc_diag[:, g, :], start=True, stop=True)
                    e.then_inc(oc_done, 1)
            pe.wait_ge(sc_sub, NT)
            pe.wait_ge(yc_ready, NT)
            for i in range(NNU + 3):
                u = NDU + i
                if i < NNU:
                    scores(u)
                if 2 <= i < NNU + 2:
                    transposes(u - 2)
                if i >= 3:
                    if i >= 13 and (i - 3) % 5 == 0:
                        pe.wait_ge(o_nsa_read, (i - 3) // 5 - 1)
                    values(u - 3)

            pe.wait_ge(s_biased, NU)
            pe.wait_ge(pT_ready, NU)

            def gate_pair(i):
                for u in range(2):
                    pe.wait_ge(lo_ready, 2 * i + (GATE + u + 1))
                    pe.wait_ge(act_read, 2 * i + (PAIR_GATE + u - 1))
                    cols_step((GATE + u) % 2)

            with pe.Fori(0, 2) as i:
                gate_pair(i)
            pe.wait_ge(o_nsa_read, NSA_H)
            for c in range(2):
                for g in range(3):
                    if c == 0:
                        pe.wait_ge(odil_scaled, 4 * (g + 1))
                    if 3 * c + g >= 4:
                        pe.wait_ge(yd_summed, 3 * c + g - 3)
                    for r in range(4):
                        e = pe.transpose(ps[:, 4 + (3 * c + g) % 4, r * P:r * P + P],
                                         o_dil[:, g, r, 2 * c:2 * c + 2, :].rearrange("p a b -> p (a b)"), ident[:, :])
                    e.then_inc(ydT_done, 1)
            gate_pair(2)
            pe.wait_ge(yd_summed, 6)
            pe.wait_ge(y_nsa_ready, 1)
            for c in range(4):
                for t in range(NT):
                    e = pe.transpose(ps[:, 4 + c, t * P:t * P + P],
                                     y_nsa[:, t, 2 * c:2 * c + 2, :].rearrange("p a b -> p (a b)"), ident[:, :])
                e.then_inc(ynT_done, 1)
            gate_pair(3)

            pe.wait_ge(lo_ready, BDIL + 1)
            pe.wait_ge(ydlo_ready, 2)
            pe.wait_ge(ynlo_ready, 4)
            ydp, ynp = (yd_hi, yd_lo), (yn_hi, yn_lo)
            for m in range(KD):
                if m >= 4:
                    pe.wait_ge(b_gated, m - 3)
                for k in range(2):
                    for q, (a, b) in enumerate(MODES):
                        e = pe.matmul(ps[:, 4 + m % 4, :], part(a, BDIL % 2, k * D + m * P, P), ydp[b][:, k, :],
                                      start=(k == 0 and q == 0), stop=(k == 1 and q == 2))
                e.then_inc(b_done if m < KD - 1 else w_used, 1)
            pe.wait_ge(act_read, PAIR_FFN2)
            for m in range(KD):
                n = BNSA + m // 4
                if m % 4 == 0:
                    pe.wait_ge(lo_ready, n + 1)
                if m >= 4:
                    pe.wait_ge(a_gated, m - 3)
                for k in range(4):
                    for q, (a, b) in enumerate(MODES):
                        e = pe.matmul(ps[:, m % 4, :], part(a, n % 2, k * S + (m % 4) * P, P), ynp[b][:, k, :],
                                      start=(k == 0 and q == 0), stop=(k == 3 and q == 2))
                e.then_inc(a_done if m % 4 < 3 else w_used, 1)
            pe.wait_ge(b_gated, KD)
            for i in range(4):
                n = OUT + i
                pe.wait_ge(lo_ready, n + 1)
                for c in range(2):
                    if 2 * i + c < 4:
                        pe.wait_ge(a_gated, 4 + 2 * i + c + 1)
                    for k in range(KD):
                        if i == 0 and c == 0:
                            pe.wait_ge(mlo_ready, k + 1)
                        for q, (a, b) in enumerate(MODES):
                            e = pe.matmul(ps[:, 2 * i + c, :], part(a, n % 2, k * 256 + c * P, P), xn[b][:, k, :],
                                          start=(k == 0 and q == 0), stop=(k == KD - 1 and q == 2))
                    e.then_inc(w_used if c else y_done, 1)
            norm_y(1)
            split_norm(2)
            ffn(FFN2, PAIR_FFN2, UP, 2, 2)
            for m in range(KD):
                pe.wait_ge(x_new, 3 * KD + m + 1)
                if m >= 4:
                    pe.wait_ge(o_copied, m - 3)
                for t in range(NT):
                    e = pe.transpose(ps[:, m % 4, t * P:t * P + P], xres[:, m, t * P:t * P + P], ident[:, :])
                e.then_inc(oT_done, 1)


INPUTS = ["x", "ffn1_norm_pre", "ffn1_w_gu", "ffn1_w_down", "ffn1_norm_post", "mix_norm_pre", "w_in",
          "cmp_pos_k", "cmp_w1_k", "cmp_w2_k", "cmp_pos_v", "cmp_w1_v", "cmp_w2_v",
          "w_branch_nsa", "w_branch_dil", "w_out", "mix_norm_post",
          "ffn2_norm_pre", "ffn2_w_gu", "ffn2_w_down", "ffn2_norm_post", "rel_bias"]


def kernel(**inputs):
    import concourse.bacc as bacc
    from concourse.bass_utils import run_bass_kernel_spmd

    nc = bacc.Bacc("TRN2", target_bir_lowering=False, num_devices=1)
    arrays, args = {}, []
    for name in INPUTS:
        a = np.ascontiguousarray(inputs[name])
        if name != "rel_bias":
            a = a[0]
        arrays[f"in_{name}"] = a
    arrays["bucket_of_distance"] = bucket_table()
    for name, a in arrays.items():
        args.append(nc.dram_tensor(name, a.shape, mybir.dt.from_np(a.dtype), kind="ExternalInput").ap())
    args.append(nc.dram_tensor("out", (S, D), F32, kind="ExternalOutput").ap())
    layer_kernel(nc, *args)
    r = run_bass_kernel_spmd(nc, [arrays], core_ids=[0])
    return r.results[0]["out"].reshape(1, S, D)
```

```python
import math

import concourse.bass as bass
import numpy as np
from concourse import mybir

F32 = mybir.dt.float32
F32R = mybir.dt.float32r
ALU = mybir.AluOpType
ACT = mybir.ActivationFunctionType
AX_X = mybir.AxisListType.X

P = 128
S, D, F = 512, 1024, 2816
NT = S // P
KD = D // P
KF = F // P
HD = 64
NSA_H, NSA_G, HPG = 8, 2, 4
DIL_H, SLOTS = 12, 4
CB, CS = 32, 16
NCMP = (S - CB) // CS + 1
CPAD = 32
BUCKETS, MAX_DIST = 32, 2048
EPS = 1e-6
SCALE = HD ** -0.5
MASKED = 1e30
BIGGEST = 3e38

QN = 0
KCMP, VCMP, KSLC, VSLC, KWIN, VWIN = (NSA_H * HD + i * NSA_G * HD for i in range(6))
GN = NSA_H * HD + 6 * NSA_G * HD
QD = GN + 3 * NSA_H
KDL = QD + DIL_H * HD
VDL = KDL + DIL_H * HD
GA = VDL + DIL_H * HD
GB = GA + D

DIL_KEYS = 2 * P
NSA_W = 640
CMP_W = 1024
D0_W = 384
D12_W = 256
NSA_AT, CMP_AT = 0, NSA_W
D0_AT = CMP_AT + CMP_W
D1_AT = D0_AT + D0_W
D2_AT = D1_AT + D12_W
TAB_W = D2_AT + D12_W
assert TAB_W == 5 * S
BIAS_PARTS = ((0, 1), (2, 3, 4))
BIAS_BANKS = (4, 5, 6, 4, 5)
CMP_ZERO = CB - 1 + CS * (CPAD - 1)

W = 2048
UP, DOWN = KF, KF // 2
FFN1 = 0
PROJ = FFN1 + UP + DOWN
NPROJ, NV, NCOMP = 10, 4, 4
MIX = PROJ + NPROJ
GATE = MIX + NV + NCOMP
NGATE = 8
BDIL = GATE + NGATE
BNSA = BDIL + 1
OUT = BNSA + 2
FFN2 = OUT + 4
STEPS = FFN2 + UP + DOWN
PAIR_PROJ = UP
PAIR_GATE = PAIR_PROJ + NPROJ + NV
PAIR_FFN2 = PAIR_GATE + NGATE


def bucket(d):
    d = np.maximum(d, 0)
    exact = BUCKETS // 2
    large = exact + (np.log(np.maximum(d, exact).astype(np.float32) / np.float32(exact))
                     / np.float32(math.log(MAX_DIST / exact)) * (BUCKETS - exact)).astype(np.int32)
    return np.where(d < exact, d, np.minimum(large, BUCKETS - 1))


def bucket_table():
    i = np.arange(TAB_W)
    dist = np.zeros(TAB_W, np.int64)
    keep = np.ones(TAB_W, bool)
    a = i[NSA_AT:CMP_AT] - NSA_AT
    dist[NSA_AT:CMP_AT] = S - 1 - a
    dist[CMP_AT:D0_AT] = np.arange(CMP_W) - (CMP_ZERO)
    d0 = DIL_KEYS - 1 - np.arange(D0_W)
    dist[D0_AT:D1_AT] = d0
    keep[D0_AT:D1_AT] = d0 <= P
    d1 = P - 1 - np.arange(D12_W)
    dist[D1_AT:D2_AT] = 4 * d1
    dist[D2_AT:TAB_W] = 4 * d1
    keep[D2_AT:TAB_W] = d1 % 4 == 0
    keep &= dist >= 0
    out = np.zeros((BUCKETS + 1, TAB_W), np.float32)
    out[bucket(dist), i] = keep
    out[BUCKETS] = ~keep
    return out


def units():
    dil, nsa = [], []
    cmp_ = [[("c", None, t, [0, 1])] for t in range(NT)]
    for j in range(DIL_H):
        if j < SLOTS:
            dil.append([("d0", j, t, [t - 1, t] if t else [0]) for t in (0, 1)])
            dil.append([("d0", j, t, [t - 1, t]) for t in (2, 3)])
        else:
            dil.append([("d12", j, r, [r]) for r in range(4)])
    for c in range(NSA_H):
        h = c // 2 + HPG * (c % 2)
        full = lambda b, t: (b, h, t, list(range(t + 1)))
        nsa += [[full("s", 1), full("w", 1)], [full("s", 3)], [full("w", 3)],
                [full("s", 0), full("s", 2)], [full("w", 2), full("w", 0)]]
    return dil, cmp_, nsa


def place(row):
    kind, _, t, _ = row
    return (t // 2 * 2 if t % 2 else 4 + t // 2) + (kind == "w") * (1 if t % 2 else 2)


def layer_kernel(nc, x, g1_pre, w1_gu, w1_down, g1_post, gm_pre, w_in, pos_k, cw1_k, cw2_k,
                 pos_v, cw1_v, cw2_v, w_bn, w_bd, w_out, gm_post, g2_pre, w2_gu, w2_down, g2_post,
                 rel, onehot, out):
    DIL, CMP, NSA = units()
    NDU, NNU = len(DIL), len(NSA)
    N0 = NDU + NT

    K = 1024
    ARENA = 207 * K
    base = (nc.sbuf_base + 31) // 32 * 32
    nc.alloc_sbuf_tensor("arena", [P, ARENA], mybir.dt.uint8)

    def at(name, offset, shape, dt=F32):
        return nc.alloc_sbuf_tensor_at(name, [P] + shape, dt, offset=base + offset)

    xres = at("xres", 0, [KD, S])
    xn_hi = at("xn_hi", 16 * K, [KD, S], F32R)
    xn_lo = at("xn_lo", 32 * K, [KD, S], F32R)
    ring_raw = at("ring_raw", 48 * K, [2, W])
    ring_hi = at("ring_hi", 64 * K, [2, W], F32R)
    ring_lo = at("ring_lo", 80 * K, [2, W], F32R)
    R = 96 * K
    Y = R + 88 * K
    SM = Y + 16 * K
    hT_hi = at("hT_hi", R, [KF * S], F32R)
    hT_lo = at("hT_lo", R + 44 * K, [KF * S], F32R)
    ysb = at("ysb", Y, [KD, S])
    silu_g = at("silu_g", Y, [2, S])
    h_f32 = at("h_f32", Y + 4 * K, [2, S])
    sq_ffn = at("sq_ffn", 32 * K, [S])
    sq_mix = at("sq_mix", R, [S])
    x_tok = at("x_tok", R, [NT, D])
    gains_row = at("gains_row", R + 16 * K, [P])
    x_sq = at("x_sq", R + 28 * K, [KD, S])
    onehot_sb = at("onehot_sb", R + 56 * K, [TAB_W])
    bias_vec = at("bias_vec", R + 68 * K, [TAB_W])
    o_tok = at("o_tok", R, [NT, D])
    qn = at("qn", R, [4, S])
    kv4 = at("kv4", R + 8 * K, [4, S])
    qd = at("qd", R + 16 * K, [6, S])
    kd = at("kd", R + 28 * K, [6, S])
    v_all = at("v_all", R + 40 * K, [NT, D])
    bias_d0 = at("bias_d0", R + 56 * K, [SLOTS, DIL_KEYS])
    bias_d12 = at("bias_d12", R + 60 * K, [8, P])
    bias_cT = at("bias_cT", R + 64 * K, [NSA_G, S])
    o_dil = at("o_dil", R + 68 * K, [3, 4, SLOTS, HD])
    s_sb = at("s_sb", R + 80 * K, [2, S])
    p_sb = at("p_sb", R + 84 * K, [2, S])
    pT_sb = at("pT_sb", R + 88 * K, [2, S])
    y_nsa = at("y_nsa", R + 92 * K, [NT, NSA_H, HD])
    wg_raw = at("wg_raw", R + 68 * K, [KD, 24])
    wg_hi = at("wg_hi", R + 68 * K + 768, [KD, 24], F32R)
    wg_lo = at("wg_lo", R + 69 * K + 512, [KD, 24], F32R)
    w2k = at("w2k", R + 70 * K + 256, [2, 2, HD])
    w2v = at("w2v", R + 71 * K + 256, [2, HD])
    vb_hi = at("vb_hi", R + 72 * K, [16, 64], F32R)
    vb_lo = at("vb_lo", R + 76 * K, [16, 64], F32R)
    blk = at("blk", R + 80 * K, [16, 64])
    kb_hi = at("kb_hi", R + 84 * K, [16, 64], F32R)
    kb_lo = at("kb_lo", R + 88 * K, [16, 64], F32R)
    pair_k = at("pair_k", R + 92 * K, [NSA_G, S])
    pair_v = at("pair_v", R + 96 * K, [NSA_G, S])
    hid_row = at("hid_row", R + 80 * K, [2, 2, P])
    gates_row = at("gates_row", R + 82 * K, [S])
    vc_diag = at("vc_diag", R + 100 * K + 128, [NSA_G, HPG * HD])
    gates = at("gates", R + 102 * K + 128, [NT, NSA_H, 3])
    f_nsa = at("f_nsa", R + 102 * K + 512, [2, 8])
    f_c = at("f_c", R + 102 * K + 640, [NT, 8])
    nm_c = at("nm_c", R + 102 * K + 768, [2, 8])
    den_c = at("den_c", R + 102 * K + 832, [8])
    st_p = at("st_p", R + 103 * K, [4, 4, SLOTS])
    st_0 = at("st_0", R + 103 * K + 256, [NT, 2, SLOTS])
    st_n = at("st_n", R + 103 * K + 384, [NT, 4, SLOTS])
    e_n = at("e_n", R + 103 * K + 640, [3, NT, SLOTS])
    w_n = at("w_n", R + 103 * K + 832, [NT, SLOTS])
    bias_n = at("bias_n", R + 16 * K, [NSA_H, S])
    o_tmp = at("o_tmp", R + 32 * K, [2, S])
    sig = at("sig", R + 16 * K, [2 * KD, S])
    yn_hi = at("yn_hi", R + 48 * K, [4, S], F32R)
    yn_lo = at("yn_lo", R + 56 * K, [4, S], F32R)
    yd_hi = at("yd_hi", R, [2, S], F32R)
    yd_lo = at("yd_lo", R + 4 * K, [2, S], F32R)
    yd = at("yd", R + 8 * K, [2, S])
    mrg = at("mrg", R + 80 * K, [2, 2, S])
    o = [SM]

    def small(name, shape, dt=F32):
        t = at(name, o[0], shape, dt)
        o[0] += (4 * int(np.prod(shape)) + 31) // 32 * 32
        assert o[0] <= ARENA
        return t

    sq = small("sq", [S])
    acc = small("acc", [S])
    rb = at("rb", SM, [S])
    hid_k = at("hid_k", SM, [2, 64])
    hid_v = at("hid_v", SM + 2 * K, [2, NSA_G, HPG, CPAD])
    ident = small("ident", [P])
    ones = small("ones", [P])
    eps = small("eps", [1])
    gains = small("gains", [6, KD])
    sd = small("sd", [NT])
    rstd = small("rstd", [NT])
    tab = small("tab", [20])
    posT = small("posT", [2, 16])
    stat_m = small("stat_m", [16])
    stat_d = small("stat_d", [16])
    c_p = small("c_p", [4, 2, SLOTS])
    c_n = small("c_n", [NT, 2, SLOTS])
    valid = small("valid", [1])
    warm = small("warm", [1])
    x_ss = small("x_ss", [NT])
    kc_pad = small("kc_pad", [2 * NSA_G, CPAD])
    ps = nc.alloc_psum_tensor("ps", [P, 8, S], F32)

    vec_dram = nc.dram_tensor("bias_by_distance", [20, TAB_W], F32, kind="Internal").ap()
    rep_n = nc.dram_tensor("bias_rows_sparse", [P, NSA_H, NSA_W], F32, kind="Internal").ap()
    rep_d0 = nc.dram_tensor("bias_rows_dense", [P, SLOTS, D0_W], F32, kind="Internal").ap()
    rep_d1 = nc.dram_tensor("bias_rows_strided4", [P, SLOTS, D12_W], F32, kind="Internal").ap()
    rep_d2 = nc.dram_tensor("bias_rows_strided16", [P, SLOTS, D12_W], F32, kind="Internal").ap()
    rep_c = nc.dram_tensor("bias_rows_compressed", [CPAD, NSA_H, CMP_W], F32, kind="Internal").ap()
    st_dram = nc.dram_tensor("dilated_stats", [S, 16], F32, kind="Internal").ap()
    c_dram = nc.dram_tensor("dilated_weights", [S, 8], F32, kind="Internal").ap()

    sem = lambda name: nc.alloc_semaphore(name)
    raw_loaded = [sem("raw_loaded0"), sem("raw_loaded1")]
    hi_half, g1_loaded = sem("hi_half"), sem("g1_loaded")
    g_scaled, up_scaled, x_summed = sem("g_scaled"), sem("up_scaled"), sem("x_summed")
    hi_ready, lo_ready, w_used = sem("hi_ready"), sem("lo_ready"), sem("w_used")
    x_loaded = [sem(f"x_loaded{t}") for t in range(NT)]
    small_loaded, gains_loaded, x_sums = sem("small_loaded"), sem("gains_loaded"), sem("x_sums")
    consts, vec_mm, vec_copied, vec_stored = sem("consts"), sem("vec_mm"), sem("vec_copied"), sem("vec_stored")
    tab_ready, rows_stored = sem("tab_ready"), sem("rows_stored")
    xT_done = sem("xT_done")
    act_read, dve_read = sem("act_read"), sem("dve_read")
    h_ready, hhi_ready, hlo_ready = sem("h_ready"), sem("hhi_ready"), sem("hlo_ready")
    y_done, y_squared, y_summed = sem("y_done"), sem("y_squared"), sem("y_summed")
    ss_done, sd_ready, rstd_ready, rb_ready = sem("ss_done"), sem("sd_ready"), sem("rstd_ready"), sem("rb_ready")
    x_scaled, x_new, x_new_pool, x_squared = sem("x_scaled"), sem("x_new"), sem("x_new_pool"), sem("x_squared")
    u_ready, xhi_ready, xlo_ready, xlo_pool = sem("u_ready"), sem("xhi_ready"), sem("xlo_ready"), sem("xlo_pool")
    oT_done, o_copied, out_stored = sem("oT_done"), sem("o_copied"), sem("out_stored")
    biases_loaded, bias_n_loaded, cmp_loaded = sem("biases_loaded"), sem("bias_n_loaded"), sem("cmp_loaded")
    wg_loaded, wg_hi_ready, wg_lo_ready = sem("wg_loaded"), sem("wg_hi_ready"), sem("wg_lo_ready")
    gn_done, gates_ready = sem("gn_done"), sem("gates_ready")
    pairs_loaded, blk_ready, bhi_ready, blo_ready = [sem("pair_k_loaded"), sem("pair_v_loaded")], sem("blk_ready"), sem("bhi_ready"), sem("blo_ready")
    hid_ready, c2_done, kc_ready = sem("hid_ready"), sem("c2_done"), sem("kc_ready")
    hidT_done, hidT_ready, g_row_ready, gT_done = sem("hidT_done"), sem("hidT_ready"), sem("g_row_ready"), sem("gT_done")
    s_done, s_biased, p_ready, pT_done, pT_ready, o_read = (
        sem("s_done"), sem("s_biased"), sem("p_ready"), sem("pT_done"), sem("pT_ready"), sem("o_read"))
    yc_ready = sem("yc_ready")
    stats_stored, stats_loaded, e_in, e_ready, c_ready, c_stored, c_loaded = (
        sem("stats_stored"), sem("stats_loaded"), sem("e_in"), sem("e_ready"), sem("c_ready"), sem("c_stored"), sem("c_loaded"))
    w2_loaded = sem("w2_loaded")
    cT_gains = sem("gains_transposed")
    gains_ready = sem("gains_ready")
    o_nsa_read = sem("o_nsa_read")
    pv_done = sem("pv_done")
    odil_scaled, ydT_done, yd_summed, ydhi_ready, ydlo_ready = (
        sem("odil_scaled"), sem("ydT_done"), sem("yd_summed"), sem("ydhi_ready"), sem("ydlo_ready"))
    y_nsa_ready, ynT_done, ynhi_ready, ynlo_ready = sem("y_nsa_ready"), sem("ynT_done"), sem("ynhi_ready"), sem("ynlo_ready")
    b_done, b_gated, a_done, a_gated, merged, mhi_ready, mlo_ready = (
        sem("b_done"), sem("b_gated"), sem("a_done"), sem("a_gated"), sem("merged"), sem("mhi_ready"), sem("mlo_ready"))
    dve_chain = sem("dve_chain")

    f32 = lambda ap: ap.bitcast(F32)
    heads2 = lambda ap: ap.rearrange("p (a b) -> p a b", b=HD)
    by_k = lambda ap: ap.rearrange("(k p) c -> p k c", p=P)
    MODES = ((0, 0), (0, 1), (1, 0))
    ring = (ring_hi, ring_lo)
    xn = (xn_hi, xn_lo)
    hT = (hT_hi, hT_lo)

    def stat_dil(row):
        _, j, t, _ = row
        g, slot = j // SLOTS, j % SLOTS
        if g == 0:
            return st_0[:, t, 0, slot:slot + 1], st_0[:, t, 1, slot:slot + 1]
        return (st_p[:, t, 2 * (g - 1), slot:slot + 1], st_p[:, t, 2 * (g - 1) + 1, slot:slot + 1])

    def stat_nsa(turn):
        def of(row):
            i = 8 * (turn % 2) + place(row)
            return stat_m[:, i:i + 1], stat_d[:, i:i + 1]
        return of

    def stats_of(u):
        return stat_dil if u < NDU else stat_nsa((u - N0) // 5)

    def paired_views(dst, c):
        out = []
        for h in range(2):
            to = dst[:, c % 2, :].rearrange("p (k h g d) -> p k h g d", h=2, g=2, d=HD)[:, :, h]
            of = ring_raw[:, c % 2, :].rearrange("p (k g h d) -> p k g h d", h=2, g=2, d=HD)[:, :, :, h]
            out.append((to, of))
        return out

    def y_event(p, m):
        if p == 1:
            return (w_used, OUT + m // 2 + 1) if m % 2 else (y_done, KD - 1 + m // 2 + 1)
        first, end = (0, PROJ) if p == 0 else (KD - 1 + 4, STEPS)
        return (y_done, first + m + 1) if m < KD - 1 else (w_used, end)

    def xlo_event(r, m):
        if r == 1:
            return (xlo_pool, m // 2 + 1) if m % 2 else (xlo_ready, KD + m // 2 + 1)
        return xlo_ready, m + 1 if r == 0 else KD + KD // 2 + m + 1


    def x_event(r, m):
        if r and m % 2:
            return x_new_pool, KD // 2 * (r - 1) + m // 2 + 1
        return x_new, (m + 1 if r == 0 else KD + KD // 2 * (r - 1) + m // 2 + 1)

    def square_of(p, m):
        return acc if m == 0 else sq if m % 2 else sq_mix if p == 1 else sq_ffn

    def b_event(m):
        return (b_done, m + 1) if m < KD - 1 else (w_used, BDIL + 1)

    def a_event(m):
        return (a_done, m + 1 - m // 4) if m % 4 < 3 else (w_used, BNSA + m // 4 + 1)

    ALL = DIL + CMP + NSA
    NU = len(ALL)
    block = nc.Block()
    with block:

        @block.sync
        def _(sp):
            for t in range(NT):
                sp.dma_start(x_tok[:, t, :], x[t * P:t * P + P, :]).then_inc(x_loaded[t], 16)

            def load(i, c, first, second):
                if not (isinstance(i, int) and 2 * i + c < 2):
                    sp.wait_ge(lo_ready, 2 * i + (c - 1))
                for dst, src in (first, second):
                    sp.dma_start(dst, src).then_inc(raw_loaded[c % 2], 16)

            def view(c, inner):
                return ring_raw[:, c % 2, :].rearrange("p (k c) -> p k c", c=inner)

            def load_up(w_gu, base, i, u):
                v = view(base + u, 256)
                load(i, base + u,
                     (v[:, :, 0:P], by_k(w_gu[:, bass.ds(i * (2 * P) + u * P, P)])),
                     (v[:, :, P:256], by_k(w_gu[:, bass.ds(i * (2 * P) + (u * P + F), P)])))

            def load_down(w_down, base, i, u):
                v = view(base + u, D)
                load(i, base + u, (v[:, 0, :], w_down[bass.ds(i * (4 * P) + 2 * u * P, P), :]),
                     (v[:, 1, :], w_down[bass.ds(i * (4 * P) + (2 * u + 1) * P, P), :]))

            def load_cols(n, w, c0):
                v = view(n, 256)
                src = by_k(w[:, c0:c0 + 256])
                load(0, n, (v[:, 0:4, :], src[:, 0:4, :]), (v[:, 4:8, :], src[:, 4:8, :]))

            def load_two(n, w, c0, c1):
                v = view(n, 256)
                load(0, n, (v[:, :, 0:P], by_k(w[:, c0:c0 + P])), (v[:, :, P:256], by_k(w[:, c1:c1 + P])))

            def load_ffn(w_gu, w_down, base):
                for u in range(2):
                    load_up(w_gu, base, 0, u)
                with sp.Fori(1, UP // 2) as i:
                    for u in range(2):
                        load_up(w_gu, base, i, u)
                load_down(w_down, base + UP, 0, 0)
                with sp.Fori(0, (DOWN - 1) // 2) as i:
                    for u in range(1, 3):
                        load_down(w_down, base + UP, i, u)

            load_ffn(w1_gu, w1_down, FFN1)
            for i in range(2):
                load_two(PROJ + i, w_in, QN + P * i, QN + P * (i + 2))
            load_cols(PROJ + 2, w_in, KCMP)
            load_two(PROJ + 3, w_in, KSLC, KWIN)
            for i in range(3):
                load_cols(PROJ + 4 + i, w_in, QD + 256 * i)
            for i in range(3):
                load_cols(PROJ + 7 + i, w_in, KDL + 256 * i)
            for i, w1 in enumerate((cw1_k, cw1_k, cw1_v, cw1_v)):
                if i == 0:
                    load_two(MIX, w_in, VSLC, VWIN)
                else:
                    load_cols(MIX + 2 * i, w_in, VDL + 256 * (i - 1))
                load_cols(MIX + 2 * i + 1, w1[(i % 2) * D:(i % 2) * D + D, :], 0)
            for i in range(NGATE):
                load_cols(GATE + i, w_in, GA + 256 * i)
            v = view(BDIL, D)
            load(0, BDIL, (v[:, 0, :], w_bd[0:P, :]), (v[:, 1, :], w_bd[P:2 * P, :]))
            for i in range(2):
                v, src = view(BNSA + i, S), by_k(w_bn[:, i * S:i * S + S])
                load(0, BNSA + i, (v[:, 0:2, :], src[:, 0:2, :]), (v[:, 2:4, :], src[:, 2:4, :]))
            for i in range(4):
                load_cols(OUT + i, w_out, 256 * i)
            load_ffn(w2_gu, w2_down, FFN2)
            for i in range(4):
                sp.wait_ge(o_copied, 2 * i + 2)
                sp.dma_start(out[:, 256 * i:256 * i + 256].rearrange("(t p) d -> p t d", p=P),
                             o_tok[:, :, 256 * i:256 * i + 256]).then_inc(out_stored, 16)
            sp.wait_ge(out_stored, 64)

        @block.gpsimd
        def _(pool):
            pool.memset(ident[:, :], 0.0).then_inc(consts, 1)
            pool.memset(ones[:, :], 1.0).then_inc(consts, 1)
            pool.memset(eps[:, :], EPS).then_inc(consts, 1)
            pool.memset(valid[:, :], 1.0).then_inc(consts, 1)
            pool.wait_ge(consts, 4)
            pool.affine_select(out=ident[:, :], in_=ident[:, :], compare_op=ALU.not_equal, fill=1.0,
                               base=0, pattern=[[-1, P]], channel_multiplier=1).then_inc(consts, 1)
            pool.affine_select(out=valid[:, :], in_=valid[:, :], compare_op=ALU.is_ge, fill=0.0,
                               base=-(CB - 1), pattern=[[0, 1]], channel_multiplier=1).then_inc(consts, 1)
            pool.dma_start(tab[0:BUCKETS, :], rel).then_inc(small_loaded, 16)
            pool.dma_start(onehot_sb[0:BUCKETS + 1, :], onehot).then_inc(small_loaded, 16)
            def add_y(r):
                for m in range(1, KD, 2):
                    pool.wait_ge(x_scaled, KD * (r - 1) + m + 1)
                    pool.tensor_tensor(xres[:, m, :], xres[:, m, :], ysb[:, m, :], ALU.add).then_inc(x_new_pool, 1)

            def split_norm():
                for m in range(1, KD, 2):
                    pool.wait_ge(xhi_ready, KD + m + 1)
                    pool.tensor_tensor(xn_lo[:, m, :], ysb[:, m, :], f32(xn_hi[:, m, :]), ALU.subtract).then_inc(xlo_pool, 1)

            def sum_squares():
                for m in range(1, KD):
                    pool.wait_ge(x_squared, KD + m + 1)
                    if m > 1:
                        pool.wait_ge(x_summed, m - 1)
                    pool.tensor_tensor(acc[:, :], x_sq[:, 0, :] if m == 1 else acc[:, :], x_sq[:, m, :],
                                       ALU.add).then_inc(x_summed, 1)

            pool.wait_ge(vec_copied, 5)
            pool.dma_start(vec_dram, bias_vec[0:20, :]).then_inc(vec_stored, 16)
            pool.wait_ge(vec_stored, 16)

            for dst, head, at0 in ((rep_n, 0, NSA_AT), (rep_d0, NSA_H, D0_AT), (rep_d1, NSA_H + SLOTS, D1_AT),
                                   (rep_d2, NSA_H + 2 * SLOTS, D2_AT), (rep_c, 0, CMP_AT)):
                rows, heads, width = dst.shape
                src = bass.AP(tensor=vec_dram.tensor, offset=head * TAB_W + at0,
                              ap=[[0, rows], [TAB_W, heads], [1, width]])
                pool.dma_start(dst, src).then_inc(rows_stored, 16)
            pool.wait_ge(rows_stored, 80)

            def spread(rows, step, first, width):
                n, heads, w = rows.shape
                return bass.AP(tensor=rows.tensor, offset=first, ap=[[heads * w - step, n], [w, heads], [1, width]])

            add_y(1)
            split_norm()
            pool.wait_ge(w_used, PROJ)
            pool.dma_start(wg_raw[:, :, :], by_k(w_in[:, GN:GN + 24])).then_inc(wg_loaded, 16)
            for dst, w2 in ((w2k[:, :, 0, :], cw2_k), (w2k[:, :, 1, :], cw2_k), (w2v[:, :, :], cw2_v)):
                pool.dma_start(dst, w2.rearrange("(c p) d -> p c d", p=P)).then_inc(w2_loaded, 16)
            pool.dma_start(bias_d0[:, :, :], spread(rep_d0, 1, P - 1, DIL_KEYS)).then_inc(biases_loaded, 16)
            pool.dma_start(bias_d12[:, 0:4, :], spread(rep_d1, 1, P - 1, P)).then_inc(biases_loaded, 16)
            pool.dma_start(bias_d12[:, 4:8, :], spread(rep_d2, 1, P - 1, P)).then_inc(biases_loaded, 16)
            for g in range(NSA_G):
                for h in range(HPG):
                    src = bass.AP(tensor=rep_c.tensor, offset=(g * HPG + h) * CMP_W + CMP_ZERO - (CB - 1),
                                  ap=[[NSA_H * CMP_W - CS, CPAD], [1, S]])
                    pool.dma_start(bias_cT[h * CPAD:(h + 1) * CPAD, g, :], src).then_inc(cmp_loaded, 16)
            for i, (pair, chunk_ready) in enumerate(((pair_k, act_read), (pair_v, dve_read))):
                pool.wait_ge(chunk_ready, PAIR_PROJ + 3 if i == 0 else 3)
                if i == 0:
                    pool.wait_ge(xhi_ready, 2 * KD)
                for g in range(NSA_G):
                    src = kv4[g * HD:g * HD + HD, i, :]
                    pool.dma_start(pair[0:HD, g, :], src).then_inc(pairs_loaded[i], 16)
                    pool.dma_start(pair[HD:P, g, 0:S - 1], src[:, 1:S]).then_inc(pairs_loaded[i], 16)
            pool.wait_ge(s_done, NDU)
            pool.dma_start(bias_n[:, :, :], spread(rep_n, 1, P - 1, S)).then_inc(bias_n_loaded, 16)
            pool.wait_ge(p_ready, NDU)
            pool.dma_start(st_dram.rearrange("(l r) c -> l (r c)", r=4),
                           st_p[:, :, :, :].rearrange("p a b c -> p (a b c)")).then_inc(stats_stored, 16)
            pool.wait_ge(stats_stored, 16)
            pool.dma_start(st_n[:, :, :, :].rearrange("p t a b -> p t (a b)"),
                           st_dram.rearrange("(t p) c -> p t c", p=P)).then_inc(stats_loaded, 16)
            pool.wait_ge(c_ready, 1)
            pool.dma_start(c_dram.rearrange("(t p) c -> p t c", p=P),
                           c_n[:, :, :, :].rearrange("p t a b -> p t (a b)")).then_inc(c_stored, 16)
            pool.wait_ge(c_stored, 16)
            pool.dma_start(c_p[:, :, :, :].rearrange("p a b c -> p (a b c)"),
                           c_dram.rearrange("(l r) c -> l (r c)", r=4)).then_inc(c_loaded, 16)
            pool.wait_ge(c_loaded, 16)
            pool.wait_ge(o_read, NDU)
            for g in range(3):
                for r in range(4):
                    c = e_n[:, 0, r, :] if g == 0 else c_p[:, r, g - 1, :]
                    pool.tensor_tensor(o_dil[:, g, r, :, :], o_dil[:, g, r, :, :],
                                       c.unsqueeze(2).broadcast_to([P, SLOTS, HD]), ALU.mult).then_inc(odil_scaled, 1)
            add_y(2)
            sum_squares()
            add_y(3)

        @block.scalar
        def _(act):
            def hi(i, c, paired=False):
                act.wait_ge(raw_loaded[c % 2], 32 * i + 32 * (c // 2 + 1))
                if not (isinstance(i, int) and 2 * i + c < 2):
                    act.wait_ge(w_used, 2 * i + (c - 1))
                for dst, src in paired_views(ring_hi, c) if paired else [(ring_hi[:, c % 2, :], ring_raw[:, c % 2, :])]:
                    e = act.activation(dst, src, ACT.Copy)
                e.then_inc(hi_ready, 1)

            def hi_halves(n):
                act.wait_ge(raw_loaded[n % 2], 32 * (n // 2 + 1))
                act.wait_ge(w_used, n - 1)
                for half, done in ((slice(0, W // 2), hi_half), (slice(W // 2, W), hi_ready)):
                    act.activation(ring_hi[:, n % 2, half], ring_raw[:, n % 2, half], ACT.Copy).then_inc(done, 1)

            def root(i):
                act.wait_ge(ss_done, i)
                act.activation(sd[:, :], ps[:, 4 if i % 2 else 6, 0:S:P], ACT.Sqrt, scale=1.0 / D,
                               bias=eps[:, :]).then_inc(sd_ready, 1)

            def warm_root():
                act.wait_ge(consts, 6)
                act.activation(warm[:, :], eps[:, :], ACT.Sqrt, scale=1.0 / D, bias=eps[:, :])

            def split_norm():
                for m in range(KD):
                    act.wait_ge(*x_event(1, m))
                    act.activation(ysb[:, m, :], xres[:, m, :], ACT.Square).then_inc(x_squared, 1)
                root(2)
                for m in range(KD):
                    act.wait_ge(u_ready, m + 1)
                    act.activation(xn_hi[:, m, :], ysb[:, m, :], ACT.Copy).then_inc(xhi_ready, 1)

            def round_x(r, g, chunks=range(KD)):
                for m in chunks:
                    act.wait_ge(*x_event(r, m))
                    act.activation(xn_hi[:, m, :], xres[:, m, :], ACT.Copy, scale=gains[:, g, m:m + 1]).then_inc(xhi_ready, 1)
                    if r:
                        act.activation(x_sq[:, m, :], xres[:, m, :], ACT.Square).then_inc(x_squared, 1)

            def take_y(p, m):
                if m == 0:
                    warm_root()
                act.wait_ge(*y_event(p, m))
                if m >= 3:
                    act.wait_ge(y_summed, 7 * p + m - 2)
                act.activation(square_of(p, m)[:, :], ps[:, m, :], ACT.Square).then_inc(y_squared, 1)
                act.activation(ysb[:, m, :], ps[:, m, :], ACT.Copy)

            def ffn(base, pair0, h0, p):
                def up(i, u):
                    act.wait_ge(g_scaled, 2 * i + (h0 + u + 1))
                    act.activation(silu_g[:, u, :], silu_g[:, u, :], ACT.Silu).then_inc(act_read, 1)
                    if not (isinstance(i, int) and 2 * i + u == 0):
                        hi(i, base + u + 2)
                    act.wait_ge(h_ready, 2 * i + (h0 + u + 1))
                    act.activation(hT_hi[:, bass.ds(i * (2 * S) + u * S, S)], h_f32[:, u, :], ACT.Copy).then_inc(hhi_ready, 1)

                hi(0, base + 2)
                if p:
                    root(4)
                for u in range(2):
                    up(0, u)
                    for c in BIAS_PARTS[u] if p == 0 else ():
                        act.wait_ge(vec_mm, c + 1)
                        act.activation(bias_vec[0:20, c * S:c * S + S], ps[0:20, BIAS_BANKS[c], :], ACT.Copy,
                                       scale=-1.0).then_inc(vec_copied, 1)
                with act.Fori(1, UP // 2) as i:
                    for u in range(2):
                        up(i, u)
                n = base + UP + 2
                hi(0, n)
                with act.Fori(0, (DOWN - 3) // 2) as i:
                    for u in range(1, 3):
                        hi(i, n + u)
                if p == 0:
                    hi(0, PROJ, paired=True)
                for m in range(KD):
                    take_y(p, m)
                root(2 * p + 1)

            for i, g in enumerate((g1_pre, g1_post, gm_pre, gm_post, g2_pre, g2_post)):
                act.dma_start(gains_row[i * KD:i * KD + KD, :], g.rearrange("(m p) -> m p", p=P)).then_inc(gains_loaded if i else g1_loaded, 16)
            for i, pos in enumerate((pos_k, pos_v)):
                act.dma_start(gains_row[6 * KD + 16 * i:6 * KD + 16 * i + 16, :],
                               pos.rearrange("(l e) d -> l (e d)", e=2)).then_inc(gains_loaded, 16)
            warm_root()
            act.wait_ge(gains_ready, 1)
            round_x(0, 0, range(0, 4))
            hi(0, 0)
            round_x(0, 0, range(4, KD))
            for t in range(NT):
                act.wait_ge(x_loaded[t], 16)
                act.activation(ysb[:, 2 * t:2 * t + 2, :].rearrange("p a b -> p (a b)"), x_tok[:, t, :], ACT.Square,
                               accum_out=x_ss[:, t:t + 1]).then_inc(x_sums, 1)
            act.wait_ge(x_sums, NT)
            act.activation(sd[:, :], x_ss[:, :], ACT.Sqrt, scale=1.0 / D, bias=eps[:, :]).then_inc(sd_ready, 1)
            hi(0, 1)
            ffn(FFN1, 0, 0, 0)
            split_norm()
            hi(0, PROJ + 1, paired=True)

            def take(dst, src, scale, strided):
                if strided:
                    dst = dst.rearrange("p (r l) -> p l r", r=4)
                    src = src.rearrange("p (l r) -> p l r", r=4)
                act.activation(dst, src, ACT.Copy, scale=scale).then_inc(act_read, 1)

            for i in range(NPROJ):
                n = PROJ + i
                act.wait_ge(w_used, n + 1)
                src = ps[:, 2 * (n % 2), :]
                if i < 2:
                    take(qn[:, 2 * i, :], src, -SCALE, False)
                elif i < 4:
                    take(kv4[:, 2 * (i - 2), :], src, 1.0, False)
                elif i < 7:
                    take(qd[:, 2 * (i - 4), :], src, -SCALE, i > 4)
                else:
                    take(kd[:, 2 * (i - 7), :], src, 1.0, i > 7)
                hi(0, n + 2)
                if i == 1:
                    act.wait_ge(wg_loaded, 16)
                    act.activation(wg_hi[:, :, :], wg_raw[:, :, :], ACT.Copy).then_inc(wg_hi_ready, 1)
                if i in (6, 8):
                    act.wait_ge(blk_ready, 2 if i == 6 else 4)
                    act.activation((kb_hi if i == 6 else vb_hi)[:, :, :], blk[:, :, :], ACT.Copy).then_inc(bhi_ready, 1)
            for i in range(NV):
                n = MIX + 2 * i
                act.wait_ge(w_used, n + 1)
                hi_halves(n + 2)
                act.activation(v_all[:, 0:2, 256 * i:256 * i + 256],
                               ps[:, 2 * ((MIX + i) % 2), :].rearrange("p (t c) -> p t c", c=256), ACT.Copy).then_inc(act_read, 1)
                act.wait_ge(w_used, n + 2)
                hi_halves(n + 3)
                if i % 2:
                    act.activation(hid_row[0:64, i // 2, :, :].rearrange("p c j -> p (c j)"), ps[0:64, 4 + i // 2, 0:256],
                                   ACT.Silu).then_inc(hid_ready, 1)
            act.wait_ge(gn_done, 1)
            act.activation(gates_row[0:24, :], ps[0:24, 7, :], ACT.Sigmoid).then_inc(g_row_ready, 1)

            def exps(u):
                act.wait_ge(s_biased, u + 1)
                if u >= 2:
                    act.wait_ge(pT_done, u - 1)
                if NDU <= u - 2 < N0:
                    act.wait_ge(pT_ready, u - 1)
                if NDU <= u < N0:
                    act.activation(p_sb[:, u % 2, 0:256], s_sb[:, u % 2, 0:256], ACT.Exp, scale=-1.0).then_inc(p_ready, 1)
                    return
                c0 = 0
                for row in ALL[u]:
                    c1 = c0 + P * len(row[3])
                    least, den = stats_of(u)(row)
                    e = act.activation(p_sb[:, u % 2, c0:c1], s_sb[:, u % 2, c0:c1], ACT.Exp, bias=least,
                                       scale=-1.0, accum_out=den)
                    c0 = c1
                e.then_inc(p_ready, 1)

            def take_o(u):
                act.wait_ge(pv_done, u + 1)
                _, j, r0, _ = ALL[u][0]
                rows = len(ALL[u])
                act.activation(o_dil[:, j // SLOTS, r0:r0 + rows, j % SLOTS, :],
                               heads2(ps[:, 5 + u % 2, 0:HD * rows]), ACT.Copy).then_inc(o_read, 1)

            for u in range(NU):
                exps(u)
                if 3 <= u < NDU + 3:
                    take_o(u - 3)
                if u == N0 + 8:
                    act.wait_ge(e_in, 1)
                    act.activation(e_n[:, :, :, :], e_n[:, :, :, :], ACT.Exp, scale=-1.0).then_inc(e_ready, 1)

            act.wait_ge(y_nsa_ready, 1)
            for i in range(NGATE):
                n = GATE + i
                act.wait_ge(w_used, n + 1)
                for c in range(2):
                    e = act.activation(sig[:, 2 * i + c, :], ps[:, 2 * (n % 2) + c, :], ACT.Sigmoid)
                e.then_inc(act_read, 1)
                hi(0, n + 2)
                if i == 4:
                    for c in range(2):
                        act.wait_ge(yd_summed, 3 * (c + 1))
                        act.activation(yd_hi[:, c, :], yd[:, c, :], ACT.Copy).then_inc(ydhi_ready, 1)
                if i == 6:
                    for c in range(4):
                        act.wait_ge(ynT_done, c + 1)
                        act.activation(yn_hi[:, c, :], ps[:, 4 + c, :], ACT.Copy).then_inc(ynhi_ready, 1)
            hi(0, BDIL + 2)
            for i in range(2):
                for m in range(4 * i, 4 * i + 4):
                    act.wait_ge(merged, m + 1)
                    act.activation(xn_hi[:, m, :], mrg[:, m % 2, 1, :], ACT.Copy).then_inc(mhi_ready, 1)
                hi(0, BNSA + i + 2)
            for i in range(4):
                take_y(1, 2 * i)
                take_y(1, 2 * i + 1)
                if i < 3:
                    hi(0, OUT + i + 2)
            root(3)
            hi(0, FFN2 + 1)
            round_x(2, 4)
            ffn(FFN2, PAIR_FFN2, UP, 2)
            for m in range(KD):
                act.wait_ge(oT_done, m + 1)
                act.activation(o_tok[:, :, m * P:m * P + P], ps[:, m % 4, :].rearrange("p (t c) -> p t c", c=P),
                               ACT.Copy).then_inc(o_copied, 1)

        @block.vector
        def _(dve):
            chained = [0]

            def chain(instruction):
                chained[0] += 1
                instruction.then_inc(dve_chain, 1)
                dve.wait_ge(dve_chain, chained[0])

            def lo(i, c, paired=False):
                dve.wait_ge(hi_ready, 2 * i + (c + 1))
                whole = [(ring_lo[:, c % 2, :], ring_raw[:, c % 2, :])]
                rounded = [ring_hi[:, c % 2, :]]
                if paired:
                    whole, rounded = paired_views(ring_lo, c), [dst for dst, _ in paired_views(ring_hi, c)]
                for (dst, src), r in zip(whole, rounded):
                    e = dve.tensor_tensor(dst, src, f32(r), ALU.subtract)
                e.then_inc(lo_ready, 1)

            def lo_halves(n, count):
                for half, ready, at in ((slice(0, W // 2), hi_half, count), (slice(W // 2, W), hi_ready, n + 1)):
                    dve.wait_ge(ready, at)
                    e = dve.tensor_tensor(ring_lo[:, n % 2, half], ring_raw[:, n % 2, half], f32(ring_hi[:, n % 2, half]), ALU.subtract)
                e.then_inc(lo_ready, 1)

            def invert(i):
                dve.wait_ge(sd_ready, i + 1)
                dve.reciprocal(rstd[:, :], sd[:, :]).then_inc(rstd_ready, 1)
                dve.wait_ge(rb_ready, i + 1)

            def split_norm(g):
                invert(2)
                for m in range(KD + 1):
                    if m < KD:
                        dve.scalar_tensor_tensor(out=ysb[:, m, :], in0=xres[:, m, :], scalar=gains[:, g, m:m + 1],
                                                 in1=ps[:, 7, :], op0=ALU.mult, op1=ALU.mult).then_inc(u_ready, 1)
                    if m % 2:
                        dve.wait_ge(xhi_ready, KD + m)
                        dve.tensor_tensor(xn_lo[:, m - 1, :], ysb[:, m - 1, :], f32(xn_hi[:, m - 1, :]),
                                          ALU.subtract).then_inc(xlo_ready, 1)

            def lo_x(r, g, m):
                dve.wait_ge(xhi_ready, KD * r + m + 1)
                dve.scalar_tensor_tensor(out=xn_lo[:, m, :], in0=xres[:, m, :], scalar=gains[:, g, m:m + 1],
                                         in1=f32(xn_hi[:, m, :]), op0=ALU.mult, op1=ALU.subtract).then_inc(xlo_ready, 1)

            def sum_y(p, m):
                dve.wait_ge(y_squared, KD * p + m + 1)
                if m >= 2:
                    dve.wait_ge(y_summed, 7 * p + m - 1)
                dve.tensor_tensor(acc[:, :], acc[:, :], square_of(p, m)[:, :], ALU.add).then_inc(y_summed, 1)

            def add_y(p, g, then=None):
                invert(2 * p + 1)
                for m in range(KD + 1):
                    if m < KD:
                        dve.scalar_tensor_tensor(out=ysb[:, m, :], in0=ysb[:, m, :], scalar=gains[:, g, m:m + 1],
                                                 in1=ps[:, 5, :], op0=ALU.mult, op1=ALU.mult).then_inc(x_scaled, 1)
                    if m % 2:
                        dve.wait_ge(x_scaled, KD * p + m)
                        dve.tensor_tensor(xres[:, m - 1, :], xres[:, m - 1, :], ysb[:, m - 1, :],
                                          ALU.add).then_inc(x_new, 1)
                    if then and m >= 2:
                        then(m - 2)
                if then:
                    then(KD - 1)

            def ffn(base, pair0, h0, p, g):
                def up(i, u):
                    first = isinstance(i, int) and 2 * i + u < 2
                    slot = (base + u) % 2
                    dve.wait_ge(w_used, 2 * i + (base + u + 1))
                    if not first:
                        dve.wait_ge(h_ready, 2 * i + (h0 + u - 1))
                        dve.wait_ge(hhi_ready, 2 * i + (h0 + u - 1))
                        dve.wait_ge(hlo_ready, 2 * i + (h0 + u - 1))
                    dve.tensor_tensor(silu_g[:, u, :], ps[:, 2 * slot, :], rb[:, :], ALU.mult).then_inc(g_scaled, 1)
                    dve.tensor_tensor(h_f32[:, u, :], ps[:, 2 * slot + 1, :], rb[:, :], ALU.mult).then_inc(up_scaled, 1)
                    dve.wait_ge(act_read, 2 * i + (pair0 + u + 1))
                    dve.wait_ge(up_scaled, 2 * i + (h0 + u + 1))
                    dve.tensor_tensor(h_f32[:, u, :], silu_g[:, u, :], h_f32[:, u, :], ALU.mult).then_inc(h_ready, 1)
                    if not (first and u == 0):
                        lo(i, base + u + 2)
                    dve.wait_ge(hhi_ready, 2 * i + (h0 + u + 1))
                    at_j = bass.ds(i * (2 * S) + u * S, S)
                    dve.tensor_tensor(hT_lo[:, at_j], h_f32[:, u, :], f32(hT_hi[:, at_j]),
                                      ALU.subtract).then_inc(hlo_ready, 1)

                lo(0, base + 1)
                lo(0, base + 2)
                if p:
                    invert(4)
                else:
                    dve.wait_ge(rb_ready, 1)
                chain(dve.tensor_copy(rb[:, :], ps[:, 7, :]))
                for u in range(2):
                    up(0, u)
                if p == 0:
                    dve.wait_ge(vec_stored, 16)
                with dve.Fori(1, UP // 2) as i:
                    for u in range(2):
                        up(i, u)
                n = base + UP + 2
                lo(0, n)
                with dve.Fori(0, (DOWN - 3) // 2) as i:
                    for u in range(1, 3):
                        lo(i, n + u)
                if p == 0:
                    lo(0, PROJ, paired=True)
                for m in range(1, KD):
                    sum_y(p, m)
                add_y(p, g)

            dve.memset(tab[BUCKETS:BUCKETS + 1, :], -MASKED).then_inc(tab_ready, 1)
            dve.wait_ge(cT_gains, 1)
            dve.tensor_copy(gains[:, 0, :], ps[:, 5, 0:KD]).then_inc(gains_ready, 1)
            dve.wait_ge(gains_ready, 1)
            for m in range(KD):
                dve.wait_ge(xT_done, m + 1)
                dve.tensor_copy(xres[:, m, :], ps[:, m % 4, :]).then_inc(x_new, 1)
                if m >= 3:
                    lo_x(0, 0, m - 3)
            lo(0, 0)
            for m in range(KD - 3, KD):
                lo_x(0, 0, m)
            dve.wait_ge(sd_ready, 1)
            dve.reciprocal(rstd[:, :], sd[:, :]).then_inc(rstd_ready, 1)
            dve.wait_ge(cT_gains, 2)
            chain(dve.tensor_copy(gains[:, 1:6, :].rearrange("p a b -> p (a b)"), ps[:, 6, KD:6 * KD]))
            dve.tensor_copy(posT[:, :, :].rearrange("p a b -> p (a b)"), ps[:, 6, 6 * KD:80])
            for g in (1, 5):
                e = dve.tensor_scalar(gains[:, g, :], gains[:, g, :], 0.5, None, ALU.mult)
            chain(e)
            ffn(FFN1, 0, 0, 0, 1)
            split_norm(2)
            lo(0, PROJ + 1, paired=True)

            dve.wait_ge(*xlo_event(1, KD - 2))
            dve.wait_ge(*xlo_event(1, KD - 1))
            chain(dve.memset(vc_diag[:, :, :], 0.0))
            chain(dve.memset(kc_pad[:, :, :], 0.0))

            def take(dst, src, scale, strided):
                if strided:
                    dst = dst.rearrange("p (r l) -> p l r", r=4)
                    src = src.rearrange("p (l r) -> p l r", r=4)
                dve.tensor_scalar(dst, src, scale, None, ALU.mult).then_inc(dve_read, 1)

            def blocks(i, pair):
                dve.wait_ge(pairs_loaded[i], 64)
                if i == 0:
                    chain(dve.memset(blk[:, :, :], 0.0))
                else:
                    dve.wait_ge(blo_ready, i)
                    dve.wait_ge(bhi_ready, i)
                for g in range(NSA_G):
                    src = pair[:, g, :].rearrange("p (n l) -> p l n", l=CS)
                    for half in range(2):
                        dst = blk[:, 8 * half:8 * half + 8, g * CPAD:g * CPAD + NCMP]
                        e = dve.tensor_tensor(dst, src[:, 0:CS:2, half:half + NCMP],
                                              posT[:, i, 8 * half:8 * half + 8].unsqueeze(2).broadcast_to([P, 8, NCMP]),
                                              ALU.add)
                    e.then_inc(blk_ready, 1)

            for i in range(NPROJ):
                n = PROJ + i
                dve.wait_ge(w_used, n + 1)
                src = ps[:, 2 * (n % 2) + 1, :]
                if i < 2:
                    take(qn[:, 2 * i + 1, :], src, -SCALE, False)
                elif i < 4:
                    take(kv4[:, 2 * (i - 2) + 1, :], src, 1.0, False)
                elif i < 7:
                    take(qd[:, 2 * (i - 4) + 1, :], src, -SCALE, i > 4)
                else:
                    take(kd[:, 2 * (i - 7) + 1, :], src, 1.0, i > 7)
                lo(0, n + 2)
                if i == 1:
                    dve.wait_ge(wg_hi_ready, 1)
                    dve.tensor_tensor(wg_lo[:, :, :], wg_raw[:, :, :], f32(wg_hi[:, :, :]), ALU.subtract).then_inc(wg_lo_ready, 1)
                if i in (5, 7):
                    blocks((i - 5) // 2, pair_k if i == 5 else pair_v)
                if i in (6, 8):
                    b_hi, b_lo = (kb_hi, kb_lo) if i == 6 else (vb_hi, vb_lo)
                    dve.wait_ge(bhi_ready, (i - 4) // 2)
                    dve.tensor_tensor(b_lo[:, :, :], blk[:, :, :], f32(b_hi[:, :, :]), ALU.subtract).then_inc(blo_ready, 1)
            for i in range(NV):
                n = MIX + 2 * i
                dve.wait_ge(w_used, n + 1)
                dve.tensor_copy(v_all[:, 2:4, 256 * i:256 * i + 256],
                                ps[:, 2 * ((MIX + i) % 2) + 1, :].rearrange("p (t c) -> p t c", c=256)).then_inc(dve_read, 1)
                lo_halves(n + 2, 2 * i + 1)
                lo_halves(n + 3, 2 * i + 2)
            dve.wait_ge(hidT_done, 1)
            dve.tensor_copy(hid_k[:, :, :].rearrange("p c n -> p (c n)"), ps[:, 6, 0:P])
            for g in range(NSA_G):
                e = dve.tensor_copy(hid_v[:, :, g, :, :],
                                    ps[:, 6, P:2 * P].rearrange("p (c g n) -> p g c n", g=NSA_G, n=CPAD)[:, g].unsqueeze(2)
                                    .broadcast_to([P, 2, HPG, CPAD]))
            e.then_inc(hidT_ready, 1)
            dve.wait_ge(gT_done, 1)
            dve.tensor_copy(gates[:, :, :, :].rearrange("p t h b -> p (t h b)"), ps[:, 4, 0:NT * 24]).then_inc(gates_ready, 1)
            dve.wait_ge(c2_done, 1)
            for g in range(NSA_G):
                rows = slice(g * HD, g * HD + HD)
                dve.tensor_copy(kc_pad[rows, g, :], ps[rows, 5, g * CPAD:g * CPAD + CPAD])
            for h in range(HPG):
                rows = slice(h * CPAD, (h + 1) * CPAD)
                e = dve.tensor_copy(vc_diag[rows, :, h * HD:h * HD + HD], heads2(ps[rows, 5, P:2 * P]))
            e.then_inc(kc_ready, 1)

            def bias_of(row):
                kind, h, t, keys = row
                if kind == "d0":
                    return bias_d0[:, h, DIL_KEYS - P * len(keys):DIL_KEYS]
                if kind == "d12":
                    return bias_d12[:, h - SLOTS, :]
                return bias_n[:, h, S - P * len(keys):S]

            def add_bias(u):
                dve.wait_ge(s_done, u + 1)
                if u >= 2:
                    dve.wait_ge(p_ready, u - 1)
                if NDU <= u < N0:
                    t = u - NDU
                    sc = ps[:, u % 3, 0:256]
                    chain(dve.tensor_reduce(nm_c[:, t % 2, :], sc.rearrange("p (h n) -> p h n", n=CPAD), AX_X, ALU.min))
                    dve.tensor_tensor(s_sb[:, u % 2, 0:256].rearrange("p (g h n) -> p h g n", g=NSA_G, n=CPAD),
                                      sc.rearrange("p (h g n) -> p h g n", g=NSA_G, n=CPAD),
                                      nm_c[:, t % 2, :].rearrange("p (h g) -> p h g", g=NSA_G).unsqueeze(3)
                                      .broadcast_to([P, HPG, NSA_G, CPAD]), ALU.subtract).then_inc(s_biased, 1)
                    return
                c0 = 0
                for row in ALL[u]:
                    c1 = c0 + P * len(row[3])
                    least, _ = stats_of(u)(row)
                    e = dve.tensor_tensor_reduce(out=s_sb[:, u % 2, c0:c1], in0=ps[:, u % 3, c0:c1], in1=bias_of(row),
                                                 scale=1.0, scalar=BIGGEST, op0=ALU.add, op1=ALU.min, accum_out=least)
                    c0 = c1
                e.then_inc(s_biased, 1)

            def take_pT(u):
                dve.wait_ge(pT_done, u + 1)
                if u >= 2:
                    dve.wait_ge(pv_done, u - 1)
                w = P * sum(len(row[3]) for row in ALL[u])
                dve.tensor_copy(pT_sb[:, u % 2, 0:w], ps[:, 3 + u % 2, 0:w]).then_inc(pT_ready, 1)

            dve.wait_ge(biases_loaded, 48)
            by_head = lambda ap: ap.rearrange("p (h n) -> p h n", n=CPAD)
            spread_head = lambda ap, n: ap.unsqueeze(2).broadcast_to([P, NSA_H, n])

            def cmp_sums(t):
                u = NDU + t
                dve.wait_ge(p_ready, u + 1)
                chain(dve.tensor_reduce(den_c[:, :], by_head(p_sb[:, u % 2, 0:256]), AX_X, ALU.add))

            def cmp_factors(t):
                chain(dve.reciprocal(den_c[:, :], den_c[:, :]))
                chain(dve.tensor_tensor(f_c[:, t, :], den_c[:, :], gates[:, t, :, 0], ALU.mult))
                if t == 0:
                    chain(dve.tensor_scalar(f_c[:, t, :], f_c[:, t, :], valid[:, :], None, ALU.mult))

            def cmp_out(t):
                dve.wait_ge(pv_done, NDU + t + 1)
                dve.tensor_tensor(y_nsa[:, t, :, :], heads2(ps[:, 7 - t % 2, :]), spread_head(f_c[:, t, :], HD),
                                  ALU.mult).then_inc(yc_ready, 1)

            def take_head(turn):
                h = turn // 2 + HPG * (turn % 2)
                o8 = 8 * (turn % 2)
                u1 = N0 + 5 * (turn + 1)
                dve.wait_ge(p_ready, u1)
                den = stat_d[:, o8:o8 + 8]
                f = f_nsa[:, turn % 2, :]
                chain(dve.reciprocal(f, den))
                odd, even = f[:, 0:4].rearrange("p (t b) -> p t b", b=2), f[:, 4:8].rearrange("p (b t) -> p t b", b=2)
                dve.tensor_tensor(odd, odd, gates[:, 1:NT:2, h, 1:3], ALU.mult)
                chain(dve.tensor_tensor(even, even, gates[:, 0:NT:2, h, 1:3], ALU.mult))
                dve.wait_ge(pv_done, u1)
                o = o_tmp[:, turn % 2, :].rearrange("p (b t d) -> p t b d", b=2, d=HD)
                o_ps = ps[:, 5 + turn % 2, :]
                spread4 = lambda ap: ap.unsqueeze(3).broadcast_to([P, 2, 2, HD])
                dve.tensor_tensor(o[:, 1:NT:2], o_ps[:, 0:256].rearrange("p (t b d) -> p t b d", b=2, d=HD), spread4(odd), ALU.mult)
                dve.tensor_tensor(o[:, 0:NT:2], o_ps[:, 256:512].rearrange("p (b t d) -> p t b d", b=2, d=HD), spread4(even),
                                  ALU.mult).then_inc(o_nsa_read, 1)
                dve.wait_ge(o_nsa_read, turn + 1)
                for b in range(2):
                    chain(dve.tensor_tensor(y_nsa[:, :, h, :], y_nsa[:, :, h, :],
                                            heads2(o_tmp[:, turn % 2, b * 256:b * 256 + 256]), ALU.add))

            def dil_weights():
                dve.wait_ge(stats_loaded, 16)
                st = lambda g, k: st_0[:, :, k, :] if g == 0 else st_n[:, :, 2 * (g - 1) + k, :]
                chain(dve.tensor_tensor(w_n[:, :, :], st(0, 0), st(1, 0), ALU.min))
                chain(dve.tensor_tensor(w_n[:, :, :], w_n[:, :, :], st(2, 0), ALU.min))
                for g in range(3):
                    e = dve.tensor_tensor(e_n[:, g, :, :], st(g, 0), w_n[:, :, :], ALU.subtract)
                e.then_inc(e_in, 1)

            def dil_norm():
                st = lambda g, k: st_0[:, :, k, :] if g == 0 else st_n[:, :, 2 * (g - 1) + k, :]
                dve.wait_ge(e_ready, 1)
                chain(dve.tensor_tensor(w_n[:, :, :], e_n[:, 0, :, :], st(0, 1), ALU.mult))
                for g in (1, 2):
                    chain(dve.tensor_tensor(st(g, 1), e_n[:, g, :, :], st(g, 1), ALU.mult))
                    chain(dve.tensor_tensor(w_n[:, :, :], w_n[:, :, :], st(g, 1), ALU.add))
                chain(dve.reciprocal(w_n[:, :, :], w_n[:, :, :]))
                for g in (1, 2):
                    dve.tensor_tensor(c_n[:, :, g - 1, :], e_n[:, g, :, :], w_n[:, :, :], ALU.mult)
                dve.tensor_tensor(e_n[:, 0, :, :], e_n[:, 0, :, :], w_n[:, :, :], ALU.mult).then_inc(c_ready, 1)

            for u in range(NU + 5):
                if u == N0:
                    dve.wait_ge(bias_n_loaded, 16)
                if NDU <= u - 4 < N0:
                    cmp_out(u - 4 - NDU)
                if u < NU:
                    add_bias(u)
                if NDU <= u - 2 < N0:
                    cmp_sums(u - 2 - NDU)
                if 2 <= u < NU + 2:
                    take_pT(u - 2)
                if NDU <= u - 2 < N0:
                    cmp_factors(u - 2 - NDU)
                i = u - N0
                if i == 6:
                    dil_weights()
                if i == 11:
                    dil_norm()
                if i >= 9 and (i - 9) % 5 == 0:
                    if i == 9:
                        dve.wait_ge(yc_ready, NT)
                    take_head((i - 9) // 5)
            e = dve.memset(w_n[:, :, :], 0.0)
            e.then_inc(y_nsa_ready, 1)

            for i in range(NGATE):
                if i != 3:
                    lo(0, GATE + i + 2)
                if i == 3:
                    for c in range(2):
                        for g in range(3):
                            dve.wait_ge(ydT_done, 3 * c + g + 1)
                            src = ps[:, 4 + (3 * c + g) % 4, :]
                            if g == 0:
                                dve.tensor_copy(yd[:, c, :], src).then_inc(yd_summed, 1)
                            else:
                                dve.wait_ge(yd_summed, 3 * c + g)
                                dst = yd[:, c, :].rearrange("p (l r) -> p r l", r=4)
                                dve.tensor_tensor(dst, src.rearrange("p (r l) -> p r l", r=4), dst,
                                                  ALU.add).then_inc(yd_summed, 1)
                    lo(0, GATE + i + 2)
                if i == 4:
                    for c in range(2):
                        dve.wait_ge(ydhi_ready, c + 1)
                        dve.tensor_tensor(yd_lo[:, c, :], yd[:, c, :], f32(yd_hi[:, c, :]), ALU.subtract).then_inc(ydlo_ready, 1)
                if i == 6:
                    for c in range(4):
                        dve.wait_ge(ynhi_ready, c + 1)
                        dve.tensor_tensor(yn_lo[:, c, :], ps[:, 4 + c, :], f32(yn_hi[:, c, :]), ALU.subtract).then_inc(ynlo_ready, 1)
            dve.wait_ge(act_read, PAIR_FFN2)
            for m in range(KD):
                dve.wait_ge(*b_event(m))
                dve.tensor_tensor(sig[:, KD + m, :], sig[:, KD + m, :], ps[:, 4 + m % 4, :], ALU.mult).then_inc(b_gated, 1)
            lo(0, BDIL + 2)
            for m in range(KD):
                dve.wait_ge(*a_event(m))
                if m == 0:
                    dve.wait_ge(b_gated, KD)
                dve.tensor_tensor(mrg[:, m % 2, 0, :], sig[:, m, :], ps[:, m % 4, :], ALU.mult).then_inc(a_gated, 1)
                dve.wait_ge(a_gated, m + 1)
                dve.tensor_tensor(mrg[:, m % 2, 1, :], mrg[:, m % 2, 0, :], sig[:, KD + m, :], ALU.add).then_inc(merged, 1)
                for done in ([m - 1] if m else []) + ([m] if m == KD - 1 else []):
                    dve.wait_ge(mhi_ready, done + 1)
                    dve.tensor_tensor(xn_lo[:, done, :], mrg[:, done % 2, 1, :], f32(xn_hi[:, done, :]),
                                      ALU.subtract).then_inc(mlo_ready, 1)
                if m % 4 == 3:
                    lo(0, BNSA + m // 4 + 2)
            for i in range(4):
                for m in (2 * i, 2 * i + 1):
                    if m:
                        sum_y(1, m)
                if i < 3:
                    lo(0, OUT + i + 2)
            add_y(1, 3, lambda m: lo_x(2, 4, m))
            ffn(FFN2, PAIR_FFN2, UP, 2, 5)

        @block.tensor
        def _(pe):
            def part(kind, slot, k0, width):
                return ring[kind][:, slot, k0:k0 + width]

            def cols_step(slot, norm=None, between={}):
                for k in range(KD):
                    if k in between:
                        between[k]()
                    if norm is not None:
                        pe.wait_ge(*xlo_event(norm, k))
                    for c in range(2):
                        for i, (a, b) in enumerate(MODES):
                            e = pe.matmul(ps[:, 2 * slot + c, :], part(a, slot, k * 256 + c * P, P), xn[b][:, k, :],
                                          start=(k == 0 and i == 0), stop=(k == KD - 1 and i == 2))
                e.then_inc(w_used, 1)

            def keep_warm(n, bank):
                for _ in range(n):
                    pe.matmul(ps[:, bank, 0:P], ident[:, :], ident[:, :], start=True, stop=True)

            def column_sums(bank, src, first, last):
                for t in range(NT):
                    e = pe.matmul(ps[:, bank, t * P:t * P + P], src[:, t * P:t * P + P], ones[:, :],
                                  start=(first and t == 0), stop=last, skip_group_check=True)
                return e

            def spread_rstd(i, bank, warm):
                keep_warm(warm, 6 if i == 0 else 3)
                pe.wait_ge(rstd_ready, i + 1)
                for t in range(NT):
                    e = pe.matmul(ps[:, bank, t * P:t * P + P], rstd[:, t:t + 1].broadcast_to([P, P]), ident[:, :],
                                  start=True, stop=True)
                e.then_inc(rb_ready, 1)

            def split_norm():
                for m in range(KD):
                    pe.wait_ge(x_squared, m + 1)
                    e = column_sums(6, ysb[:, m, :], m == 0, m == KD - 1)
                e.then_inc(ss_done, 1)
                spread_rstd(2, 7, 3)
                keep_warm(6, 3)

            def transpose_gains():
                pe.wait_ge(gains_loaded, 112)
                pe.transpose(ps[:, 6, 0:80], gains_row[0:80, :], ident[0:80, 0:80]).then_inc(cT_gains, 1)

            def sum_x():
                pe.wait_ge(x_summed, KD - 1)
                column_sums(6, acc[:, :], True, True).then_inc(ss_done, 1)

            def norm_y(p):
                pe.wait_ge(y_summed, 7 * p + 7)
                column_sums(4, acc[:, :], True, True).then_inc(ss_done, 1)
                spread_rstd(2 * p + 1, 5, 3)
                keep_warm(8, 3)

            def ffn(base, pair0, h0, p, norm):
                def up(i, u):
                    pe.wait_ge(lo_ready, 2 * i + (base + u + 1))
                    if not (isinstance(i, int) and 2 * i + u < 2):
                        pe.wait_ge(up_scaled, 2 * i + (h0 + u - 1))
                    first = isinstance(i, int) and i == 0
                    cols_step((base + u) % 2, norm if first and u == 0 else None,
                              {5: sum_x, 7: lambda: spread_rstd(4, 7, 0)} if first and u == 1 and p else
                              {4: transpose_gains, 7: lambda: spread_rstd(0, 7, 0)} if first and u == 0 and not p else {})

                def down(i, u, order=range(KD), start=False, stop=False):
                    n0 = base + UP + u
                    pe.wait_ge(lo_ready, 2 * i + (n0 + 1))
                    for m in order:
                        if start and m == 0:
                            pe.wait_ge(up_scaled, h0 + UP)
                        for kk in range(2):
                            at_k = bass.ds(i * (4 * S) + (2 * u + kk) * S, S)
                            for q, (a, b) in enumerate(MODES):
                                e = pe.matmul(ps[:, m, :], part(a, n0 % 2, kk * D + m * P, P), hT[b][:, at_k],
                                              start=(start and kk == 0 and q == 0), stop=(stop and kk == 1 and q == 2),
                                              skip_group_check=True)
                        if stop and m < KD - 1:
                            e.then_inc(y_done, 1)
                    e.then_inc(w_used, 1)

                for u in range(2):
                    up(0, u)
                    if p == 0:
                        pe.wait_ge(small_loaded, 32)
                        pe.wait_ge(tab_ready, 1)
                        for c in BIAS_PARTS[u]:
                            if c >= 3:
                                pe.wait_ge(vec_copied, c - 2)
                            pe.matmul(ps[0:20, BIAS_BANKS[c], :], tab[0:BUCKETS + 1, :], onehot_sb[0:BUCKETS + 1, c * S:c * S + S],
                                      start=True, stop=True).then_inc(vec_mm, 1)
                with pe.Fori(1, UP // 2) as i:
                    for u in range(2):
                        up(i, u)
                pe.wait_ge(hlo_ready, h0 + UP - 2)
                if p == 0:
                    pe.wait_ge(vec_copied, 5)
                down(0, 0, order=(4, 5, 6, 7, 0, 1, 2, 3), start=True)
                with pe.Fori(0, (DOWN - 3) // 2) as i:
                    for u in range(1, 3):
                        down(i, u)
                down(0, DOWN - 2)
                pe.wait_ge(hlo_ready, h0 + UP)
                down(0, DOWN - 1, stop=True)
                norm_y(p)

            pe.wait_ge(consts, 6)
            pe.wait_ge(consts, 6)
            keep_warm(14, 6)
            pe.wait_ge(g1_loaded, 16)
            pe.transpose(ps[:, 5, 0:KD], gains_row[0:KD, :], ident[0:KD, 0:KD]).then_inc(cT_gains, 1)
            for m in range(KD):
                if m >= 4:
                    pe.wait_ge(x_new, m - 3)
                for t in range(NT):
                    if m == 0:
                        pe.wait_ge(x_loaded[t], 16)
                    e = pe.transpose(ps[:, m % 4, t * P:t * P + P], x_tok[:, t, m * P:m * P + P], ident[:, :])
                e.then_inc(xT_done, 1)
            ffn(FFN1, 0, 0, 0, 0)
            split_norm()

            def proj(i, u):
                pe.wait_ge(lo_ready, 2 * i + (PROJ + u + 1))
                if not (isinstance(i, int) and i == 0):
                    pe.wait_ge(act_read, 2 * i + (PAIR_PROJ + u - 1))
                    pe.wait_ge(dve_read, 2 * i + (u - 1))
                cols_step((PROJ + u) % 2, 1 if isinstance(i, int) and i == 0 and u == 0 else None)

            for u in range(2):
                proj(0, u)
            with pe.Fori(1, NPROJ // 2) as i:
                for u in range(2):
                    proj(i, u)
            def compress(i):
                n = MIX + 2 * i + 1
                pe.wait_ge(lo_ready, n + 1)
                kv = i // 2
                if i % 2 == 0:
                    pe.wait_ge(blo_ready, kv + 1)
                blocks = ((kb_hi, kb_lo), (vb_hi, vb_lo))[kv]
                for l in range(8):
                    for q, (a, b) in enumerate(MODES):
                        e = pe.matmul(ps[0:64, 4 + kv, 0:256], blocks[b][:, 8 * (i % 2) + l, :], part(a, n % 2, l * 256, 256),
                                      start=(i % 2 == 0 and l == 0 and q == 0), stop=(i % 2 == 1 and l == 7 and q == 2),
                                      skip_group_check=True)
                e.then_inc(w_used, 1)

            for i in range(NV):
                n = MIX + 2 * i
                pair = 2 * ((MIX + i) % 2)
                pe.wait_ge(lo_ready, n + 1)
                pe.wait_ge(act_read, PAIR_PROJ + NPROJ + i - 1)
                pe.wait_ge(dve_read, NPROJ + i - 1)
                for t in range(NT):
                    tokens = slice(t * P, t * P + P) if i < 2 else slice(t, S, 4)
                    for k in range(KD):
                        for q, (a, b) in enumerate(MODES):
                            e = pe.matmul(ps[:, pair + t // 2, (t % 2) * 256:(t % 2) * 256 + 256],
                                          xn[b][:, k, tokens], part(a, n % 2, k * 256, 256),
                                          start=(k == 0 and q == 0), stop=(k == KD - 1 and q == 2))
                e.then_inc(w_used, 1)
                compress(i)
            pe.wait_ge(wg_lo_ready, 1)
            wg = (wg_hi, wg_lo)
            for k in range(KD):
                for q, (a, b) in enumerate(MODES):
                    e = pe.matmul(ps[0:24, 7, :], wg[a][:, k, :], xn[b][:, k, :],
                                  start=(k == 0 and q == 0), stop=(k == KD - 1 and q == 2))
            e.then_inc(gn_done, 1)
            pe.wait_ge(hid_ready, 2)
            for kv in range(2):
                for c in range(2):
                    e = pe.transpose(ps[:, 6, (2 * kv + c) * 64:(2 * kv + c) * 64 + 64], hid_row[0:64, kv, c, :], ident[0:64, 0:64])
            e.then_inc(hidT_done, 1)
            pe.wait_ge(g_row_ready, 1)
            for t in range(NT):
                e = pe.transpose(ps[:, 4, t * 24:t * 24 + 24], gates_row[0:24, t * P:t * P + P], ident[0:24, 0:24])
            e.then_inc(gT_done, 1)
            pe.wait_ge(w2_loaded, 48)
            pe.wait_ge(hidT_ready, 1)
            for c in range(2):
                pe.matmul(ps[:, 5, 0:64], w2k[:, c, :, :].rearrange("p a b -> p (a b)"), hid_k[:, c, :],
                          start=(c == 0), stop=(c == 1))
            for g in range(NSA_G):
                for c in range(2):
                    e = pe.matmul(ps[:, 5, P + g * HD:P + g * HD + HD],
                                  hid_v[:, c, g, :, :].rearrange("p a b -> p (a b)"), w2v[:, c, :], start=(c == 0), stop=(c == 1))
            e.then_inc(c2_done, 1)

            def widen(row):
                kind, h, t, _ = row
                if (kind, t) == ("w", 0) or h == DIL_H - 1:
                    return 0, 0
                return (HD, 0) if (kind, t) == ("w", 2) else (0, HD)

            def operands(row):
                before, after = widen(row)
                kind, h, t, keys = row
                if kind[0] == "d":
                    rows = slice((h % 2) * HD, (h % 2) * HD + HD)
                    q = qd[rows, h // 2, t * P:t * P + P]
                    k = kd[rows, h // 2, keys[0] * P:(keys[-1] + 1) * P]
                    v = [v_all[:, x, 256 + h * HD:256 + h * HD + HD + after] for x in keys]
                else:
                    g = h // HPG
                    rows = slice(g * HD, g * HD + HD)
                    q = qn[rows, h % HPG, t * P:t * P + P]
                    k = kv4[rows, 2 + (kind == "w"), keys[0] * P:(keys[-1] + 1) * P]
                    c0 = (kind == "w") * P + g * HD
                    v = [v_all[:, x, c0 - before:c0 + HD + after] for x in keys]
                return q, k, v

            def scores(u):
                if u >= 3:
                    pe.wait_ge(s_biased, u - 2)
                if NDU <= u < N0:
                    t = u - NDU
                    tokens = slice(t * P, t * P + P)
                    by_group = ps[:, u % 3, 0:256].rearrange("p (h g n) -> p g h n", g=NSA_G, n=CPAD)
                    for g in range(NSA_G):
                        pe.matmul(by_group[:, g], bias_cT[:, g, tokens], ident[:, :], start=(g == 0), stop=False,
                                  skip_group_check=True)
                    for h in range(HPG):
                        e = pe.matmul(ps[:, u % 3, 64 * h:64 * h + P], qn[:, h, tokens],
                                      kc_pad[:, :, :].rearrange("p g n -> p (g n)"), start=False, stop=True, skip_group_check=True)
                    e.then_inc(s_done, 1)
                    return
                c0 = 0
                for row in ALL[u]:
                    q, k, _ = operands(row)
                    c1 = c0 + P * len(row[3])
                    e = pe.matmul(ps[:, u % 3, c0:c1], q, k, start=True, stop=True)
                    c0 = c1
                e.then_inc(s_done, 1)

            def transposes(u):
                pe.wait_ge(p_ready, u + 1)
                if u >= 2:
                    pe.wait_ge(pT_ready, u - 1)
                n = sum(len(row[3]) for row in ALL[u])
                for x in range(n):
                    e = pe.transpose(ps[:, 3 + u % 2, x * P:x * P + P], p_sb[:, u % 2, x * P:x * P + P], ident[:, :])
                e.then_inc(pT_done, 1)

            def values(u):
                pe.wait_ge(pT_ready, u + 1)
                if NDU <= u < N0:
                    t = u - NDU
                    if t == 1:
                        pe.wait_ge(o_read, NDU)
                    if t >= 2:
                        pe.wait_ge(yc_ready, t - 1)
                    for g in range(NSA_G):
                        e = pe.matmul(ps[:, 7 - t % 2, g * 256:g * 256 + 256], pT_sb[:, u % 2, g * P:g * P + P],
                                      vc_diag[:, g, :], start=True, stop=True)
                    e.then_inc(pv_done, 1)
                    return
                x = 0
                for i, row in enumerate(ALL[u]):
                    _, _, v = operands(row)
                    if u < NDU:
                        bank, o0 = 5 + u % 2, i * HD
                    else:
                        bank, o0 = 5 + (u - N0) // 5 % 2, place(row) * HD
                    before, after = widen(row)
                    for j, vj in enumerate(v):
                        e = pe.matmul(ps[:, bank, o0 - before:o0 + HD + after], pT_sb[:, u % 2, x * P:x * P + P], vj,
                                      start=(j == 0), stop=(j == len(v) - 1))
                        x += 1
                e.then_inc(pv_done, 1)

            pe.wait_ge(dve_read, NPROJ + NV)
            pe.wait_ge(act_read, PAIR_GATE)
            pe.wait_ge(gates_ready, 1)
            for i in range(NU + 3):
                if i == NDU:
                    pe.wait_ge(kc_ready, 1)
                    pe.wait_ge(cmp_loaded, 16 * NSA_H)
                if i < NU:
                    scores(i)
                if 2 <= i < NU + 2:
                    transposes(i - 2)
                u = i - 3
                if u >= 0:
                    if 2 <= u < NDU:
                        pe.wait_ge(o_read, u - 1)
                    if u == N0 + 5:
                        pe.wait_ge(yc_ready, NT)
                    if u >= N0 + 10 and (u - N0) % 5 == 0:
                        pe.wait_ge(o_nsa_read, (u - N0) // 5 - 1)
                    values(u)

            pe.wait_ge(s_biased, NU)
            pe.wait_ge(pT_ready, NU)

            def gate_pair(i):
                for u in range(2):
                    pe.wait_ge(lo_ready, 2 * i + (GATE + u + 1))
                    pe.wait_ge(act_read, 2 * i + (PAIR_GATE + u - 1))
                    cols_step((GATE + u) % 2)

            with pe.Fori(0, 2) as i:
                gate_pair(i)
            pe.wait_ge(o_nsa_read, NSA_H)
            for c in range(2):
                for g in range(3):
                    if c == 0:
                        pe.wait_ge(odil_scaled, 4 * (g + 1))
                    if 3 * c + g >= 4:
                        pe.wait_ge(yd_summed, 3 * c + g - 3)
                    for r in range(4):
                        e = pe.transpose(ps[:, 4 + (3 * c + g) % 4, r * P:r * P + P],
                                         o_dil[:, g, r, 2 * c:2 * c + 2, :].rearrange("p a b -> p (a b)"), ident[:, :])
                    e.then_inc(ydT_done, 1)
            gate_pair(2)
            pe.wait_ge(yd_summed, 6)
            pe.wait_ge(y_nsa_ready, 1)
            for c in range(4):
                for t in range(NT):
                    e = pe.transpose(ps[:, 4 + c, t * P:t * P + P],
                                     y_nsa[:, t, 2 * c:2 * c + 2, :].rearrange("p a b -> p (a b)"), ident[:, :])
                e.then_inc(ynT_done, 1)
            gate_pair(3)

            pe.wait_ge(lo_ready, BDIL + 1)
            pe.wait_ge(ydlo_ready, 2)
            pe.wait_ge(ynlo_ready, 4)
            ydp, ynp = (yd_hi, yd_lo), (yn_hi, yn_lo)
            for m in range(KD):
                if m >= 4:
                    pe.wait_ge(b_gated, m - 3)
                for k in range(2):
                    for q, (a, b) in enumerate(MODES):
                        e = pe.matmul(ps[:, 4 + m % 4, :], part(a, BDIL % 2, k * D + m * P, P), ydp[b][:, k, :],
                                      start=(k == 0 and q == 0), stop=(k == 1 and q == 2))
                e.then_inc(b_done if m < KD - 1 else w_used, 1)
            pe.wait_ge(act_read, PAIR_FFN2)
            for m in range(KD):
                n = BNSA + m // 4
                if m % 4 == 0:
                    pe.wait_ge(lo_ready, n + 1)
                if m >= 4:
                    pe.wait_ge(a_gated, m - 3)
                for k in range(4):
                    for q, (a, b) in enumerate(MODES):
                        e = pe.matmul(ps[:, m % 4, :], part(a, n % 2, k * S + (m % 4) * P, P), ynp[b][:, k, :],
                                      start=(k == 0 and q == 0), stop=(k == 3 and q == 2))
                e.then_inc(a_done if m % 4 < 3 else w_used, 1)
            pe.wait_ge(b_gated, KD)
            for i in range(4):
                n = OUT + i
                pe.wait_ge(lo_ready, n + 1)
                if i < 2:
                    pe.wait_ge(a_gated, 4 + 2 * i + 2)
                order = [(k, c) for k in range(KD) for c in range(2)] if i == 0 else [(k, c) for c in range(2) for k in range(KD)]
                for k, c in order:
                    if i == 0 and c == 0:
                        pe.wait_ge(mlo_ready, k + 1)
                    for q, (a, b) in enumerate(MODES):
                        e = pe.matmul(ps[:, 2 * i + c, :], part(a, n % 2, k * 256 + c * P, P), xn[b][:, k, :],
                                      start=(k == 0 and q == 0), stop=(k == KD - 1 and q == 2))
                    if k == KD - 1:
                        e.then_inc(w_used if c else y_done, 1)
            norm_y(1)
            ffn(FFN2, PAIR_FFN2, UP, 2, 2)
            for m in range(KD):
                pe.wait_ge(*x_event(3, m))
                if m >= 4:
                    pe.wait_ge(o_copied, m - 3)
                for t in range(NT):
                    e = pe.transpose(ps[:, m % 4, t * P:t * P + P], xres[:, m, t * P:t * P + P], ident[:, :])
                e.then_inc(oT_done, 1)


INPUTS = ["x", "ffn1_norm_pre", "ffn1_w_gu", "ffn1_w_down", "ffn1_norm_post", "mix_norm_pre", "w_in",
          "cmp_pos_k", "cmp_w1_k", "cmp_w2_k", "cmp_pos_v", "cmp_w1_v", "cmp_w2_v",
          "w_branch_nsa", "w_branch_dil", "w_out", "mix_norm_post",
          "ffn2_norm_pre", "ffn2_w_gu", "ffn2_w_down", "ffn2_norm_post", "rel_bias"]


def kernel(**inputs):
    import concourse.bacc as bacc
    from concourse.bass_utils import run_bass_kernel_spmd

    nc = bacc.Bacc("TRN2", target_bir_lowering=False, num_devices=1)
    arrays, args = {}, []
    for name in INPUTS:
        a = np.ascontiguousarray(inputs[name])
        if name != "rel_bias":
            a = a[0]
        arrays[f"in_{name}"] = a
    arrays["bucket_of_distance"] = bucket_table()
    for name, a in arrays.items():
        args.append(nc.dram_tensor(name, a.shape, mybir.dt.from_np(a.dtype), kind="ExternalInput").ap())
    args.append(nc.dram_tensor("out", (S, D), F32, kind="ExternalOutput").ap())
    layer_kernel(nc, *args)
    r = run_bass_kernel_spmd(nc, [arrays], core_ids=[0])
    return r.results[0]["out"].reshape(1, S, D)
```

```python
import math

import concourse.bass as bass
import numpy as np
from concourse import mybir

F32 = mybir.dt.float32
F32R = mybir.dt.float32r
ALU = mybir.AluOpType
ACT = mybir.ActivationFunctionType
AX_X = mybir.AxisListType.X

P = 128
S, D, F = 512, 1024, 2816
NT = S // P
KD = D // P
KF = F // P
HD = 64
NSA_H, NSA_G, HPG = 8, 2, 4
DIL_H, SLOTS = 12, 4
CB, CS = 32, 16
NCMP = (S - CB) // CS + 1
CPAD = 32
BUCKETS, MAX_DIST = 32, 2048
EPS = 1e-6
SCALE = HD ** -0.5
MASKED = 1e30
BIGGEST = 3e38

QN = 0
KCMP, VCMP, KSLC, VSLC, KWIN, VWIN = (NSA_H * HD + i * NSA_G * HD for i in range(6))
GN = NSA_H * HD + 6 * NSA_G * HD
QD = GN + 3 * NSA_H
KDL = QD + DIL_H * HD
VDL = KDL + DIL_H * HD
GA = VDL + DIL_H * HD
GB = GA + D

DIL_KEYS = 2 * P
NSA_W = 640
CMP_W = 1024
D0_W = 384
D12_W = 256
NSA_AT, CMP_AT = 0, NSA_W
D0_AT = CMP_AT + CMP_W
D1_AT = D0_AT + D0_W
D2_AT = D1_AT + D12_W
TAB_W = D2_AT + D12_W
assert TAB_W == 5 * S
BIAS_PARTS = ((0, 1), (2, 3, 4))
BIAS_BANKS = (4, 5, 6, 4, 5)
CMP_ZERO = CB - 1 + CS * (CPAD - 1)

W = 2048
UP, DOWN = KF, KF // 2
FFN1 = 0
PROJ = FFN1 + UP + DOWN
NPROJ, NV, NCOMP = 10, 4, 4
MIX = PROJ + NPROJ
GATE = MIX + NV + NCOMP
NGATE = 8
BDIL = GATE + NGATE
BNSA = BDIL + 1
OUT = BNSA + 2
FFN2 = OUT + 4
STEPS = FFN2 + UP + DOWN
PAIR_PROJ = UP
PAIR_GATE = PAIR_PROJ + NV
PAIR_FFN2 = PAIR_GATE + NGATE


def bucket(d):
    d = np.maximum(d, 0)
    exact = BUCKETS // 2
    large = exact + (np.log(np.maximum(d, exact).astype(np.float32) / np.float32(exact))
                     / np.float32(math.log(MAX_DIST / exact)) * (BUCKETS - exact)).astype(np.int32)
    return np.where(d < exact, d, np.minimum(large, BUCKETS - 1))


def bucket_table():
    i = np.arange(TAB_W)
    dist = np.zeros(TAB_W, np.int64)
    keep = np.ones(TAB_W, bool)
    a = i[NSA_AT:CMP_AT] - NSA_AT
    dist[NSA_AT:CMP_AT] = S - 1 - a
    dist[CMP_AT:D0_AT] = np.arange(CMP_W) - (CMP_ZERO)
    d0 = DIL_KEYS - 1 - np.arange(D0_W)
    dist[D0_AT:D1_AT] = d0
    keep[D0_AT:D1_AT] = d0 <= P
    d1 = P - 1 - np.arange(D12_W)
    dist[D1_AT:D2_AT] = 4 * d1
    dist[D2_AT:TAB_W] = 4 * d1
    keep[D2_AT:TAB_W] = d1 % 4 == 0
    keep &= dist >= 0
    out = np.zeros((BUCKETS + 1, TAB_W), np.float32)
    out[bucket(dist), i] = keep
    out[BUCKETS] = ~keep
    return out


def units():
    dil, nsa = [], []
    cmp_ = [[("c", None, t, [0, 1])] for t in range(NT)]
    for j in range(DIL_H):
        if j < SLOTS:
            dil.append([("d0", j, t, [t - 1, t] if t else [0]) for t in (0, 1)])
            dil.append([("d0", j, t, [t - 1, t]) for t in (2, 3)])
        else:
            dil.append([("d12", j, r, [r]) for r in range(4)])
    for c in range(NSA_H):
        h = c // 2 + HPG * (c % 2)
        full = lambda b, t: (b, h, t, list(range(t + 1)))
        nsa += [[full("s", 1), full("w", 1)], [full("s", 3)], [full("w", 3)],
                [full("s", 0), full("s", 2)], [full("w", 2), full("w", 0)]]
    return dil, cmp_, nsa


def place(row):
    kind, _, t, _ = row
    return (t // 2 * 2 if t % 2 else 4 + t // 2) + (kind == "w") * (1 if t % 2 else 2)


def layer_kernel(nc, x, g1_pre, w1_gu, w1_down, g1_post, gm_pre, w_in, pos_k, cw1_k, cw2_k,
                 pos_v, cw1_v, cw2_v, w_bn, w_bd, w_out, gm_post, g2_pre, w2_gu, w2_down, g2_post,
                 rel, onehot, out):
    DIL, CMP, NSA = units()
    NDU, NNU = len(DIL), len(NSA)
    N0 = NDU + NT

    K = 1024
    ARENA = 207 * K
    base = (nc.sbuf_base + 31) // 32 * 32
    nc.alloc_sbuf_tensor("arena", [P, ARENA], mybir.dt.uint8)

    def at(name, offset, shape, dt=F32):
        return nc.alloc_sbuf_tensor_at(name, [P] + shape, dt, offset=base + offset)

    xres = at("xres", 0, [KD, S])
    xn_hi = at("xn_hi", 16 * K, [KD, S], F32R)
    xn_lo = at("xn_lo", 32 * K, [KD, S], F32R)
    ring_raw = at("ring_raw", 48 * K, [2, W])
    ring_hi = at("ring_hi", 64 * K, [2, W], F32R)
    ring_lo = at("ring_lo", 80 * K, [2, W], F32R)
    R = 96 * K
    Y = R + 88 * K
    SM = Y + 16 * K
    hT_hi = at("hT_hi", R, [KF * S], F32R)
    hT_lo = at("hT_lo", R + 44 * K, [KF * S], F32R)
    ysb = at("ysb", Y, [KD, S])
    silu_g = at("silu_g", Y, [2, S])
    h_f32 = at("h_f32", Y + 4 * K, [2, S])
    sq_ffn = at("sq_ffn", 32 * K, [S])
    sq_mix = at("sq_mix", R, [S])
    x_tok = at("x_tok", R, [NT, D])
    gains_row = at("gains_row", R + 16 * K, [P])
    x_sq = at("x_sq", R + 28 * K, [KD, S])
    onehot_sb = at("onehot_sb", R + 56 * K, [TAB_W])
    bias_vec = at("bias_vec", R + 68 * K, [TAB_W])
    x_fin = [at("x_fin0", Y + 8 * K, [NT, D // 2]), at("x_fin1", 0, [NT, D // 2])]
    y_gained = at("y_gained", 16 * K, [KD, S])
    o_tok = at("o_tok", R, [NT, D])
    qn = at("qn", R, [4, S])
    kv4 = at("kv4", R + 8 * K, [4, S])
    qd = at("qd", R + 16 * K, [6, S])
    kd = at("kd", R + 28 * K, [6, S])
    v_all = at("v_all", R + 40 * K, [NT, D])
    bias_d0 = at("bias_d0", R + 56 * K, [SLOTS, DIL_KEYS])
    bias_d12 = at("bias_d12", R + 60 * K, [8, P])
    bias_cT = at("bias_cT", R + 64 * K, [NSA_G, S])
    o_dil = at("o_dil", R + 68 * K, [3, 4, SLOTS, HD])
    s_sb = at("s_sb", R + 80 * K, [2, S])
    p_sb = at("p_sb", R + 84 * K, [2, S])
    pT_sb = at("pT_sb", R + 88 * K, [2, S])
    y_nsa = at("y_nsa", R + 92 * K, [NT, NSA_H, HD])
    wg_raw = at("wg_raw", R + 68 * K, [KD, 24])
    wg_hi = at("wg_hi", R + 68 * K + 768, [KD, 24], F32R)
    wg_lo = at("wg_lo", R + 69 * K + 512, [KD, 24], F32R)
    w2k = at("w2k", R + 70 * K + 256, [2, 2, HD])
    w2v = at("w2v", R + 71 * K + 256, [2, HD])
    vb_hi = at("vb_hi", R + 72 * K, [16, 64], F32R)
    vb_lo = at("vb_lo", R + 76 * K, [16, 64], F32R)
    blk = at("blk", R + 80 * K, [16, 64])
    kb_hi = at("kb_hi", R + 84 * K, [16, 64], F32R)
    kb_lo = at("kb_lo", R + 88 * K, [16, 64], F32R)
    pair_k = at("pair_k", R + 92 * K, [NSA_G, S])
    pair_v = at("pair_v", R + 96 * K, [NSA_G, S])
    hid_row = at("hid_row", R + 80 * K, [2, 2, P])
    gates_row = at("gates_row", R + 96 * K, [S])
    vc_diag = at("vc_diag", R + 100 * K + 128, [NSA_G, HPG * HD])
    gates = at("gates", R + 102 * K + 128, [NT, NSA_H, 3])
    f_nsa = at("f_nsa", R + 102 * K + 512, [2, 8])
    f_c = at("f_c", R + 102 * K + 640, [NT, 8])
    nm_c = at("nm_c", R + 102 * K + 768, [2, 8])
    den_c = at("den_c", R + 102 * K + 832, [8])
    st_p = at("st_p", R + 103 * K, [4, 4, SLOTS])
    st_0 = at("st_0", R + 103 * K + 256, [NT, 2, SLOTS])
    st_n = at("st_n", R + 103 * K + 384, [NT, 4, SLOTS])
    e_n = at("e_n", R + 103 * K + 640, [3, NT, SLOTS])
    w_n = at("w_n", R + 103 * K + 832, [NT, SLOTS])
    bias_n = at("bias_n", R + 16 * K, [NSA_H, S])
    o_tmp = at("o_tmp", R + 32 * K, [2, S])
    sig = at("sig", R + 16 * K, [2 * KD, S])
    yn_hi = at("yn_hi", R + 48 * K, [4, S], F32R)
    yn_lo = at("yn_lo", R + 56 * K, [4, S], F32R)
    yd_hi = at("yd_hi", R, [2, S], F32R)
    yd_lo = at("yd_lo", R + 4 * K, [2, S], F32R)
    yd = at("yd", R + 8 * K, [2, S])
    mrg = at("mrg", R + 80 * K, [2, 2, S])
    o = [SM]

    def small(name, shape, dt=F32):
        t = at(name, o[0], shape, dt)
        o[0] += (4 * int(np.prod(shape)) + 31) // 32 * 32
        assert o[0] <= ARENA
        return t

    sq = small("sq", [S])
    acc = small("acc", [S])
    rb = at("rb", SM, [S])
    hid_k = at("hid_k", R + 88 * K, [2, 64])
    hid_v = at("hid_v", SM + 2 * K, [2, NSA_G, HPG, CPAD])
    ident = small("ident", [P])
    ones = small("ones", [P])
    eps = small("eps", [1])
    gains = small("gains", [6, KD])
    sd = small("sd", [NT])
    rstd = small("rstd", [NT])
    tab = small("tab", [20])
    posT = small("posT", [2, 16])
    stat_m = small("stat_m", [16])
    stat_d = small("stat_d", [16])
    c_p = small("c_p", [4, 2, SLOTS])
    c_n = small("c_n", [NT, 2, SLOTS])
    valid = small("valid", [1])
    warm = small("warm", [1])
    x_ss = small("x_ss", [NT])
    rstd_s = small("rstd_s", [4])
    kc_pad = small("kc_pad", [2 * NSA_G, CPAD])
    ps = nc.alloc_psum_tensor("ps", [P, 8, S], F32)

    vec_dram = nc.dram_tensor("bias_by_distance", [20, TAB_W], F32, kind="Internal").ap()
    rep_n = nc.dram_tensor("bias_rows_sparse", [P, NSA_H, NSA_W], F32, kind="Internal").ap()
    rep_d0 = nc.dram_tensor("bias_rows_dense", [P, SLOTS, D0_W], F32, kind="Internal").ap()
    rep_d1 = nc.dram_tensor("bias_rows_strided4", [P, SLOTS, D12_W], F32, kind="Internal").ap()
    rep_d2 = nc.dram_tensor("bias_rows_strided16", [P, SLOTS, D12_W], F32, kind="Internal").ap()
    rep_c = nc.dram_tensor("bias_rows_compressed", [CPAD, NSA_H, CMP_W], F32, kind="Internal").ap()
    st_dram = nc.dram_tensor("dilated_stats", [S, 16], F32, kind="Internal").ap()
    c_dram = nc.dram_tensor("dilated_weights", [S, 8], F32, kind="Internal").ap()

    sem = lambda name: nc.alloc_semaphore(name)
    raw_loaded = [sem("raw_loaded0"), sem("raw_loaded1")]
    hi_half, g1_loaded = sem("hi_half"), sem("g1_loaded")
    xfT_done, xf_copied, y_copied, o_ready = sem("xfT_done"), sem("xf_copied"), sem("y_copied"), sem("o_ready")
    g_scaled, up_scaled, x_summed = sem("g_scaled"), sem("up_scaled"), sem("x_summed")
    hi_ready, lo_ready, w_used = sem("hi_ready"), sem("lo_ready"), sem("w_used")
    x_loaded = [sem(f"x_loaded{t}") for t in range(NT)]
    small_loaded, gains_loaded, x_sums = sem("small_loaded"), sem("gains_loaded"), sem("x_sums")
    consts, vec_mm, vec_copied, vec_stored = sem("consts"), sem("vec_mm"), sem("vec_copied"), sem("vec_stored")
    tab_ready, rows_stored = sem("tab_ready"), sem("rows_stored")
    xT_done = sem("xT_done")
    act_read, dve_read = sem("act_read"), sem("dve_read")
    h_ready, hhi_ready, hlo_ready = sem("h_ready"), sem("hhi_ready"), sem("hlo_ready")
    y_done, y_squared, y_summed = sem("y_done"), sem("y_squared"), sem("y_summed")
    ss_done, sd_ready, rstd_ready, rb_ready = sem("ss_done"), sem("sd_ready"), sem("rstd_ready"), sem("rb_ready")
    x_scaled, x_new, x_new_pool, x_squared = sem("x_scaled"), sem("x_new"), sem("x_new_pool"), sem("x_squared")
    xhi_ready, xlo_ready, gates_scaled, gn_scaled, rstd_s_done = (
        sem("xhi_ready"), sem("xlo_ready"), sem("gates_scaled"), sem("gn_scaled"), sem("rstd_s_done"))
    rstd_s_ready = sem("rstd_s_ready")
    oT_done, out_stored = sem("oT_done"), sem("out_stored")
    biases_loaded, bias_n_loaded, cmp_loaded = sem("biases_loaded"), sem("bias_n_loaded"), sem("cmp_loaded")
    wg_loaded, wg_hi_ready, wg_lo_ready = sem("wg_loaded"), sem("wg_hi_ready"), sem("wg_lo_ready")
    gn_done, gates_ready = sem("gn_done"), sem("gates_ready")
    pairs_loaded, blk_ready, bhi_ready, blo_ready = [sem("pair_k_loaded"), sem("pair_v_loaded")], sem("blk_ready"), sem("bhi_ready"), sem("blo_ready")
    hid_ready, c2_done, kc_ready = sem("hid_ready"), sem("c2_done"), sem("kc_ready")
    hidT_done, hidT_ready, g_row_ready, gT_done = sem("hidT_done"), sem("hidT_ready"), sem("g_row_ready"), sem("gT_done")
    s_done, s_biased, p_ready, pT_done, pT_ready, o_read = (
        sem("s_done"), sem("s_biased"), sem("p_ready"), sem("pT_done"), sem("pT_ready"), sem("o_read"))
    yc_ready = sem("yc_ready")
    stats_stored, stats_loaded, e_in, e_ready, c_ready, c_stored, c_loaded = (
        sem("stats_stored"), sem("stats_loaded"), sem("e_in"), sem("e_ready"), sem("c_ready"), sem("c_stored"), sem("c_loaded"))
    w2_loaded = sem("w2_loaded")
    cT_gains = sem("gains_transposed")
    gains_ready = sem("gains_ready")
    o_nsa_read = sem("o_nsa_read")
    pv_done = sem("pv_done")
    odil_scaled, ydT_done, yd_summed, ydhi_ready, ydlo_ready = (
        sem("odil_scaled"), sem("ydT_done"), sem("yd_summed"), sem("ydhi_ready"), sem("ydlo_ready"))
    y_nsa_ready, ynT_done, ynhi_ready, ynlo_ready = sem("y_nsa_ready"), sem("ynT_done"), sem("ynhi_ready"), sem("ynlo_ready")
    b_done, b_gated, a_done, a_gated, merged, mhi_ready, mlo_ready = (
        sem("b_done"), sem("b_gated"), sem("a_done"), sem("a_gated"), sem("merged"), sem("mhi_ready"), sem("mlo_ready"))
    dve_chain = sem("dve_chain")

    f32 = lambda ap: ap.bitcast(F32)
    heads2 = lambda ap: ap.rearrange("p (a b) -> p a b", b=HD)
    by_k = lambda ap: ap.rearrange("(k p) c -> p k c", p=P)
    MODES = ((0, 0), (0, 1), (1, 0))
    ring = (ring_hi, ring_lo)
    xn = (xn_hi, xn_lo)
    hT = (hT_hi, hT_lo)

    def stat_dil(row):
        _, j, t, _ = row
        g, slot = j // SLOTS, j % SLOTS
        if g == 0:
            return st_0[:, t, 0, slot:slot + 1], st_0[:, t, 1, slot:slot + 1]
        return (st_p[:, t, 2 * (g - 1), slot:slot + 1], st_p[:, t, 2 * (g - 1) + 1, slot:slot + 1])

    def stat_nsa(turn):
        def of(row):
            i = 8 * (turn % 2) + place(row)
            return stat_m[:, i:i + 1], stat_d[:, i:i + 1]
        return of

    def stats_of(u):
        return stat_dil if u < NDU else stat_nsa((u - N0) // 5)

    def paired_views(dst, c):
        out = []
        for h in range(2):
            to = dst[:, c % 2, :].rearrange("p (k h g d) -> p k h g d", h=2, g=2, d=HD)[:, :, h]
            of = ring_raw[:, c % 2, :].rearrange("p (k g h d) -> p k g h d", h=2, g=2, d=HD)[:, :, :, h]
            out.append((to, of))
        return out

    def y_event(p, m):
        if p == 1:
            return (w_used, OUT + m // 2 + 1) if m % 2 else (y_done, KD - 1 + m // 2 + 1)
        first, end = (0, PROJ) if p == 0 else (KD - 1 + 4, STEPS)
        return (y_done, first + m + 1) if m < KD - 1 else (w_used, end)

    FIN = (((0, 4, 0), (1, 5, 0), (2, 6, 0)), ((3, 4, 1), (4, 5, 2)), ((5, 4, 4), (6, 5, 5), (7, 6, 5)))

    def xlo_event(r, m):
        return xlo_ready, KD * r + m + 1

    def x_event(r, m):
        if r in (1, 2):
            return x_new_pool, KD * (r - 1) + m + 1
        return x_new, m + 1

    def square_of(p, m):
        return acc if m == 0 else sq if m % 2 else sq_mix if p == 1 else sq_ffn

    def b_event(m):
        return (b_done, m + 1) if m < KD - 1 else (w_used, BDIL + 1)

    def a_event(m):
        return (a_done, m + 1 - m // 4) if m % 4 < 3 else (w_used, BNSA + m // 4 + 1)

    ALL = DIL + CMP + NSA
    NU = len(ALL)
    block = nc.Block()
    with block:

        @block.sync
        def _(sp):
            for t in range(NT):
                sp.dma_start(x_tok[:, t, :], x[t * P:t * P + P, :]).then_inc(x_loaded[t], 16)

            def load(i, c, first, second):
                if not (isinstance(i, int) and 2 * i + c < 2):
                    sp.wait_ge(lo_ready, 2 * i + (c - 1))
                for dst, src in (first, second):
                    sp.dma_start(dst, src).then_inc(raw_loaded[c % 2], 16)

            def view(c, inner):
                return ring_raw[:, c % 2, :].rearrange("p (k c) -> p k c", c=inner)

            def load_up(w_gu, base, i, u):
                v = view(base + u, 256)
                load(i, base + u,
                     (v[:, :, 0:P], by_k(w_gu[:, bass.ds(i * (2 * P) + u * P, P)])),
                     (v[:, :, P:256], by_k(w_gu[:, bass.ds(i * (2 * P) + (u * P + F), P)])))

            def load_down(w_down, base, i, u):
                v = view(base + u, D)
                load(i, base + u, (v[:, 0, :], w_down[bass.ds(i * (4 * P) + 2 * u * P, P), :]),
                     (v[:, 1, :], w_down[bass.ds(i * (4 * P) + (2 * u + 1) * P, P), :]))

            def load_cols(n, w, c0):
                v = view(n, 256)
                src = by_k(w[:, c0:c0 + 256])
                load(0, n, (v[:, 0:4, :], src[:, 0:4, :]), (v[:, 4:8, :], src[:, 4:8, :]))

            def load_two(n, w, c0, c1):
                v = view(n, 256)
                load(0, n, (v[:, :, 0:P], by_k(w[:, c0:c0 + P])), (v[:, :, P:256], by_k(w[:, c1:c1 + P])))

            def load_ffn(w_gu, w_down, base):
                for u in range(2):
                    load_up(w_gu, base, 0, u)
                with sp.Fori(1, UP // 2) as i:
                    for u in range(2):
                        load_up(w_gu, base, i, u)
                load_down(w_down, base + UP, 0, 0)
                with sp.Fori(0, (DOWN - 1) // 2) as i:
                    for u in range(1, 3):
                        load_down(w_down, base + UP, i, u)

            load_ffn(w1_gu, w1_down, FFN1)
            for i in range(2):
                load_two(PROJ + i, w_in, QN + P * i, QN + P * (i + 2))
            load_cols(PROJ + 2, w_in, KCMP)
            load_two(PROJ + 3, w_in, KSLC, KWIN)
            for i in range(3):
                load_cols(PROJ + 4 + i, w_in, QD + 256 * i)
            for i in range(3):
                load_cols(PROJ + 7 + i, w_in, KDL + 256 * i)
            for i, w1 in enumerate((cw1_k, cw1_k, cw1_v, cw1_v)):
                if i == 0:
                    load_two(MIX, w_in, VSLC, VWIN)
                else:
                    load_cols(MIX + 2 * i, w_in, VDL + 256 * (i - 1))
                load_cols(MIX + 2 * i + 1, w1[(i % 2) * D:(i % 2) * D + D, :], 0)
            for i in range(NGATE):
                load_cols(GATE + i, w_in, GA + 256 * i)
            v = view(BDIL, D)
            load(0, BDIL, (v[:, 0, :], w_bd[0:P, :]), (v[:, 1, :], w_bd[P:2 * P, :]))
            for i in range(2):
                v, src = view(BNSA + i, S), by_k(w_bn[:, i * S:i * S + S])
                load(0, BNSA + i, (v[:, 0:2, :], src[:, 0:2, :]), (v[:, 2:4, :], src[:, 2:4, :]))
            for i in range(4):
                load_cols(OUT + i, w_out, 256 * i)
            load_ffn(w2_gu, w2_down, FFN2)
            for j in range(2 * NT):
                t, cols = j % NT, slice(j // NT * S, j // NT * S + S)
                sp.wait_ge(o_ready, j + 1)
                sp.dma_start(out[t * P:t * P + P, cols], o_tok[:, t, cols]).then_inc(out_stored, 16)
            sp.wait_ge(out_stored, 16 * 2 * NT)

        @block.gpsimd
        def _(pool):
            pool.memset(ident[:, :], 0.0).then_inc(consts, 1)
            pool.memset(ones[:, :], 1.0).then_inc(consts, 1)
            pool.memset(eps[:, :], EPS).then_inc(consts, 1)
            pool.memset(valid[:, :], 1.0).then_inc(consts, 1)
            pool.wait_ge(consts, 4)
            pool.affine_select(out=ident[:, :], in_=ident[:, :], compare_op=ALU.not_equal, fill=1.0,
                               base=0, pattern=[[-1, P]], channel_multiplier=1).then_inc(consts, 1)
            pool.affine_select(out=valid[:, :], in_=valid[:, :], compare_op=ALU.is_ge, fill=0.0,
                               base=-(CB - 1), pattern=[[0, 1]], channel_multiplier=1).then_inc(consts, 1)
            pool.dma_start(tab[0:BUCKETS, :], rel).then_inc(small_loaded, 16)
            pool.dma_start(onehot_sb[0:BUCKETS + 1, :], onehot).then_inc(small_loaded, 16)
            def add_y(r):
                for m in range(KD):
                    pool.wait_ge(x_scaled, KD * (r - 1) + m + 1)
                    pool.tensor_tensor(xres[:, m, :], xres[:, m, :], ysb[:, m, :], ALU.add).then_inc(x_new_pool, 1)

            def sum_squares(r):
                for m in range(1, KD):
                    pool.wait_ge(x_squared, KD * (r - 1) + m + 1)
                    if m > 1:
                        pool.wait_ge(x_summed, (KD - 1) * (r - 1) + m - 1)
                    pool.tensor_tensor(acc[:, :], x_sq[:, 0, :] if m == 1 else acc[:, :], x_sq[:, m, :],
                                       ALU.add).then_inc(x_summed, 1)

            pool.wait_ge(vec_copied, 5)
            pool.dma_start(vec_dram, bias_vec[0:20, :]).then_inc(vec_stored, 16)
            pool.wait_ge(vec_stored, 16)

            for dst, head, at0 in ((rep_n, 0, NSA_AT), (rep_d0, NSA_H, D0_AT), (rep_d1, NSA_H + SLOTS, D1_AT),
                                   (rep_d2, NSA_H + 2 * SLOTS, D2_AT), (rep_c, 0, CMP_AT)):
                rows, heads, width = dst.shape
                src = bass.AP(tensor=vec_dram.tensor, offset=head * TAB_W + at0,
                              ap=[[0, rows], [TAB_W, heads], [1, width]])
                pool.dma_start(dst, src).then_inc(rows_stored, 16)
            pool.wait_ge(rows_stored, 80)

            def spread(rows, step, first, width):
                n, heads, w = rows.shape
                return bass.AP(tensor=rows.tensor, offset=first, ap=[[heads * w - step, n], [w, heads], [1, width]])

            add_y(1)
            sum_squares(1)
            pool.wait_ge(w_used, PROJ)
            pool.dma_start(wg_raw[:, :, :], by_k(w_in[:, GN:GN + 24])).then_inc(wg_loaded, 16)
            for dst, w2 in ((w2k[:, :, 0, :], cw2_k), (w2k[:, :, 1, :], cw2_k), (w2v[:, :, :], cw2_v)):
                pool.dma_start(dst, w2.rearrange("(c p) d -> p c d", p=P)).then_inc(w2_loaded, 16)
            pool.dma_start(bias_d0[:, :, :], spread(rep_d0, 1, P - 1, DIL_KEYS)).then_inc(biases_loaded, 16)
            pool.dma_start(bias_d12[:, 0:4, :], spread(rep_d1, 1, P - 1, P)).then_inc(biases_loaded, 16)
            pool.dma_start(bias_d12[:, 4:8, :], spread(rep_d2, 1, P - 1, P)).then_inc(biases_loaded, 16)
            for g in range(NSA_G):
                for h in range(HPG):
                    src = bass.AP(tensor=rep_c.tensor, offset=(g * HPG + h) * CMP_W + CMP_ZERO - (CB - 1),
                                  ap=[[NSA_H * CMP_W - CS, CPAD], [1, S]])
                    pool.dma_start(bias_cT[h * CPAD:(h + 1) * CPAD, g, :], src).then_inc(cmp_loaded, 16)
            pool.wait_ge(dve_read, 3)
            for i, pair in enumerate((pair_k, pair_v)):
                for g in range(NSA_G):
                    src = kv4[g * HD:g * HD + HD, i, :]
                    pool.dma_start(pair[0:HD, g, :], src).then_inc(pairs_loaded[i], 16)
                    pool.dma_start(pair[HD:P, g, 0:S - 1], src[:, 1:S]).then_inc(pairs_loaded[i], 16)
            pool.wait_ge(s_done, NDU)
            pool.dma_start(bias_n[:, :, :], spread(rep_n, 1, P - 1, S)).then_inc(bias_n_loaded, 16)
            pool.wait_ge(p_ready, NDU)
            pool.dma_start(st_dram.rearrange("(l r) c -> l (r c)", r=4),
                           st_p[:, :, :, :].rearrange("p a b c -> p (a b c)")).then_inc(stats_stored, 16)
            pool.wait_ge(stats_stored, 16)
            pool.dma_start(st_n[:, :, :, :].rearrange("p t a b -> p t (a b)"),
                           st_dram.rearrange("(t p) c -> p t c", p=P)).then_inc(stats_loaded, 16)
            pool.wait_ge(c_ready, 1)
            pool.dma_start(c_dram.rearrange("(t p) c -> p t c", p=P),
                           c_n[:, :, :, :].rearrange("p t a b -> p t (a b)")).then_inc(c_stored, 16)
            pool.wait_ge(c_stored, 16)
            pool.dma_start(c_p[:, :, :, :].rearrange("p a b c -> p (a b c)"),
                           c_dram.rearrange("(l r) c -> l (r c)", r=4)).then_inc(c_loaded, 16)
            pool.wait_ge(c_loaded, 16)
            pool.wait_ge(o_read, NDU)
            for g in range(3):
                for r in range(4):
                    c = e_n[:, 0, r, :] if g == 0 else c_p[:, r, g - 1, :]
                    pool.tensor_tensor(o_dil[:, g, r, :, :], o_dil[:, g, r, :, :],
                                       c.unsqueeze(2).broadcast_to([P, SLOTS, HD]), ALU.mult).then_inc(odil_scaled, 1)
            add_y(2)
            sum_squares(2)

        @block.scalar
        def _(act):
            def hi(i, c, paired=False):
                act.wait_ge(raw_loaded[c % 2], 32 * i + 32 * (c // 2 + 1))
                if not (isinstance(i, int) and 2 * i + c < 2):
                    act.wait_ge(w_used, 2 * i + (c - 1))
                for dst, src in paired_views(ring_hi, c) if paired else [(ring_hi[:, c % 2, :], ring_raw[:, c % 2, :])]:
                    e = act.activation(dst, src, ACT.Copy)
                e.then_inc(hi_ready, 1)

            def hi_halves(n):
                act.wait_ge(raw_loaded[n % 2], 32 * (n // 2 + 1))
                act.wait_ge(w_used, n - 1)
                for half, done in ((slice(0, W // 2), hi_half), (slice(W // 2, W), hi_ready)):
                    act.activation(ring_hi[:, n % 2, half], ring_raw[:, n % 2, half], ACT.Copy).then_inc(done, 1)

            def root(i):
                act.wait_ge(ss_done, i)
                act.activation(sd[:, :], ps[:, 7 if i == 5 else 4 if i % 2 else 6, 0:S:P], ACT.Sqrt, scale=1.0 / D,
                               bias=eps[:, :]).then_inc(sd_ready, 1)

            def warm_root():
                act.wait_ge(consts, 6)
                act.activation(warm[:, :], eps[:, :], ACT.Sqrt, scale=1.0 / D, bias=eps[:, :])

            def round_x(r, g, chunks=range(KD)):
                for m in chunks:
                    act.wait_ge(*x_event(r, m))
                    act.activation(xn_hi[:, m, :], xres[:, m, :], ACT.Copy, scale=gains[:, g, m:m + 1]).then_inc(xhi_ready, 1)
                    if r:
                        act.activation(x_sq[:, m, :], xres[:, m, :], ACT.Square).then_inc(x_squared, 1)

            def take_y(p, m):
                if m == 0:
                    warm_root()
                act.wait_ge(*y_event(p, m))
                if m >= 3:
                    act.wait_ge(y_summed, (KD - 2) * p + m - 2)
                act.activation(square_of(p, m)[:, :], ps[:, m, :], ACT.Square).then_inc(y_squared, 1)
                if p == 2:
                    act.activation(y_gained[:, m, :], ps[:, m, :], ACT.Copy, scale=gains[:, 5, m:m + 1]).then_inc(y_copied, 1)
                else:
                    act.activation(ysb[:, m, :], ps[:, m, :], ACT.Copy)

            def copy_x(part):
                for j, bank, copies in FIN[part]:
                    act.wait_ge(xfT_done, j + 1)
                    act.activation(x_fin[j // NT][:, j % NT, :], ps[:, bank, :], ACT.Copy).then_inc(xf_copied, 1)

            def ffn(base, pair0, h0, p):
                def up(i, u):
                    act.wait_ge(g_scaled, 2 * i + (h0 + u + 1))
                    act.activation(silu_g[:, u, :], silu_g[:, u, :], ACT.Silu).then_inc(act_read, 1)
                    if p == 2 and isinstance(i, int) and u == 1:
                        copy_x(2)
                    if not (isinstance(i, int) and 2 * i + u == 0):
                        hi(i, base + u + 2)
                    act.wait_ge(h_ready, 2 * i + (h0 + u + 1))
                    act.activation(hT_hi[:, bass.ds(i * (2 * S) + u * S, S)], h_f32[:, u, :], ACT.Copy).then_inc(hhi_ready, 1)

                if p:
                    copy_x(0)
                hi(0, base + 2)
                if p:
                    copy_x(1)
                    root(4)
                for u in range(2):
                    up(0, u)
                    for c in BIAS_PARTS[u] if p == 0 else ():
                        act.wait_ge(vec_mm, c + 1)
                        act.activation(bias_vec[0:20, c * S:c * S + S], ps[0:20, BIAS_BANKS[c], :], ACT.Copy,
                                       scale=-1.0).then_inc(vec_copied, 1)
                with act.Fori(1, UP // 2) as i:
                    for u in range(2):
                        up(i, u)
                n = base + UP + 2
                hi(0, n)
                with act.Fori(0, (DOWN - 3) // 2) as i:
                    for u in range(1, 3):
                        hi(i, n + u)
                if p == 0:
                    hi(0, PROJ, paired=True)
                for m in range(KD):
                    take_y(p, m)
                root(2 * p + 1)

            for i, g in enumerate((g1_pre, g1_post, gm_pre, gm_post, g2_pre, g2_post)):
                act.dma_start(gains_row[i * KD:i * KD + KD, :], g.rearrange("(m p) -> m p", p=P)).then_inc(gains_loaded if i else g1_loaded, 16)
            for i, pos in enumerate((pos_k, pos_v)):
                act.dma_start(gains_row[6 * KD + 16 * i:6 * KD + 16 * i + 16, :],
                               pos.rearrange("(l e) d -> l (e d)", e=2)).then_inc(gains_loaded, 16)
            warm_root()
            act.wait_ge(gains_ready, 1)
            round_x(0, 0, range(0, 4))
            hi(0, 0)
            round_x(0, 0, range(4, KD))
            for t in range(NT):
                act.wait_ge(x_loaded[t], 16)
                act.activation(ysb[:, 2 * t:2 * t + 2, :].rearrange("p a b -> p (a b)"), x_tok[:, t, :], ACT.Square,
                               accum_out=x_ss[:, t:t + 1]).then_inc(x_sums, 1)
            act.wait_ge(x_sums, NT)
            act.activation(sd[:, :], x_ss[:, :], ACT.Sqrt, scale=1.0 / D, bias=eps[:, :]).then_inc(sd_ready, 1)
            hi(0, 1)
            ffn(FFN1, 0, 0, 0)
            hi(0, PROJ + 1, paired=True)
            round_x(1, 2)
            hi(0, PROJ + 2)
            root(2)
            for i in range(NPROJ):
                n = PROJ + i
                if i:
                    hi(0, n + 2)
                if i == 1:
                    act.wait_ge(wg_loaded, 16)
                    act.activation(wg_hi[:, :, :], wg_raw[:, :, :], ACT.Copy).then_inc(wg_hi_ready, 1)
                if i in (6, 8):
                    act.wait_ge(blk_ready, 2 if i == 6 else 4)
                    act.activation((kb_hi if i == 6 else vb_hi)[:, :, :], blk[:, :, :], ACT.Copy).then_inc(bhi_ready, 1)
            for i in range(NV):
                n = MIX + 2 * i
                act.wait_ge(w_used, n + 1)
                hi_halves(n + 2)
                if i == 2:
                    act.wait_ge(rstd_s_ready, 1)
                for t in range(2):
                    e = act.activation(v_all[:, t, 256 * i:256 * i + 256], ps[:, 2 * ((MIX + i) % 2), t * 256:t * 256 + 256],
                                       ACT.Copy, scale=(rstd if i < 2 else rstd_s)[:, t:t + 1])
                e.then_inc(act_read, 1)
                act.wait_ge(w_used, n + 2)
                hi_halves(n + 3)
                if i % 2:
                    act.activation(hid_row[0:64, i // 2, :, :].rearrange("p c j -> p (c j)"), ps[0:64, 4 + i // 2, 0:256],
                                   ACT.Silu).then_inc(hid_ready, 1)
            def exps(u):
                act.wait_ge(s_biased, u + 1)
                if u >= 2:
                    act.wait_ge(pT_done, u - 1)
                if NDU <= u - 2 < N0:
                    act.wait_ge(pT_ready, u - 1)
                if NDU <= u < N0:
                    act.activation(p_sb[:, u % 2, 0:256], s_sb[:, u % 2, 0:256], ACT.Exp, scale=-1.0).then_inc(p_ready, 1)
                    return
                c0 = 0
                for row in ALL[u]:
                    c1 = c0 + P * len(row[3])
                    least, den = stats_of(u)(row)
                    e = act.activation(p_sb[:, u % 2, c0:c1], s_sb[:, u % 2, c0:c1], ACT.Exp, bias=least,
                                       scale=-1.0, accum_out=den)
                    c0 = c1
                e.then_inc(p_ready, 1)

            def take_o(u):
                act.wait_ge(pv_done, u + 1)
                _, j, r0, _ = ALL[u][0]
                rows = len(ALL[u])
                act.activation(o_dil[:, j // SLOTS, r0:r0 + rows, j % SLOTS, :],
                               heads2(ps[:, 5 + u % 2, 0:HD * rows]), ACT.Copy).then_inc(o_read, 1)

            for u in range(NU):
                exps(u)
                if u == 5:
                    act.wait_ge(gn_scaled, 1)
                    act.activation(gates_row[0:24, :], gates_row[0:24, :], ACT.Sigmoid).then_inc(g_row_ready, 1)
                if 3 <= u < NDU + 3:
                    take_o(u - 3)
                if u == N0 + 8:
                    act.wait_ge(e_in, 1)
                    act.activation(e_n[:, :, :, :], e_n[:, :, :, :], ACT.Exp, scale=-1.0).then_inc(e_ready, 1)

            act.wait_ge(y_nsa_ready, 1)
            for i in range(NGATE):
                n = GATE + i
                act.wait_ge(gates_scaled, i + 1)
                both = sig[:, 2 * i:2 * i + 2, :].rearrange("p a b -> p (a b)")
                act.activation(both, both, ACT.Sigmoid).then_inc(act_read, 1)
                hi(0, n + 2)
                if i == 4:
                    for c in range(2):
                        act.wait_ge(yd_summed, 3 * (c + 1))
                        act.activation(yd_hi[:, c, :], yd[:, c, :], ACT.Copy).then_inc(ydhi_ready, 1)
                if i == 6:
                    for c in range(4):
                        act.wait_ge(ynT_done, c + 1)
                        act.activation(yn_hi[:, c, :], ps[:, 4 + c, :], ACT.Copy).then_inc(ynhi_ready, 1)
            hi(0, BDIL + 2)
            for i in range(2):
                for m in range(4 * i, 4 * i + 4):
                    act.wait_ge(merged, m + 1)
                    act.activation(xn_hi[:, m, :], mrg[:, m % 2, 1, :], ACT.Copy).then_inc(mhi_ready, 1)
                hi(0, BNSA + i + 2)
            for i in range(4):
                take_y(1, 2 * i)
                take_y(1, 2 * i + 1)
                if i < 3:
                    hi(0, OUT + i + 2)
            root(3)
            hi(0, FFN2 + 1)
            round_x(2, 4)
            ffn(FFN2, PAIR_FFN2, UP, 2)

        @block.vector
        def _(dve):
            chained = [0]

            def chain(instruction):
                chained[0] += 1
                instruction.then_inc(dve_chain, 1)
                dve.wait_ge(dve_chain, chained[0])

            def lo(i, c, paired=False):
                dve.wait_ge(hi_ready, 2 * i + (c + 1))
                whole = [(ring_lo[:, c % 2, :], ring_raw[:, c % 2, :])]
                rounded = [ring_hi[:, c % 2, :]]
                if paired:
                    whole, rounded = paired_views(ring_lo, c), [dst for dst, _ in paired_views(ring_hi, c)]
                for (dst, src), r in zip(whole, rounded):
                    e = dve.tensor_tensor(dst, src, f32(r), ALU.subtract)
                e.then_inc(lo_ready, 1)

            def lo_halves(n, count):
                for half, ready, at in ((slice(0, W // 2), hi_half, count), (slice(W // 2, W), hi_ready, n + 1)):
                    dve.wait_ge(ready, at)
                    e = dve.tensor_tensor(ring_lo[:, n % 2, half], ring_raw[:, n % 2, half], f32(ring_hi[:, n % 2, half]), ALU.subtract)
                e.then_inc(lo_ready, 1)

            def invert(i):
                dve.wait_ge(sd_ready, i + 1)
                dve.reciprocal(rstd[:, :], sd[:, :]).then_inc(rstd_ready, 1)
                dve.wait_ge(rb_ready, i + 1)

            def lo_x(r, g, m):
                dve.wait_ge(xhi_ready, KD * r + m + 1)
                dve.scalar_tensor_tensor(out=xn_lo[:, m, :], in0=xres[:, m, :], scalar=gains[:, g, m:m + 1],
                                         in1=f32(xn_hi[:, m, :]), op0=ALU.mult, op1=ALU.subtract).then_inc(xlo_ready, 1)

            def sum_y(p, m):
                dve.wait_ge(y_squared, KD * p + m + 1)
                if m >= 2:
                    dve.wait_ge(y_summed, (KD - 2) * p + m - 1)
                dve.tensor_tensor(acc[:, :], acc[:, :], square_of(p, m)[:, :], ALU.add).then_inc(y_summed, 1)

            def add_y(p, g, then):
                invert(2 * p + 1)
                for m in range(KD + 1):
                    if m < KD:
                        dve.scalar_tensor_tensor(out=ysb[:, m, :], in0=ysb[:, m, :], scalar=gains[:, g, m:m + 1],
                                                 in1=ps[:, 5, :], op0=ALU.mult, op1=ALU.mult).then_inc(x_scaled, 1)
                    if m >= 2:
                        then(m - 2)
                then(KD - 1)

            def ffn(base, pair0, h0, p, g):
                def up(i, u):
                    first = isinstance(i, int) and 2 * i + u < 2
                    slot = (base + u) % 2
                    dve.wait_ge(w_used, 2 * i + (base + u + 1))
                    if not first:
                        dve.wait_ge(h_ready, 2 * i + (h0 + u - 1))
                        dve.wait_ge(hhi_ready, 2 * i + (h0 + u - 1))
                        dve.wait_ge(hlo_ready, 2 * i + (h0 + u - 1))
                    dve.tensor_tensor(silu_g[:, u, :], ps[:, 2 * slot, :], rb[:, :], ALU.mult).then_inc(g_scaled, 1)
                    dve.tensor_tensor(h_f32[:, u, :], ps[:, 2 * slot + 1, :], rb[:, :], ALU.mult).then_inc(up_scaled, 1)
                    dve.wait_ge(act_read, 2 * i + (pair0 + u + 1))
                    dve.wait_ge(up_scaled, 2 * i + (h0 + u + 1))
                    dve.tensor_tensor(h_f32[:, u, :], silu_g[:, u, :], h_f32[:, u, :], ALU.mult).then_inc(h_ready, 1)
                    if not (first and u == 0):
                        lo(i, base + u + 2)
                    dve.wait_ge(hhi_ready, 2 * i + (h0 + u + 1))
                    at_j = bass.ds(i * (2 * S) + u * S, S)
                    dve.tensor_tensor(hT_lo[:, at_j], h_f32[:, u, :], f32(hT_hi[:, at_j]),
                                      ALU.subtract).then_inc(hlo_ready, 1)

                lo(0, base + 1)
                lo(0, base + 2)
                if p:
                    invert(4)
                else:
                    dve.wait_ge(rb_ready, 1)
                chain(dve.tensor_copy(rb[:, :], ps[:, 7, :]))
                for u in range(2):
                    up(0, u)
                if p == 0:
                    dve.wait_ge(vec_stored, 16)
                with dve.Fori(1, UP // 2) as i:
                    for u in range(2):
                        up(i, u)
                n = base + UP + 2
                lo(0, n)
                with dve.Fori(0, (DOWN - 3) // 2) as i:
                    for u in range(1, 3):
                        lo(i, n + u)
                if p == 0:
                    lo(0, PROJ, paired=True)
                for m in range(1, KD - 1):
                    sum_y(p, m)
                if p == 0:
                    add_y(p, g, lambda m: lo_x(1, 2, m))

            dve.memset(tab[BUCKETS:BUCKETS + 1, :], -MASKED).then_inc(tab_ready, 1)
            dve.wait_ge(cT_gains, 1)
            dve.tensor_copy(gains[:, 0, :], ps[:, 5, 0:KD]).then_inc(gains_ready, 1)
            dve.wait_ge(gains_ready, 1)
            for m in range(KD):
                dve.wait_ge(xT_done, m + 1)
                dve.tensor_copy(xres[:, m, :], ps[:, m % 4, :]).then_inc(x_new, 1)
                if m >= 3:
                    lo_x(0, 0, m - 3)
                if m == 5:
                    lo(0, 0)
            for m in range(KD - 3, KD):
                lo_x(0, 0, m)
            dve.wait_ge(sd_ready, 1)
            dve.reciprocal(rstd[:, :], sd[:, :]).then_inc(rstd_ready, 1)
            dve.wait_ge(cT_gains, 2)
            chain(dve.tensor_copy(gains[:, 1:6, :].rearrange("p a b -> p (a b)"), ps[:, 6, KD:6 * KD]))
            dve.tensor_copy(posT[:, :, :].rearrange("p a b -> p (a b)"), ps[:, 6, 6 * KD:80])
            for g in (1, 5):
                e = dve.tensor_scalar(gains[:, g, :], gains[:, g, :], 0.5, None, ALU.mult)
            chain(e)
            ffn(FFN1, 0, 0, 0, 1)
            lo(0, PROJ + 1, paired=True)
            lo(0, PROJ + 2)
            dve.wait_ge(*xlo_event(1, KD - 1))
            chain(dve.memset(vc_diag[:, :, :], 0.0))
            chain(dve.memset(kc_pad[:, :, :], 0.0))
            invert(2)
            chain(dve.tensor_copy(rb[:, :], ps[:, 7, :]))

            def take(dst, n, scale, strided):
                for c in range(2):
                    to, of, by = dst[:, c, :], ps[:, 2 * (n % 2) + c, :], rb[:, :]
                    if strided:
                        to = to.rearrange("p (r l) -> p l r", r=4)
                        of, by = of.rearrange("p (l r) -> p l r", r=4), by.rearrange("p (l r) -> p l r", r=4)
                    e = dve.scalar_tensor_tensor(out=to, in0=of, scalar=scale, in1=by, op0=ALU.mult, op1=ALU.mult)
                e.then_inc(dve_read, 1)

            def blocks(i, pair):
                dve.wait_ge(pairs_loaded[i], 64)
                if i == 0:
                    chain(dve.memset(blk[:, :, :], 0.0))
                else:
                    dve.wait_ge(blo_ready, i)
                    dve.wait_ge(bhi_ready, i)
                for g in range(NSA_G):
                    src = pair[:, g, :].rearrange("p (n l) -> p l n", l=CS)
                    for half in range(2):
                        dst = blk[:, 8 * half:8 * half + 8, g * CPAD:g * CPAD + NCMP]
                        e = dve.tensor_tensor(dst, src[:, 0:CS:2, half:half + NCMP],
                                              posT[:, i, 8 * half:8 * half + 8].unsqueeze(2).broadcast_to([P, 8, NCMP]),
                                              ALU.add)
                    e.then_inc(blk_ready, 1)

            for i in range(NPROJ):
                n = PROJ + i
                dve.wait_ge(w_used, n + 1)
                if i < 2:
                    take(qn[:, 2 * i:2 * i + 2, :], n, -SCALE, False)
                elif i < 4:
                    take(kv4[:, 2 * (i - 2):2 * (i - 2) + 2, :], n, 1.0, False)
                elif i < 7:
                    take(qd[:, 2 * (i - 4):2 * (i - 4) + 2, :], n, -SCALE, i > 4)
                else:
                    take(kd[:, 2 * (i - 7):2 * (i - 7) + 2, :], n, 1.0, i > 7)
                if i:
                    lo(0, n + 2)
                if i == 1:
                    dve.wait_ge(wg_hi_ready, 1)
                    dve.tensor_tensor(wg_lo[:, :, :], wg_raw[:, :, :], f32(wg_hi[:, :, :]), ALU.subtract).then_inc(wg_lo_ready, 1)
                if i in (5, 7):
                    blocks((i - 5) // 2, pair_k if i == 5 else pair_v)
                if i in (6, 8):
                    b_hi, b_lo = (kb_hi, kb_lo) if i == 6 else (vb_hi, vb_lo)
                    dve.wait_ge(bhi_ready, (i - 4) // 2)
                    dve.tensor_tensor(b_lo[:, :, :], blk[:, :, :], f32(b_hi[:, :, :]), ALU.subtract).then_inc(blo_ready, 1)
            for i in range(NV):
                n = MIX + 2 * i
                dve.wait_ge(w_used, n + 1)
                if i == 0:
                    dve.wait_ge(rstd_s_done, 1)
                    dve.tensor_copy(rstd_s[:, :], ps[:, 6, 0:4]).then_inc(rstd_s_ready, 1)
                if i == 2:
                    dve.wait_ge(rstd_s_ready, 1)
                for t in (2, 3):
                    e = dve.tensor_scalar(v_all[:, t, 256 * i:256 * i + 256], ps[:, 2 * ((MIX + i) % 2) + 1, (t - 2) * 256:(t - 1) * 256],
                                          (rstd if i < 2 else rstd_s)[:, t:t + 1], None, ALU.mult)
                e.then_inc(dve_read, 1)
                lo_halves(n + 2, 2 * i + 1)
                lo_halves(n + 3, 2 * i + 2)
            dve.wait_ge(hidT_done, 1)
            dve.tensor_copy(hid_k[:, :, :].rearrange("p c n -> p (c n)"), ps[:, 6, 0:P])
            for g in range(NSA_G):
                e = dve.tensor_copy(hid_v[:, :, g, :, :],
                                    ps[:, 6, P:2 * P].rearrange("p (c g n) -> p g c n", g=NSA_G, n=CPAD)[:, g].unsqueeze(2)
                                    .broadcast_to([P, 2, HPG, CPAD]))
            e.then_inc(hidT_ready, 1)
            dve.wait_ge(c2_done, 1)
            for g in range(NSA_G):
                rows = slice(g * HD, g * HD + HD)
                dve.tensor_copy(kc_pad[rows, g, :], ps[rows, 5, g * CPAD:g * CPAD + CPAD])
            for h in range(HPG):
                rows = slice(h * CPAD, (h + 1) * CPAD)
                e = dve.tensor_copy(vc_diag[rows, :, h * HD:h * HD + HD], heads2(ps[rows, 5, P:2 * P]))
            e.then_inc(kc_ready, 1)
            dve.wait_ge(gn_done, 1)
            dve.tensor_tensor(gates_row[0:24, :], ps[0:24, 7, :], rb[0:24, :], ALU.mult).then_inc(gn_scaled, 1)

            def bias_of(row):
                kind, h, t, keys = row
                if kind == "d0":
                    return bias_d0[:, h, DIL_KEYS - P * len(keys):DIL_KEYS]
                if kind == "d12":
                    return bias_d12[:, h - SLOTS, :]
                return bias_n[:, h, S - P * len(keys):S]

            def add_bias(u):
                dve.wait_ge(s_done, u + 1)
                if u >= 2:
                    dve.wait_ge(p_ready, u - 1)
                if NDU <= u < N0:
                    t = u - NDU
                    sc = ps[:, u % 3, 0:256]
                    chain(dve.tensor_reduce(nm_c[:, t % 2, :], sc.rearrange("p (h n) -> p h n", n=CPAD), AX_X, ALU.min))
                    dve.tensor_tensor(s_sb[:, u % 2, 0:256].rearrange("p (g h n) -> p h g n", g=NSA_G, n=CPAD),
                                      sc.rearrange("p (h g n) -> p h g n", g=NSA_G, n=CPAD),
                                      nm_c[:, t % 2, :].rearrange("p (h g) -> p h g", g=NSA_G).unsqueeze(3)
                                      .broadcast_to([P, HPG, NSA_G, CPAD]), ALU.subtract).then_inc(s_biased, 1)
                    return
                c0 = 0
                for row in ALL[u]:
                    c1 = c0 + P * len(row[3])
                    least, _ = stats_of(u)(row)
                    e = dve.tensor_tensor_reduce(out=s_sb[:, u % 2, c0:c1], in0=ps[:, u % 3, c0:c1], in1=bias_of(row),
                                                 scale=1.0, scalar=BIGGEST, op0=ALU.add, op1=ALU.min, accum_out=least)
                    c0 = c1
                e.then_inc(s_biased, 1)

            def take_pT(u):
                dve.wait_ge(pT_done, u + 1)
                if u >= 2:
                    dve.wait_ge(pv_done, u - 1)
                w = P * sum(len(row[3]) for row in ALL[u])
                dve.tensor_copy(pT_sb[:, u % 2, 0:w], ps[:, 3 + u % 2, 0:w]).then_inc(pT_ready, 1)

            dve.wait_ge(biases_loaded, 48)
            by_head = lambda ap: ap.rearrange("p (h n) -> p h n", n=CPAD)
            spread_head = lambda ap, n: ap.unsqueeze(2).broadcast_to([P, NSA_H, n])

            def cmp_sums(t):
                u = NDU + t
                dve.wait_ge(p_ready, u + 1)
                chain(dve.tensor_reduce(den_c[:, :], by_head(p_sb[:, u % 2, 0:256]), AX_X, ALU.add))

            def cmp_factors(t):
                chain(dve.reciprocal(den_c[:, :], den_c[:, :]))
                chain(dve.tensor_tensor(f_c[:, t, :], den_c[:, :], gates[:, t, :, 0], ALU.mult))
                if t == 0:
                    chain(dve.tensor_scalar(f_c[:, t, :], f_c[:, t, :], valid[:, :], None, ALU.mult))

            def cmp_out(t):
                dve.wait_ge(pv_done, NDU + t + 1)
                dve.tensor_tensor(y_nsa[:, t, :, :], heads2(ps[:, 7 - t % 2, :]), spread_head(f_c[:, t, :], HD),
                                  ALU.mult).then_inc(yc_ready, 1)

            def take_head(turn):
                h = turn // 2 + HPG * (turn % 2)
                o8 = 8 * (turn % 2)
                u1 = N0 + 5 * (turn + 1)
                dve.wait_ge(p_ready, u1)
                den = stat_d[:, o8:o8 + 8]
                f = f_nsa[:, turn % 2, :]
                chain(dve.reciprocal(f, den))
                odd, even = f[:, 0:4].rearrange("p (t b) -> p t b", b=2), f[:, 4:8].rearrange("p (b t) -> p t b", b=2)
                dve.tensor_tensor(odd, odd, gates[:, 1:NT:2, h, 1:3], ALU.mult)
                chain(dve.tensor_tensor(even, even, gates[:, 0:NT:2, h, 1:3], ALU.mult))
                dve.wait_ge(pv_done, u1)
                o = o_tmp[:, turn % 2, :].rearrange("p (b t d) -> p t b d", b=2, d=HD)
                o_ps = ps[:, 5 + turn % 2, :]
                spread4 = lambda ap: ap.unsqueeze(3).broadcast_to([P, 2, 2, HD])
                dve.tensor_tensor(o[:, 1:NT:2], o_ps[:, 0:256].rearrange("p (t b d) -> p t b d", b=2, d=HD), spread4(odd), ALU.mult)
                dve.tensor_tensor(o[:, 0:NT:2], o_ps[:, 256:512].rearrange("p (b t d) -> p t b d", b=2, d=HD), spread4(even),
                                  ALU.mult).then_inc(o_nsa_read, 1)
                dve.wait_ge(o_nsa_read, turn + 1)
                for b in range(2):
                    chain(dve.tensor_tensor(y_nsa[:, :, h, :], y_nsa[:, :, h, :],
                                            heads2(o_tmp[:, turn % 2, b * 256:b * 256 + 256]), ALU.add))

            def dil_weights():
                dve.wait_ge(stats_loaded, 16)
                st = lambda g, k: st_0[:, :, k, :] if g == 0 else st_n[:, :, 2 * (g - 1) + k, :]
                chain(dve.tensor_tensor(w_n[:, :, :], st(0, 0), st(1, 0), ALU.min))
                chain(dve.tensor_tensor(w_n[:, :, :], w_n[:, :, :], st(2, 0), ALU.min))
                for g in range(3):
                    e = dve.tensor_tensor(e_n[:, g, :, :], st(g, 0), w_n[:, :, :], ALU.subtract)
                e.then_inc(e_in, 1)

            def dil_norm():
                st = lambda g, k: st_0[:, :, k, :] if g == 0 else st_n[:, :, 2 * (g - 1) + k, :]
                dve.wait_ge(e_ready, 1)
                chain(dve.tensor_tensor(w_n[:, :, :], e_n[:, 0, :, :], st(0, 1), ALU.mult))
                for g in (1, 2):
                    chain(dve.tensor_tensor(st(g, 1), e_n[:, g, :, :], st(g, 1), ALU.mult))
                    chain(dve.tensor_tensor(w_n[:, :, :], w_n[:, :, :], st(g, 1), ALU.add))
                chain(dve.reciprocal(w_n[:, :, :], w_n[:, :, :]))
                for g in (1, 2):
                    dve.tensor_tensor(c_n[:, :, g - 1, :], e_n[:, g, :, :], w_n[:, :, :], ALU.mult)
                dve.tensor_tensor(e_n[:, 0, :, :], e_n[:, 0, :, :], w_n[:, :, :], ALU.mult).then_inc(c_ready, 1)

            for u in range(NU + 5):
                if u == 10:
                    dve.wait_ge(gT_done, 1)
                    dve.tensor_copy(gates[:, :, :, :].rearrange("p t h b -> p (t h b)"), ps[:, 7, 0:NT * 24]).then_inc(gates_ready, 1)
                if u == NDU:
                    dve.wait_ge(gates_ready, 1)
                if u == N0:
                    dve.wait_ge(bias_n_loaded, 16)
                if NDU <= u - 4 < N0:
                    cmp_out(u - 4 - NDU)
                if u < NU:
                    add_bias(u)
                if NDU <= u - 2 < N0:
                    cmp_sums(u - 2 - NDU)
                if 2 <= u < NU + 2:
                    take_pT(u - 2)
                if NDU <= u - 2 < N0:
                    cmp_factors(u - 2 - NDU)
                i = u - N0
                if i == 6:
                    dil_weights()
                if i == 11:
                    dil_norm()
                if i >= 9 and (i - 9) % 5 == 0:
                    if i == 9:
                        dve.wait_ge(yc_ready, NT)
                    take_head((i - 9) // 5)
            e = dve.memset(w_n[:, :, :], 0.0)
            e.then_inc(y_nsa_ready, 1)

            dve.wait_ge(y_nsa_ready, 1)
            for i in range(NGATE):
                n = GATE + i
                dve.wait_ge(w_used, n + 1)
                for c in range(2):
                    e = dve.tensor_tensor(sig[:, 2 * i + c, :], ps[:, 2 * (n % 2) + c, :], rb[:, :], ALU.mult)
                e.then_inc(gates_scaled, 1)
                if i not in (3, NGATE - 1):
                    lo(0, GATE + i + 2)
                if i == 3:
                    for c in range(2):
                        for g in range(3):
                            dve.wait_ge(ydT_done, 3 * c + g + 1)
                            src = ps[:, 4 + (3 * c + g) % 4, :]
                            if g == 0:
                                dve.tensor_copy(yd[:, c, :], src).then_inc(yd_summed, 1)
                            else:
                                dve.wait_ge(yd_summed, 3 * c + g)
                                dst = yd[:, c, :].rearrange("p (l r) -> p r l", r=4)
                                dve.tensor_tensor(dst, src.rearrange("p (r l) -> p r l", r=4), dst,
                                                  ALU.add).then_inc(yd_summed, 1)
                    lo(0, GATE + i + 2)
                if i == 4:
                    for c in range(2):
                        dve.wait_ge(ydhi_ready, c + 1)
                        dve.tensor_tensor(yd_lo[:, c, :], yd[:, c, :], f32(yd_hi[:, c, :]), ALU.subtract).then_inc(ydlo_ready, 1)
                if i == 6:
                    for c in range(4):
                        dve.wait_ge(ynhi_ready, c + 1)
                        dve.tensor_tensor(yn_lo[:, c, :], ps[:, 4 + c, :], f32(yn_hi[:, c, :]), ALU.subtract).then_inc(ynlo_ready, 1)
            for m in range(KD):
                if m == 4:
                    lo(0, BDIL + 1)
                dve.wait_ge(act_read, PAIR_GATE + 4 + m // 2 + 1)
                dve.wait_ge(*b_event(m))
                dve.tensor_tensor(sig[:, KD + m, :], sig[:, KD + m, :], ps[:, 4 + m % 4, :], ALU.mult).then_inc(b_gated, 1)
            lo(0, BDIL + 2)
            for m in range(KD):
                dve.wait_ge(*a_event(m))
                if m == 0:
                    dve.wait_ge(b_gated, KD)
                dve.tensor_tensor(mrg[:, m % 2, 0, :], sig[:, m, :], ps[:, m % 4, :], ALU.mult).then_inc(a_gated, 1)
                dve.wait_ge(a_gated, m + 1)
                dve.tensor_tensor(mrg[:, m % 2, 1, :], mrg[:, m % 2, 0, :], sig[:, KD + m, :], ALU.add).then_inc(merged, 1)
                for done in ([m - 1] if m else []) + ([m] if m == KD - 1 else []):
                    dve.wait_ge(mhi_ready, done + 1)
                    dve.tensor_tensor(xn_lo[:, done, :], mrg[:, done % 2, 1, :], f32(xn_hi[:, done, :]),
                                      ALU.subtract).then_inc(mlo_ready, 1)
                if m % 4 == 3:
                    lo(0, BNSA + m // 4 + 2)
            for i in range(4):
                for m in (2 * i, 2 * i + 1):
                    if 0 < m < KD - 1:
                        sum_y(1, m)
                if i < 3:
                    lo(0, OUT + i + 2)
            add_y(1, 3, lambda m: lo_x(2, 4, m))
            ffn(FFN2, PAIR_FFN2, UP, 2, 5)
            dve.wait_ge(sd_ready, 6)
            chain(dve.reciprocal(rstd[:, :], sd[:, :]))
            for j in range(2 * NT):
                half, t = j // NT, j % NT
                dve.wait_ge(oT_done, j + 1)
                dve.scalar_tensor_tensor(out=o_tok[:, t, half * S:half * S + S], in0=ps[:, j, :], scalar=rstd[:, t:t + 1],
                                         in1=x_fin[half][:, t, :], op0=ALU.mult, op1=ALU.add).then_inc(o_ready, 1)

        @block.tensor
        def _(pe):
            def part(kind, slot, k0, width):
                return ring[kind][:, slot, k0:k0 + width]

            def cols_step(slot, norm=None, between={}):
                for k in range(KD):
                    if k in between:
                        between[k]()
                    if norm is not None:
                        pe.wait_ge(*xlo_event(norm, k))
                    for c in range(2):
                        for i, (a, b) in enumerate(MODES):
                            e = pe.matmul(ps[:, 2 * slot + c, :], part(a, slot, k * 256 + c * P, P), xn[b][:, k, :],
                                          start=(k == 0 and i == 0), stop=(k == KD - 1 and i == 2))
                e.then_inc(w_used, 1)

            def keep_warm(n, bank):
                for _ in range(n):
                    pe.matmul(ps[:, bank, 0:P], ident[:, :], ident[:, :], start=True, stop=True)

            def column_sums(bank, src, first, last):
                for t in range(NT):
                    e = pe.matmul(ps[:, bank, t * P:t * P + P], src[:, t * P:t * P + P], ones[:, :],
                                  start=(first and t == 0), stop=last, skip_group_check=True)
                return e

            def spread_rstd(i, bank, warm):
                keep_warm(warm, 6 if i == 0 else 3)
                pe.wait_ge(rstd_ready, i + 1)
                for t in range(NT):
                    e = pe.matmul(ps[:, bank, t * P:t * P + P], rstd[:, t:t + 1].broadcast_to([P, P]), ident[:, :],
                                  start=True, stop=True)
                e.then_inc(rb_ready, 1)

            def transpose_gains():
                pe.wait_ge(gains_loaded, 112)
                pe.transpose(ps[:, 6, 0:80], gains_row[0:80, :], ident[0:80, 0:80]).then_inc(cT_gains, 1)

            def x_by_token(part):
                for j, bank, copies in FIN[part]:
                    if copies:
                        pe.wait_ge(xf_copied, copies)
                    for c in range(4):
                        e = pe.transpose(ps[:, bank, c * P:c * P + P],
                                         xres[:, j // NT * 4 + c, j % NT * P:j % NT * P + P], ident[:, :])
                    e.then_inc(xfT_done, 1)

            def sum_x(r):
                pe.wait_ge(x_summed, (KD - 1) * r)
                if r == 2:
                    pe.wait_ge(xf_copied, 3)
                column_sums(6, acc[:, :], True, True).then_inc(ss_done, 1)

            def sum_squares(p, bank):
                pe.wait_ge(y_summed, (KD - 2) * (p + 1))
                column_sums(bank, acc[:, :], True, False)
                pe.wait_ge(y_squared, KD * (p + 1))
                column_sums(bank, square_of(p, KD - 1)[:, :], False, True).then_inc(ss_done, 1)

            def norm_y(p):
                sum_squares(p, 4)
                spread_rstd(2 * p + 1, 5, 3)
                keep_warm(8, 3)

            def ffn(base, pair0, h0, p, norm):
                def up(i, u):
                    pe.wait_ge(lo_ready, 2 * i + (base + u + 1))
                    if not (isinstance(i, int) and 2 * i + u < 2):
                        pe.wait_ge(up_scaled, 2 * i + (h0 + u - 1))
                    first = isinstance(i, int) and i == 0
                    cols_step((base + u) % 2, norm if first and u == 0 else None,
                              {3: lambda: x_by_token(1), 4: lambda: sum_x(2), 6: lambda: spread_rstd(4, 7, 0)} if first and u == 1 and p else
                              {4: transpose_gains, 7: lambda: spread_rstd(0, 7, 0)} if first and u == 0 and not p else {})

                def down(i, u, order=range(KD), start=False, stop=False):
                    n0 = base + UP + u
                    pe.wait_ge(lo_ready, 2 * i + (n0 + 1))
                    for m in order:
                        if start and m == 0:
                            pe.wait_ge(up_scaled, h0 + UP)
                        for kk in range(2):
                            at_k = bass.ds(i * (4 * S) + (2 * u + kk) * S, S)
                            for q, (a, b) in enumerate(MODES):
                                e = pe.matmul(ps[:, m, :], part(a, n0 % 2, kk * D + m * P, P), hT[b][:, at_k],
                                              start=(start and kk == 0 and q == 0), stop=(stop and kk == 1 and q == 2),
                                              skip_group_check=True)
                        if stop and m < KD - 1:
                            e.then_inc(y_done, 1)
                    e.then_inc(w_used, 1)

                for u in range(2):
                    up(0, u)
                    if p == 2:
                        x_by_token(2 * u)
                    if p == 0:
                        pe.wait_ge(small_loaded, 32)
                        pe.wait_ge(tab_ready, 1)
                        for c in BIAS_PARTS[u]:
                            if c >= 3:
                                pe.wait_ge(vec_copied, c - 2)
                            pe.matmul(ps[0:20, BIAS_BANKS[c], :], tab[0:BUCKETS + 1, :], onehot_sb[0:BUCKETS + 1, c * S:c * S + S],
                                      start=True, stop=True).then_inc(vec_mm, 1)
                with pe.Fori(1, UP // 2) as i:
                    for u in range(2):
                        up(i, u)
                pe.wait_ge(hlo_ready, h0 + UP - 2)
                if p == 0:
                    pe.wait_ge(vec_copied, 5)
                else:
                    pe.wait_ge(xf_copied, 2 * NT)
                down(0, 0, order=(4, 5, 6, 7, 0, 1, 2, 3), start=True)
                with pe.Fori(0, (DOWN - 3) // 2) as i:
                    for u in range(1, 3):
                        down(i, u)
                down(0, DOWN - 2)
                pe.wait_ge(hlo_ready, h0 + UP)
                down(0, DOWN - 1, stop=True)
                if p == 0:
                    norm_y(p)

            pe.wait_ge(consts, 6)
            keep_warm(14, 6)
            pe.wait_ge(g1_loaded, 16)
            pe.transpose(ps[:, 5, 0:KD], gains_row[0:KD, :], ident[0:KD, 0:KD]).then_inc(cT_gains, 1)
            for m in range(KD):
                if m >= 4:
                    pe.wait_ge(x_new, m - 3)
                for t in range(NT):
                    if m == 0:
                        pe.wait_ge(x_loaded[t], 16)
                    e = pe.transpose(ps[:, m % 4, t * P:t * P + P], x_tok[:, t, m * P:m * P + P], ident[:, :])
                e.then_inc(xT_done, 1)
            keep_warm(16, 6)
            ffn(FFN1, 0, 0, 0, 0)
            def proj(i, u):
                pe.wait_ge(lo_ready, 2 * i + (PROJ + u + 1))
                first = isinstance(i, int) and i == 0
                if not first:
                    pe.wait_ge(dve_read, 2 * i + (u - 1))
                cols_step((PROJ + u) % 2, 1 if first and u == 0 else None,
                          {4: lambda: sum_x(1), 6: lambda: spread_rstd(2, 7, 0)} if first and u else {})

            for u in range(2):
                proj(0, u)
            with pe.Fori(1, NPROJ // 2) as i:
                for u in range(2):
                    proj(i, u)
            def compress(i):
                n = MIX + 2 * i + 1
                pe.wait_ge(lo_ready, n + 1)
                kv = i // 2
                if i % 2 == 0:
                    pe.wait_ge(blo_ready, kv + 1)
                blocks = ((kb_hi, kb_lo), (vb_hi, vb_lo))[kv]
                for l in range(8):
                    for q, (a, b) in enumerate(MODES):
                        e = pe.matmul(ps[0:64, 4 + kv, 0:256], blocks[b][:, 8 * (i % 2) + l, :], part(a, n % 2, l * 256, 256),
                                      start=(i % 2 == 0 and l == 0 and q == 0), stop=(i % 2 == 1 and l == 7 and q == 2),
                                      skip_group_check=True)
                e.then_inc(w_used, 1)

            for r in range(4):
                e = pe.matmul(ps[:, 6, r:r + 1], rb[0:1, r:S:4], ones[0:1, 0:1], start=True, stop=True)
            e.then_inc(rstd_s_done, 1)
            for i in range(NV):
                n = MIX + 2 * i
                pair = 2 * ((MIX + i) % 2)
                pe.wait_ge(lo_ready, n + 1)
                pe.wait_ge(act_read, PAIR_PROJ + i - 1)
                pe.wait_ge(dve_read, NPROJ + i - 1)
                for t in range(NT):
                    tokens = slice(t * P, t * P + P) if i < 2 else slice(t, S, 4)
                    for k in range(KD):
                        for q, (a, b) in enumerate(MODES):
                            e = pe.matmul(ps[:, pair + t // 2, (t % 2) * 256:(t % 2) * 256 + 256],
                                          xn[b][:, k, tokens], part(a, n % 2, k * 256, 256),
                                          start=(k == 0 and q == 0), stop=(k == KD - 1 and q == 2))
                e.then_inc(w_used, 1)
                compress(i)
            pe.wait_ge(wg_lo_ready, 1)
            wg = (wg_hi, wg_lo)
            for k in range(KD):
                if k == 5:
                    pe.wait_ge(hid_ready, 2)
                    for kv in range(2):
                        for c in range(2):
                            e = pe.transpose(ps[:, 6, (2 * kv + c) * 64:(2 * kv + c) * 64 + 64], hid_row[0:64, kv, c, :],
                                             ident[0:64, 0:64])
                    e.then_inc(hidT_done, 1)
                for q, (a, b) in enumerate(MODES):
                    e = pe.matmul(ps[0:24, 7, :], wg[a][:, k, :], xn[b][:, k, :],
                                  start=(k == 0 and q == 0), stop=(k == KD - 1 and q == 2))
            e.then_inc(gn_done, 1)
            pe.wait_ge(w2_loaded, 48)
            pe.wait_ge(hidT_ready, 1)
            for c in range(2):
                pe.matmul(ps[:, 5, 0:64], w2k[:, c, :, :].rearrange("p a b -> p (a b)"), hid_k[:, c, :],
                          start=(c == 0), stop=(c == 1))
            for g in range(NSA_G):
                for c in range(2):
                    e = pe.matmul(ps[:, 5, P + g * HD:P + g * HD + HD],
                                  hid_v[:, c, g, :, :].rearrange("p a b -> p (a b)"), w2v[:, c, :], start=(c == 0), stop=(c == 1))
            e.then_inc(c2_done, 1)

            def widen(row):
                kind, h, t, _ = row
                if (kind, t) == ("w", 0) or h == DIL_H - 1:
                    return 0, 0
                return (HD, 0) if (kind, t) == ("w", 2) else (0, HD)

            def operands(row):
                before, after = widen(row)
                kind, h, t, keys = row
                if kind[0] == "d":
                    rows = slice((h % 2) * HD, (h % 2) * HD + HD)
                    q = qd[rows, h // 2, t * P:t * P + P]
                    k = kd[rows, h // 2, keys[0] * P:(keys[-1] + 1) * P]
                    v = [v_all[:, x, 256 + h * HD:256 + h * HD + HD + after] for x in keys]
                else:
                    g = h // HPG
                    rows = slice(g * HD, g * HD + HD)
                    q = qn[rows, h % HPG, t * P:t * P + P]
                    k = kv4[rows, 2 + (kind == "w"), keys[0] * P:(keys[-1] + 1) * P]
                    c0 = (kind == "w") * P + g * HD
                    v = [v_all[:, x, c0 - before:c0 + HD + after] for x in keys]
                return q, k, v

            def scores(u):
                if u >= 3:
                    pe.wait_ge(s_biased, u - 2)
                if NDU <= u < N0:
                    t = u - NDU
                    tokens = slice(t * P, t * P + P)
                    by_group = ps[:, u % 3, 0:256].rearrange("p (h g n) -> p g h n", g=NSA_G, n=CPAD)
                    for g in range(NSA_G):
                        pe.matmul(by_group[:, g], bias_cT[:, g, tokens], ident[:, :], start=(g == 0), stop=False,
                                  skip_group_check=True)
                    for h in range(HPG):
                        e = pe.matmul(ps[:, u % 3, 64 * h:64 * h + P], qn[:, h, tokens],
                                      kc_pad[:, :, :].rearrange("p g n -> p (g n)"), start=False, stop=True, skip_group_check=True)
                    e.then_inc(s_done, 1)
                    return
                c0 = 0
                for row in ALL[u]:
                    q, k, _ = operands(row)
                    c1 = c0 + P * len(row[3])
                    e = pe.matmul(ps[:, u % 3, c0:c1], q, k, start=True, stop=True)
                    c0 = c1
                e.then_inc(s_done, 1)

            def transposes(u):
                pe.wait_ge(p_ready, u + 1)
                if u >= 2:
                    pe.wait_ge(pT_ready, u - 1)
                n = sum(len(row[3]) for row in ALL[u])
                for x in range(n):
                    e = pe.transpose(ps[:, 3 + u % 2, x * P:x * P + P], p_sb[:, u % 2, x * P:x * P + P], ident[:, :])
                e.then_inc(pT_done, 1)

            def values(u):
                pe.wait_ge(pT_ready, u + 1)
                if NDU <= u < N0:
                    t = u - NDU
                    if t == 1:
                        pe.wait_ge(o_read, NDU)
                    if t >= 2:
                        pe.wait_ge(yc_ready, t - 1)
                    for g in range(NSA_G):
                        e = pe.matmul(ps[:, 7 - t % 2, g * 256:g * 256 + 256], pT_sb[:, u % 2, g * P:g * P + P],
                                      vc_diag[:, g, :], start=True, stop=True)
                    e.then_inc(pv_done, 1)
                    return
                x = 0
                for i, row in enumerate(ALL[u]):
                    _, _, v = operands(row)
                    if u < NDU:
                        bank, o0 = 5 + u % 2, i * HD
                    else:
                        bank, o0 = 5 + (u - N0) // 5 % 2, place(row) * HD
                    before, after = widen(row)
                    for j, vj in enumerate(v):
                        e = pe.matmul(ps[:, bank, o0 - before:o0 + HD + after], pT_sb[:, u % 2, x * P:x * P + P], vj,
                                      start=(j == 0), stop=(j == len(v) - 1))
                        x += 1
                e.then_inc(pv_done, 1)

            pe.wait_ge(dve_read, NPROJ + NV)
            pe.wait_ge(act_read, PAIR_GATE)
            for i in range(NU + 3):
                if i == 8:
                    pe.wait_ge(g_row_ready, 1)
                    for t in range(NT):
                        e = pe.transpose(ps[:, 7, t * 24:t * 24 + 24], gates_row[0:24, t * P:t * P + P], ident[0:24, 0:24])
                    e.then_inc(gT_done, 1)
                if i == NDU:
                    pe.wait_ge(kc_ready, 1)
                    pe.wait_ge(cmp_loaded, 16 * NSA_H)
                    pe.wait_ge(gates_ready, 1)
                if i < NU:
                    scores(i)
                if 2 <= i < NU + 2:
                    transposes(i - 2)
                u = i - 3
                if u >= 0:
                    if 2 <= u < NDU:
                        pe.wait_ge(o_read, u - 1)
                    if u == N0 + 5:
                        pe.wait_ge(yc_ready, NT)
                    if u >= N0 + 10 and (u - N0) % 5 == 0:
                        pe.wait_ge(o_nsa_read, (u - N0) // 5 - 1)
                    values(u)

            pe.wait_ge(s_biased, NU)
            pe.wait_ge(pT_ready, NU)

            def gate_pair(i):
                for u in range(2):
                    pe.wait_ge(lo_ready, 2 * i + (GATE + u + 1))
                    pe.wait_ge(act_read, 2 * i + (PAIR_GATE + u - 1))
                    cols_step((GATE + u) % 2)

            with pe.Fori(0, 2) as i:
                gate_pair(i)
            pe.wait_ge(o_nsa_read, NSA_H)
            for c in range(2):
                for g in range(3):
                    if c == 0:
                        pe.wait_ge(odil_scaled, 4 * (g + 1))
                    if 3 * c + g >= 4:
                        pe.wait_ge(yd_summed, 3 * c + g - 3)
                    for r in range(4):
                        e = pe.transpose(ps[:, 4 + (3 * c + g) % 4, r * P:r * P + P],
                                         o_dil[:, g, r, 2 * c:2 * c + 2, :].rearrange("p a b -> p (a b)"), ident[:, :])
                    e.then_inc(ydT_done, 1)
            gate_pair(2)
            pe.wait_ge(yd_summed, 6)
            pe.wait_ge(y_nsa_ready, 1)
            for c in range(4):
                for t in range(NT):
                    e = pe.transpose(ps[:, 4 + c, t * P:t * P + P],
                                     y_nsa[:, t, 2 * c:2 * c + 2, :].rearrange("p a b -> p (a b)"), ident[:, :])
                e.then_inc(ynT_done, 1)
            gate_pair(3)

            pe.wait_ge(lo_ready, BDIL + 1)
            pe.wait_ge(ydlo_ready, 2)
            pe.wait_ge(ynlo_ready, 4)
            ydp, ynp = (yd_hi, yd_lo), (yn_hi, yn_lo)
            for m in range(KD):
                if m >= 4:
                    pe.wait_ge(b_gated, m - 3)
                for k in range(2):
                    for q, (a, b) in enumerate(MODES):
                        e = pe.matmul(ps[:, 4 + m % 4, :], part(a, BDIL % 2, k * D + m * P, P), ydp[b][:, k, :],
                                      start=(k == 0 and q == 0), stop=(k == 1 and q == 2))
                e.then_inc(b_done if m < KD - 1 else w_used, 1)
            pe.wait_ge(act_read, PAIR_FFN2)
            for m in range(KD):
                n = BNSA + m // 4
                if m % 4 == 0:
                    pe.wait_ge(lo_ready, n + 1)
                if m >= 4:
                    pe.wait_ge(a_gated, m - 3)
                for k in range(4):
                    for q, (a, b) in enumerate(MODES):
                        e = pe.matmul(ps[:, m % 4, :], part(a, n % 2, k * S + (m % 4) * P, P), ynp[b][:, k, :],
                                      start=(k == 0 and q == 0), stop=(k == 3 and q == 2))
                e.then_inc(a_done if m % 4 < 3 else w_used, 1)
            pe.wait_ge(b_gated, KD)
            for i in range(4):
                n = OUT + i
                pe.wait_ge(lo_ready, n + 1)
                if i < 2:
                    pe.wait_ge(a_gated, 4 + 2 * i + 2)
                order = [(k, c) for k in range(KD) for c in range(2)] if i == 0 else [(k, c) for c in range(2) for k in range(KD)]
                for k, c in order:
                    if i == 0 and c == 0:
                        pe.wait_ge(mlo_ready, k + 1)
                    for q, (a, b) in enumerate(MODES):
                        e = pe.matmul(ps[:, 2 * i + c, :], part(a, n % 2, k * 256 + c * P, P), xn[b][:, k, :],
                                      start=(k == 0 and q == 0), stop=(k == KD - 1 and q == 2))
                    if k == KD - 1:
                        e.then_inc(w_used if c else y_done, 1)
            norm_y(1)
            ffn(FFN2, PAIR_FFN2, UP, 2, 2)
            def y_by_token(j):
                for c in range(4):
                    e = pe.transpose(ps[:, j, c * P:c * P + P], y_gained[:, j // NT * 4 + c, j % NT * P:j % NT * P + P], ident[:, :])
                e.then_inc(oT_done, 1)

            pe.wait_ge(y_copied, 4)
            for j in range(NT):
                y_by_token(j)
            pe.wait_ge(y_copied, KD)
            sum_squares(2, 7)
            for j in range(NT, 2 * NT - 1):
                y_by_token(j)
            pe.wait_ge(sd_ready, 6)
            y_by_token(2 * NT - 1)


INPUTS = ["x", "ffn1_norm_pre", "ffn1_w_gu", "ffn1_w_down", "ffn1_norm_post", "mix_norm_pre", "w_in",
          "cmp_pos_k", "cmp_w1_k", "cmp_w2_k", "cmp_pos_v", "cmp_w1_v", "cmp_w2_v",
          "w_branch_nsa", "w_branch_dil", "w_out", "mix_norm_post",
          "ffn2_norm_pre", "ffn2_w_gu", "ffn2_w_down", "ffn2_norm_post", "rel_bias"]


def kernel(**inputs):
    import concourse.bacc as bacc
    from concourse.bass_utils import run_bass_kernel_spmd

    nc = bacc.Bacc("TRN2", target_bir_lowering=False, num_devices=1)
    arrays, args = {}, []
    for name in INPUTS:
        a = np.ascontiguousarray(inputs[name])
        if name != "rel_bias":
            a = a[0]
        arrays[f"in_{name}"] = a
    arrays["bucket_of_distance"] = bucket_table()
    for name, a in arrays.items():
        args.append(nc.dram_tensor(name, a.shape, mybir.dt.from_np(a.dtype), kind="ExternalInput").ap())
    args.append(nc.dram_tensor("out", (S, D), F32, kind="ExternalOutput").ap())
    layer_kernel(nc, *args)
    r = run_bass_kernel_spmd(nc, [arrays], core_ids=[0])
    return r.results[0]["out"].reshape(1, S, D)
```
